# Optimizing a Trainium2 kernel written in Bass

```python
import math
import jax
import jax.numpy as jnp
from jax import lax
import numpy as np

D_MODEL = 2048
BATCH = 1
SEQ = 512
DEPTH = 1
DEC_BATCH = 8
DEC_SEQ = 1
PAST_LEN = 256
PAGE_SIZE = 128

HEAD_DIM = 128
N_HEADS = D_MODEL // 256
N_KV = N_HEADS // 4
GQA_R = N_HEADS // N_KV
D_NSA = N_HEADS * HEAD_DIM
D_GM = D_MODEL // 2
SGU_GROUPS = D_GM // 128
SGU_GW = D_GM // SGU_GROUPS
CHUNK = 128
CMP_LEN = 32
CMP_STRIDE = 16
SEL_LEN = 64
N_SEL = 16
WINDOW = 512
N_BUCKETS = 32
MAX_DIST = 128
D_FF = 4 * D_MODEL
QBLOCK = 128
EPS = 1e-6
NEG = -1e30
FORCE = 1e6
N_IN = 2 * D_GM + D_NSA + 3 * 2 * N_KV * HEAD_DIM + 3 * N_HEADS + 2 * D_MODEL

kernel_name = 'hybrid_gmlp_nsa_decode_step'

def rmsnorm(x, g):
    xf = x.astype(jnp.float32)
    y = xf * lax.rsqrt(jnp.mean(xf * xf, axis=-1, keepdims=True) + EPS)
    return y.astype(x.dtype) * g

def t5_bucket(rel):
    n = jnp.maximum(rel, 0)
    max_exact = N_BUCKETS // 2
    nf = jnp.maximum(n, 1).astype(jnp.float32)
    large = max_exact + (jnp.log(nf / max_exact) / math.log(MAX_DIST / max_exact)
                         * (N_BUCKETS - max_exact)).astype(jnp.int32)
    large = jnp.minimum(large, N_BUCKETS - 1)
    return jnp.where(n < max_exact, n, large)

def masked_softmax(s, mask):
    s = jnp.where(mask, s.astype(jnp.float32), NEG)
    p = jax.nn.softmax(s, axis=-1)
    return jnp.where(mask, p, 0.0)

def split_in(z):
    kvw = 2 * N_KV * HEAD_DIM
    sizes = (2 * D_GM, D_NSA, kvw, kvw, kvw, 3 * N_HEADS, D_MODEL, D_MODEL)
    cuts = [int(c) for c in np.cumsum(sizes)[:-1]]
    return jnp.split(z, cuts, axis=-1)

def project(x, g_mix_norm, w_in, g_sgu, g_q):
    B, T = x.shape[:2]
    z = rmsnorm(x, g_mix_norm) @ w_in
    uv, q, kvc, kvs, kvw, g_nsa, g_a, g_b = split_in(z)
    uv = jax.nn.gelu(uv)
    u = uv[..., :D_GM]
    v = rmsnorm(uv[..., D_GM:], g_sgu)
    q = rmsnorm(q.reshape(B, T, N_KV, GQA_R, HEAD_DIM), g_q) * (HEAD_DIM ** -0.5)
    rows = lambda a: a.reshape(B, T, 2, N_KV, HEAD_DIM)
    gates = jax.nn.sigmoid(g_nsa).reshape(B, T, N_KV, GQA_R, 3)
    return u, v, q, rows(kvc), rows(kvs), rows(kvw), gates, g_a, g_b

def spatial_gate(u, v, w_sgu, b_sgu):
    B, NCH, Tc = v.shape[:3]
    mask = jnp.tril(jnp.ones((Tc, Tc), dtype=bool))
    wm = jnp.where(mask, w_sgu[:, :Tc, :Tc], 0.0)
    vg = v.reshape(B, NCH, Tc, SGU_GROUPS, SGU_GW)
    s = jnp.einsum('gts,bnsgc->bntgc', wm, vg) + b_sgu[:, :Tc].T[:, :, None]
    return u * s.reshape(B, NCH, Tc, D_GM)

def compress(k, w, pos):
    B, L = k.shape[:2]
    r = CMP_LEN // CMP_STRIDE
    n = (L - CMP_LEN) // CMP_STRIDE + 1
    seg = k[:, :(n + r - 1) * CMP_STRIDE].reshape(B, n + r - 1, CMP_STRIDE, N_KV, HEAD_DIM)
    w_seg = w.reshape(r, CMP_STRIDE, HEAD_DIM, HEAD_DIM)
    p_seg = pos.reshape(r, CMP_STRIDE, 1, HEAD_DIM)
    out = jnp.einsum('bnsgd,sde->bnge', seg[:, 0:n] + p_seg[0], w_seg[0])
    for m in range(1, r):
        out = out + jnp.einsum('bnsgd,sde->bnge', seg[:, m:m + n] + p_seg[m], w_seg[m])
    return out

def nsa_keys(kvc, kvs, g_k, pos_cmp_k, w_cmp_k, pos_cmp_v, w_cmp_v):
    kc = rmsnorm(compress(kvc[:, :, 0], w_cmp_k, pos_cmp_k), g_k[0])
    vc = compress(kvc[:, :, 1], w_cmp_v, pos_cmp_v)
    c_end = jnp.arange(kc.shape[1]) * CMP_STRIDE + (CMP_LEN - 1)
    B, L = kvs.shape[:2]
    ns = -(-L // SEL_LEN)
    kvs = jnp.pad(kvs, ((0, 0), (0, ns * SEL_LEN - L), (0, 0), (0, 0), (0, 0)))
    to_blocks = lambda a: jnp.transpose(a.reshape(B, ns, SEL_LEN, N_KV, HEAD_DIM), (0, 3, 1, 2, 4))
    ks = to_blocks(rmsnorm(kvs[:, :, 0], g_k[1]))
    vs = to_blocks(kvs[:, :, 1])
    return kc, vc, c_end, ks, vs

def overlap(nc, ns):
    i = jnp.arange(nc)[:, None] * CMP_STRIDE
    j = jnp.arange(ns)[None, :] * SEL_LEN
    return ((i < j + SEL_LEN) & (i + CMP_LEN > j)).astype(jnp.float32)

def nsa_block(q, q_pos, gates, kc, vc, c_end, ks, vs, kw, vw, kw_pos, rel_bias):
    B, Tq = q.shape[:2]
    bt = rel_bias.reshape(N_BUCKETS, N_KV, GQA_R)
    rel_c = q_pos[:, None] - c_end[None, :]
    bias_c = jnp.transpose(bt[t5_bucket(rel_c)], (2, 3, 0, 1))
    s_c = jnp.einsum('btgrd,bcgd->bgrtc', q, kc) + bias_c
    p_c = masked_softmax(s_c, rel_c >= 0)
    o_c = jnp.einsum('bgrtc,bcgd->btgrd', p_c.astype(vc.dtype), vc)
    ns = ks.shape[2]
    n_pick = min(N_SEL, ns)
    imp = jnp.einsum('bgrtc,cj->bgtj', p_c, overlap(kc.shape[1], ns))
    blk = jnp.arange(ns)[None, :]
    cur = (q_pos // SEL_LEN)[:, None]
    forced = (blk == 0) | (blk == cur) | (blk == cur - 1)
    eligible = blk * SEL_LEN <= q_pos[:, None]
    imp = jnp.where(forced, FORCE, jnp.where(eligible, imp, -1.0))
    _, idx = lax.top_k(imp, n_pick)
    bi = jnp.arange(B)[:, None, None, None]
    gi = jnp.arange(N_KV)[None, :, None, None]
    k_sel = ks[bi, gi, idx]
    v_sel = vs[bi, gi, idx]
    k_pos = idx[..., None] * SEL_LEN + jnp.arange(SEL_LEN)
    rel_s = q_pos[None, None, :, None, None] - k_pos
    bias_s = jnp.moveaxis(jnp.transpose(bt, (1, 0, 2))[gi[..., None], t5_bucket(rel_s)], -1, 2)
    s_s = jnp.einsum('btgrd,bgtnsd->bgrtns', q, k_sel) + bias_s
    p_s = masked_softmax(s_s.reshape(B, N_KV, GQA_R, Tq, -1),
                         (rel_s >= 0).reshape(B, N_KV, 1, Tq, -1))
    o_s = jnp.einsum('bgrtk,bgtkd->btgrd', p_s.astype(vs.dtype),
                     v_sel.reshape(B, N_KV, Tq, -1, HEAD_DIM))
    rel_w = q_pos[:, None] - kw_pos[None, :]
    mask_w = (rel_w >= 0) & (rel_w < WINDOW) & (kw_pos[None, :] >= 0)
    bias_w = jnp.transpose(bt[t5_bucket(rel_w)], (2, 3, 0, 1))
    s_w = jnp.einsum('btgrd,bkgd->bgrtk', q, kw) + bias_w
    p_w = masked_softmax(s_w, mask_w)
    o_w = jnp.einsum('bgrtk,bkgd->btgrd', p_w.astype(vw.dtype), vw)
    return gates[..., 0:1] * o_c + gates[..., 1:2] * o_s + gates[..., 2:3] * o_w

def merge_ffn(x, o_a, o_b, g_a, g_b, w_proj_gmlp, w_proj_nsa, w_out, g_mlp_norm, w_up, w_down):
    mix = jax.nn.sigmoid(g_a) * (o_a @ w_proj_gmlp) + jax.nn.sigmoid(g_b) * (o_b @ w_proj_nsa)
    x = x + mix @ w_out
    hm = rmsnorm(x, g_mlp_norm)
    return x + jnp.square(jax.nn.relu(hm @ w_up)) @ w_down

def layer_prompt(x, rel_bias, g_mix_norm, w_in, g_sgu, w_sgu, b_sgu, g_q, g_k, pos_cmp_k, w_cmp_k,
                 pos_cmp_v, w_cmp_v, w_proj_gmlp, w_proj_nsa, w_out, g_mlp_norm, w_up, w_down):
    B, T = x.shape[:2]
    u, v, q, kvc, kvs, kvw, gates, g_a, g_b = project(x, g_mix_norm, w_in, g_sgu, g_q)
    n_ch = T // CHUNK
    o_a = spatial_gate(u.reshape(B, n_ch, CHUNK, D_GM), v.reshape(B, n_ch, CHUNK, D_GM),
                       w_sgu, b_sgu).reshape(B, T, D_GM)
    kc, vc, c_end, ks, vs = nsa_keys(kvc, kvs, g_k, pos_cmp_k, w_cmp_k, pos_cmp_v, w_cmp_v)
    pad = ((0, 0), (WINDOW, 0), (0, 0), (0, 0))
    kw = jnp.pad(rmsnorm(kvw[:, :, 0], g_k[2]), pad)
    vw = jnp.pad(kvw[:, :, 1], pad)

    def query_block(qb):
        t0 = qb * QBLOCK
        cut = lambda a, n: lax.dynamic_slice_in_dim(a, t0, n, axis=1)
        return nsa_block(cut(q, QBLOCK), t0 + jnp.arange(QBLOCK), cut(gates, QBLOCK), kc, vc, c_end,
                         ks, vs, cut(kw, WINDOW + QBLOCK), cut(vw, WINDOW + QBLOCK),
                         t0 - WINDOW + jnp.arange(WINDOW + QBLOCK), rel_bias)

    o_b = lax.map(query_block, jnp.arange(T // QBLOCK))
    o_b = jnp.moveaxis(o_b, 0, 1).reshape(B, T, D_NSA)
    y = merge_ffn(x, o_a, o_b, g_a, g_b, w_proj_gmlp, w_proj_nsa, w_out, g_mlp_norm, w_up, w_down)
    return y, kvc, kvs, kvw[:, T - min(WINDOW, T):], v[:, ((T - 1) // CHUNK) * CHUNK:]

def layer_sample(x, cache_c, cache_s, win_buf, page_table, rel_bias, g_mix_norm, w_in, g_sgu, w_sgu,
                 b_sgu, g_q, g_k, pos_cmp_k, w_cmp_k, pos_cmp_v, w_cmp_v, w_proj_gmlp, w_proj_nsa,
                 w_out, g_mlp_norm, w_up, w_down):
    B, T = x.shape[:2]
    u, v, q, kvc, kvs, kvw, gates, g_a, g_b = project(x, g_mix_norm, w_in, g_sgu, g_q)
    o_a = spatial_gate(u[:, None], v[:, None], w_sgu, b_sgu).reshape(B, T, D_GM)
    gather = lambda cache: cache[page_table].reshape(B, -1, 2, N_KV, HEAD_DIM)
    full_c = jnp.concatenate([gather(cache_c), kvc], axis=1)
    full_s = jnp.concatenate([gather(cache_s), kvs], axis=1)
    kc, vc, c_end, ks, vs = nsa_keys(full_c, full_s, g_k, pos_cmp_k, w_cmp_k, pos_cmp_v, w_cmp_v)
    nb = win_buf.shape[1]
    full_w = jnp.concatenate([win_buf, kvw], axis=1)
    kw = rmsnorm(full_w[:, :, 0], g_k[2])
    vw = full_w[:, :, 1]
    o_b = nsa_block(q, PAST_LEN + jnp.arange(T), gates, kc, vc, c_end, ks, vs, kw, vw,
                    PAST_LEN - nb + jnp.arange(nb + T), rel_bias).reshape(B, T, D_NSA)
    y = merge_ffn(x, o_a, o_b, g_a, g_b, w_proj_gmlp, w_proj_nsa, w_out, g_mlp_norm, w_up, w_down)
    return y, kvc, kvs, full_w[:, nb + T - min(WINDOW, PAST_LEN + T):], v

def setup_inputs(seed: int = 0) -> dict:
    key = jax.random.key(seed)
    ks = jax.random.split(key, 32)
    n_pages = PAST_LEN // PAGE_SIZE
    n_pool = (5 * DEC_BATCH * n_pages) // 4
    win_buf = min(WINDOW, PAST_LEN)
    nrm = lambda k, shape, scale: jax.random.normal(k, shape, jnp.float32) * scale
    gain = lambda k, shape: 1.0 + 0.02 * jax.random.normal(k, shape, jnp.float32)
    page_table = jax.random.permutation(ks[0], n_pool)[:DEC_BATCH * n_pages]
    page_table = page_table.reshape(DEC_BATCH, n_pages).astype(jnp.int32)
    return {
        'x_prompt': nrm(ks[1], (BATCH, SEQ, D_MODEL), 1.0),
        'x_sample': nrm(ks[2], (DEC_BATCH, DEC_SEQ, D_MODEL), 1.0),
        'cache_cmp_kv': nrm(ks[3], (DEPTH, n_pool, PAGE_SIZE, 2, N_KV, HEAD_DIM), 1.0),
        'cache_sel_kv': nrm(ks[4], (DEPTH, n_pool, PAGE_SIZE, 2, N_KV, HEAD_DIM), 1.0),
        'state_win_kv': nrm(ks[5], (DEPTH, DEC_BATCH, win_buf, 2, N_KV, HEAD_DIM), 1.0),
        'page_table': page_table,
        'rel_bias': nrm(ks[6], (N_BUCKETS, N_HEADS), 0.5),
        'g_mix_norm': gain(ks[7], (DEPTH, D_MODEL)),
        'w_in': nrm(ks[8], (DEPTH, D_MODEL, N_IN), D_MODEL ** -0.5),
        'g_sgu': gain(ks[9], (DEPTH, D_GM)),
        'w_sgu': nrm(ks[10], (DEPTH, SGU_GROUPS, CHUNK, CHUNK), 0.5 * CHUNK ** -0.5),
        'b_sgu': 1.0 + nrm(ks[11], (DEPTH, SGU_GROUPS, CHUNK), 0.1),
        'g_q': gain(ks[12], (DEPTH, HEAD_DIM)),
        'g_k': gain(ks[13], (DEPTH, 3, HEAD_DIM)),
        'pos_cmp_k': nrm(ks[14], (DEPTH, CMP_LEN, HEAD_DIM), 0.1),
        'w_cmp_k': nrm(ks[15], (DEPTH, CMP_LEN, HEAD_DIM, HEAD_DIM), (CMP_LEN * HEAD_DIM) ** -0.5),
        'pos_cmp_v': nrm(ks[16], (DEPTH, CMP_LEN, HEAD_DIM), 0.1),
        'w_cmp_v': nrm(ks[17], (DEPTH, CMP_LEN, HEAD_DIM, HEAD_DIM), (CMP_LEN * HEAD_DIM) ** -0.5),
        'w_proj_gmlp': nrm(ks[18], (DEPTH, D_GM, D_MODEL), D_GM ** -0.5),
        'w_proj_nsa': nrm(ks[19], (DEPTH, D_NSA, D_MODEL), D_NSA ** -0.5),
        'w_out': nrm(ks[20], (DEPTH, D_MODEL, D_MODEL), D_MODEL ** -0.5),
        'g_mlp_norm': gain(ks[21], (DEPTH, D_MODEL)),
        'w_up': nrm(ks[22], (DEPTH, D_MODEL, D_FF), D_MODEL ** -0.5),
        'w_down': nrm(ks[23], (DEPTH, D_FF, D_MODEL), D_FF ** -0.5),
    }

def reference(x_prompt, x_sample, cache_cmp_kv, cache_sel_kv, state_win_kv, page_table, rel_bias,
              g_mix_norm, w_in, g_sgu, w_sgu, b_sgu, g_q, g_k, pos_cmp_k, w_cmp_k, pos_cmp_v, w_cmp_v,
              w_proj_gmlp, w_proj_nsa, w_out, g_mlp_norm, w_up, w_down):
    x_p, x_s = x_prompt, x_sample
    outs = [[] for _ in range(8)]
    for l in range(DEPTH):
        lw = (g_mix_norm[l], w_in[l], g_sgu[l], w_sgu[l], b_sgu[l], g_q[l], g_k[l], pos_cmp_k[l],
              w_cmp_k[l], pos_cmp_v[l], w_cmp_v[l], w_proj_gmlp[l], w_proj_nsa[l], w_out[l],
              g_mlp_norm[l], w_up[l], w_down[l])
        x_p, pc, ps, pw, pv = layer_prompt(x_p, rel_bias, *lw)
        x_s, sc, ss, sw, sv = layer_sample(x_s, cache_cmp_kv[l], cache_sel_kv[l], state_win_kv[l],
                                           page_table, rel_bias, *lw)
        for lst, a in zip(outs, (pc, ps, pw, pv, sc, ss, sw, sv)):
            lst.append(a)
    p_cmp, p_sel, p_win, p_v, s_cmp, s_sel, s_win, s_v = [jnp.stack(a) for a in outs]
    return (x_p, x_s, p_cmp, p_sel, p_win, p_v, s_cmp, s_sel, s_win, s_v)


_drawn_inputs = setup_inputs


def setup_inputs(seed=0):
    import zlib

    import numpy as np

    out = dict(_drawn_inputs(seed))
    spreads = {}
    factors = {'g_mix_norm': 2.73,
     'g_sgu': 2.832,
     'g_q': 8.0,
     'g_k': 8.0,
     'pos_cmp_k': 8.0,
     'g_mlp_norm': 3.158}
    for name, (base, spread) in spreads.items():
        noise = np.random.default_rng([zlib.crc32(name.encode()), seed]).standard_normal(out[name].shape)
        drawn = base * np.exp(spread * noise) if base else spread * noise
        out[name] = jnp.asarray(drawn.astype(out[name].dtype))
    for name, factor in factors.items():
        out[name] = (out[name] * factor).astype(out[name].dtype)
    return out
```

```python
from contextlib import ExitStack, contextmanager

import numpy as np

import concourse.bass as bass
from concourse import mybir

F32 = mybir.dt.float32
F32R = mybir.dt.float32r
I32 = mybir.dt.int32
ALU = mybir.AluOpType
ACT = mybir.ActivationFunctionType

P = 128
D_MODEL, SEQ, DEC, PAST, PAGE = 2048, 512, 8, 256, 128
HD, NH, NKV, REP = 128, 8, 2, 4
D_GM, GRP, D_FF = 1024, 8, 8192
CMP_LEN, STRIDE = 32, 16
N_POOL = 20
EPS = 1e-6
NEG = -1e30
NB = 32

TOK = SEQ + DEC
HT = TOK // 2
KT = D_MODEL // P
CH = 4
CK = KT // CH
CW = CK * P
MB = D_MODEL // P
NCH = SEQ // P
NPG = PAST // PAGE

U_CMP, U_KV, U_Q, U_VU, U_GATE = 0, 4, 12, 20, 36
U_PROJ = U_GATE + 2 * MB
U_OUT = U_PROJ + MB
U_FF = U_OUT + MB
FG = D_FF // D_MODEL
UNITS = U_FF + 2 * MB * FG

L_ALL = SEQ + DEC * PAST
W_ALL = L_ALL // STRIDE
KVT_W = L_ALL + CMP_LEN
W_PROMPT = (SEQ - CMP_LEN) // STRIDE + 1
W_SAMPLE = (PAST - CMP_LEN) // STRIDE + 1
W_USED = W_ALL
CJ = 8
NREL = 640
N_GATE = 3 * NH


def seen(i):
    return (P * (i + 1) - CMP_LEN) // STRIDE + 1


class Steps:

    def __init__(self, eng, sem):
        self.eng, self.sem, self.n, self.local = eng, sem, 0, 0

    def did(self, ins):
        ins.then_inc(self.sem, 1)
        self.local += 1
        self.n = self.n + 1
        self.eng.wait_ge(self.sem, self.n)

    @contextmanager
    def loop(self, first, last, per):
        with self.eng.Fori(first, last) as i:
            before, start = self.local, self.n
            self.n = start + (i - first) * per
            yield i
            assert self.local - before == per, (self.local - before, per)
        self.local = before + per * (last - first)
        self.n = start + per * (last - first)


def build(nc, t):
    with ExitStack() as ctx:
        def sem(name):
            return ctx.enter_context(nc.semaphore(name))

        def dram(name, shape):
            return nc.dram_tensor(name, shape, F32).ap()

        base = nc.sbuf_base + (-nc.sbuf_base) % 64
        top = [base]

        def at(name, shape, offset, dt=F32):
            assert offset % 32 == 0, name
            size = 4 * int(np.prod(shape[1:]))
            assert offset + size <= nc.sbuf_usable_end, (name, offset + size - nc.sbuf_usable_end)
            return nc.alloc_sbuf_tensor_at(name, shape, dt, offset=offset)

        def new(name, shape, dt=F32):
            o = top[0]
            size = 4 * int(np.prod(shape[1:]))
            top[0] = o + size + (-size) % 32
            return at(name, shape, o, dt)

        w_raw = new("w_raw", [P, 4, 2 * CW])
        w_hi = new("w_hi", [P, CH, CW], F32R)
        w_lo = new("w_lo", [P, CH, CW], F32R)
        a_hi = new("a_hi", [P, KT, TOK], F32R)
        a_lo = new("a_lo", [P, KT, TOK], F32R)
        ones = new("ones", [P, P])
        ident = new("ident", [P, P])
        gains = new("gains", [P, 48])
        z = new("z", [P, 2, TOK])
        na = new("na", [P, TOK])
        nr = new("nr", [P, TOK])
        nq = new("nq", [P, TOK])
        rstd = new("rstd", [P, TOK])
        small = new("small", [P, 192])

        g_mix = gains[:, 0:16]
        g_mlp = gains[:, 16:32]
        g_sgu = gains[:, 32:40]
        g_q = gains[:, 40:41]
        g_k = gains[:, 41:44]
        g_qs = gains[:, 44:45]
        mx = small[:, 0:3]
        mn = small[:, 4:7]
        ls = small[:, 8:11]
        rl = small[:, 12:15]
        k_ss = small[:, 16:24]
        k_a = small[:, 24:32]
        k_r = small[:, 32:40]
        k_q = small[:, 40:48]
        k_rs = small[:, 48:56]
        tok_rstd = small[:, 56:64]
        w00 = small[:, 64:72]
        v_new = small[:, 80:112].rearrange("p (s b) -> p s b", s=4)
        gs_row = small[0:NH, 112:136].rearrange("p (b j) -> p b j", b=DEC)
        vs_tmp = small[:, 136:144]
        qm = small[:, 144:160].rearrange("p (g h) -> p g h", g=NKV)
        v_new_b = small[:, 160:164]

        zone = top[0]
        q_t = new("q_t", [P, NH, TOK])
        k_t = new("k_t", [P, 4, TOK])
        v_row = new("v_row", [P, 4, NCH, HD])
        kc_t = new("kc_t", [P, NKV, W_USED])
        vc_t = new("vc_t", [P, NKV, W_USED])
        vc_p = new("vc_p", [32, NKV, HD])
        gates = new("gates", [P, NCH + 1, N_GATE])
        r1 = top[0]
        kv_t = new("kv_t", [P, 4, KVT_W])
        r1_end = top[0]
        x_raw = at("x_raw", [P, KT, TOK], r1)
        u_t = at("u_t", [P, GRP, TOK], r1)
        v_t = at("v_t", [P, GRP, TOK], r1 + 4 * GRP * TOK)
        r1b = r1 + 8 * GRP * TOK
        ks_t = at("ks_t", [P, NKV, PAST + 4], r1b)
        kw_t = at("kw_t", [P, NKV, PAST + 4], r1b + 2080)
        sp = at("sp", [NH, 3, PAST + 4], r1b + 4160)
        p_s = at("p_s", [P, SEQ], r1b)
        p_w = at("p_w", [P, SEQ], r1b + 2048)
        p_c = at("p_c", [P, 32], r1b + 4096)
        assert r1b + 8192 <= r1_end
        r2 = top[0]
        w_cmp = new("w_cmp", [P, 2, CJ, HD])
        pages = new("pages", [P, 2, NPG, 512])
        r2_end = top[0]
        stage = at("stage", [P, 4, 512], r2)
        v_new_r = at("v_new_r", [1, 4, HD], r2 + 8192)
        vc_s = at("vc_s", [16, NKV, HD], r2 + 8192 + 2048)
        pt_s = at("pt_s", [P, 64], r2 + 8192 + 2048 + 1024)
        toep = at("toep", [P, SEQ], r2)
        wm = at("wm", [P, GRP, P], r2 + 2048)
        b_bc = at("b_bc", [P, GRP, P], r2 + 2048 + 4096)
        pt_sel = at("pt_sel", [P, NCH, P], r2 + 10240)
        pt_win = at("pt_win", [P, NCH, P], r2 + 12288)
        pt_cmp = at("pt_cmp", [32, P], r2 + 14336)
        r3 = top[0]
        sq = new("sq", [P, TOK])
        acc_v = new("acc_v", [P, TOK])
        wg_hi = at("wg_hi", [P, KT, N_GATE], r2 + 8192, F32R)
        wg_lo = at("wg_lo", [P, KT, N_GATE], r2 + 8192 + 1536, F32R)
        wg_raw = at("wg_raw", [P, KT, N_GATE], r2 + 8192 + 3072)
        gz = at("gz", [P, NCH + 1, N_GATE], r2 + 8192 + 4608)
        v_g = at("v_g", [P, TOK], r3)
        q_h = at("q_h", [P, SEQ], r3 + 2080)
        vr_g = new("vr_g", [P, NCH, P])
        oh = at("oh", [NB + 1, NREL], r2)
        rb = at("rb", [NB + 1, NH], r2 + 4 * NREL)
        rel_row = at("rel_row", [NH, NREL], r2 + 4 * NREL + 64)
        vc_b = new("vc_b", [P, NKV, W_SAMPLE + 1])
        rel_s = new("rel_s", [NH, PAST + 4])
        table = new("table", [1, DEC * NPG], I32)
        b_hi = at("b_hi", [P, KT, TOK], zone, F32R)
        b_lo = at("b_lo", [P, KT, TOK], zone + 4 * KT * TOK, F32R)
        r4 = zone + 8 * KT * TOK
        x2 = at("x2", [P, MB, TOK], r4)
        acc_x = at("acc_x", [P, TOK], r4 + 4 * MB * TOK)
        g_in = at("g_in", [P, 2, 2, TOK], r4)

        ca, cb, cm = na, nr, nq

        mm = nc.alloc_psum_tensor("mm", [P, 4, 512], F32)
        aux = nc.alloc_psum_tensor("aux", [P, 4, 512], F32)


        rel_d = dram("rel_d", [NH, NREL])
        toep_d = dram("toep_d", [NH, P, SEQ])
        gate_d = dram("gate_d", [DEC, N_GATE])
        merge_d = dram("merge_d", [2 * MB, P, TOK])

        raw_loaded = [sem(f"raw_loaded{n}") for n in range(4)]
        hi_split = sem("hi_split")
        lo_split = sem("lo_split")
        chunk_done = sem("chunk_done")
        mm_read = sem("mm_read")
        a_ready = sem("a_ready")
        b_ready = sem("b_ready")
        act_hi = sem("act_hi")
        act_src = sem("act_src")
        x_loaded = [sem(f"x_loaded{n}") for n in range(CH)]
        consts_loaded = sem("consts_loaded")
        consts_set = sem("consts_set")
        x_squared = sem("x_squared")
        x_summed = sem("x_summed")
        squared = sem("squared")
        summed = sem("summed")
        norm_base = sem("norm_base")
        norm_guess = sem("norm_guess")
        z_made = mm_read
        z_read = sem("z_read")
        z_stored = [sem(f"z_stored{n}") for n in range(2)]
        z_copied = sem("z_copied")
        pos_loaded = sem("pos_loaded")
        v_turned = sem("v_turned")
        v_row_made = sem("v_row_made")
        rel_made, rel_done = sem("rel_made"), sem("rel_done")
        rel_stored, toep_stored = sem("rel_stored"), sem("toep_stored")
        toep_loaded = sem("toep_loaded")
        table_loaded = sem("table_loaded")
        page_loaded = [sem(f"page_loaded{n}") for n in range(2)]
        page_turned = sem("page_turned")
        page_read = sem("page_read")
        cmp_loaded = [sem(f"cmp_loaded{n}") for n in range(2)]
        cmp_used = sem("cmp_used")
        kc_made, vc_made = sem("kc_made"), sem("vc_made")
        vcp_turned, vcp_made = sem("vcp_turned"), sem("vcp_made")
        wg_loaded, wg_hi_made, wg_split = sem("wg_loaded"), sem("wg_hi_made"), sem("wg_split")
        gates_summed, gz_made, gz_tanh, gates_made = (sem("gates_summed"), sem("gz_made"),
                                                      sem("gz_tanh"), sem("gates_made"))
        gate_stored, gate_loaded = sem("gate_stored"), sem("gate_loaded")
        stage_loaded = sem("stage_loaded")
        smp_base, smp_guess, smp_keys = sem("smp_base"), sem("smp_guess"), sem("smp_keys")
        smp_vturned, smp_vmade = sem("smp_vturned"), sem("smp_vmade")
        smp_kturned, smp_ks, smp_kw = sem("smp_kturned"), sem("smp_ks"), sem("smp_kw")
        smp_scored, smp_max, smp_exp = sem("smp_scored"), sem("smp_max"), sem("smp_exp")
        smp_probs, smp_pturned, smp_pmade = sem("smp_probs"), sem("smp_pturned"), sem("smp_pmade")
        smp_out, smp_read = sem("smp_out"), sem("smp_read")
        smp_static = sem("smp_static")
        v_acc = sem("v_acc")
        gm_loaded, w_masked, v_normed = sem("gm_loaded"), sem("w_masked"), sem("v_normed")
        v_stored, win_stored = sem("v_stored"), sem("win_stored")
        q_copied = sem("q_copied")
        scored, s_max, s_exp, probs = sem("scored"), sem("s_max"), sem("s_exp"), sem("probs")
        p_turned, pt_sel_made, pt_made = sem("p_turned"), sem("pt_sel_made"), sem("pt_made")
        b7_made, b7_read = sem("b7_made"), sem("b7_read")
        g_tanh = sem("g_tanh")
        g_stored = [sem(f"g_stored{n}") for n in range(2)]
        g_loaded = [sem(f"g_loaded{n}") for n in range(2)]
        x_in_loaded = [sem(f"x_in_loaded{n}") for n in range(2)]
        x2_made, x2_squared = sem("x2_made"), sem("x2_squared")
        y_stored = sem("y_stored")
        dve_step, act_step, pool_step = sem("dve_step"), sem("act_step"), sem("pool_step")

        def carry(eng):
            if eng is nc.vector:
                eng.memset(small[:, 170:171], 0.0)
            else:
                eng.tensor_tensor(small[:, 171:172], ones[:, 0:1], ones[:, 0:1], ALU.mult)

        def num(u):
            return 2 * u[0] + u[1]

        def after(u):
            return (u[0], 1) if u[1] == 0 else (u[0] + 1, 0)

        def straight(n):
            return (n // 2, n % 2)

        def raw(u, c):
            return w_raw[:, 2 * u[1] + c // 2, (c % 2) * CW:(c % 2 + 1) * CW]

        def pair(v):
            return mm[:, 2 * v:2 * v + 2, 0:HT]

        def halves(ap):
            return ap.rearrange("p (a b) -> p a b", a=2)

        def mm_use(u):
            return num(u)

        def more(u):
            return not (type(u[0]) is int and num(u) == UNITS - 1)

        def ff_loops(eng, up, down):
            def group(f, pairs):
                with eng.Fori(0, MB // 2) as i:
                    for p in range(2):
                        up(f, i, p)
                with eng.Fori(0, pairs) as i:
                    for p in range(2):
                        down(f, i, p)

            with eng.Fori(0, FG - 1) as f:
                group(f, MB // 2)
            group(FG - 1, MB // 2 - 1)
            for p in range(2):
                down(FG - 1, MB // 2 - 1, p)

        GATE_OF = (1, 2, 0)
        CONSTS = 16 * 4
        N_NORM_K, N_NORM_Q = 1, 5
        N_NORM_C, N_NORM_V, N_NORM_X2 = 13, 14, 15

        block = ctx.enter_context(nc.Block())

        @block.sync
        def _(sp_):
            for c in range(CH):
                sp_.dma_start(x_raw[:, CK * c:CK * (c + 1), :],
                              t["x_t"][CK * c:CK * (c + 1)].rearrange("k p n -> p k n")
                              ).then_inc(x_loaded[c], 16)
                sp_.dma_start(w_raw[:, c, :], t["w"][c // 2, :, (c % 2) * 2 * CW:(c % 2 + 1) * 2 * CW]
                              ).then_inc(raw_loaded[c], 16)
            with sp_.Fori(1, UNITS // 2) as i:
                for n in range(4):
                    sp_.wait_ge(lo_split, 8 * i - 8 + 2 * n + 2)
                    sp_.dma_start(w_raw[:, n, :], t["w"][2 * i + n // 2, :, (n % 2) * 2 * CW:(n % 2 + 1) * 2 * CW]
                                  ).then_inc(raw_loaded[n], 16)
            with sp_.Fori(0, MB) as m:
                sp_.wait_ge(mm_read, UNITS + m + 1)
                sp_.dma_start(t["y_t"][m], x2[:, m, :]).then_inc(y_stored, 16)
            sp_.wait_ge(y_stored, 16 * MB)

        @block.tensor
        def _(pe):
            def unit(u, ah, al, ready, need, hooks=(), before=None, projections=False):
                n = num(u)
                for c in range(CH):
                    if type(n) is int and n == 0:
                        x_sums[c]()
                    pe.wait_ge(lo_split, 4 * n + c + 1)
                    pe.wait_ge(ready, need(c))
                    if projections:
                        v = c // 2
                        if c % 2 == 0:
                            pe.wait_ge(mm_read, 2 * n - U_PROJ - 1 + v)
                    else:
                        v = u[1]
                        if c == 0 and not (type(n) is int and n < 2):
                            pe.wait_ge(mm_read, before(u) if before else mm_use(u) - 1)
                    first = c % 2 == 0 if projections else c == 0
                    final = c % 2 == 1 if projections else c == CH - 1
                    for k in range(CK):
                        kt = CK * c + k
                        wh, wl = w_hi[:, c, k * P:(k + 1) * P], w_lo[:, c, k * P:(k + 1) * P]
                        for w, a, part in ((wh, ah, 0), (wh, al, 1), (wl, ah, 2)):
                            for h in range(2):
                                last = pe.matmul(mm[:, 2 * v + h, 0:HT], w, a[:, kt, h * HT:(h + 1) * HT],
                                                 start=first and k == 0 and part == 0,
                                                 stop=final and k == CK - 1 and part == 2)
                    last.then_inc(chunk_done, 1)
                    if c < len(hooks) and hooks[c]:
                        hooks[c]()

            def x_sum(c):
                def go():
                    for kt in range(CK * c, CK * (c + 1)):
                        pe.wait_ge(x_squared, kt + 1)
                        for h in range(2):
                            last = pe.matmul(aux[:, h, 0:HT], ones[:, :], z[:, kt % 2, h * HT:(h + 1) * HT],
                                             start=kt == 0, stop=kt == KT - 1)
                        last.then_inc(x_summed if kt < KT - 1 else summed, 1)
                return go

            x_sums = {c: x_sum(c) for c in range(CH)}

            def norm_sum(n, src=None, made=None):
                src = sq if src is None else src
                pe.wait_ge(*(made or (squared, n)))
                pe.wait_ge(norm_base, n)
                for h in range(2):
                    last = pe.matmul(aux[:, h, 0:HT], ones[:, :], src[:, h * HT:(h + 1) * HT],
                                     start=True, stop=True)
                last.then_inc(summed, 1)

            def turn_v(j):
                def go():
                    pe.wait_ge(z_made, U_KV + 2 * j + 2)
                    pe.wait_ge(v_row_made, j)
                    for k in range(NCH):
                        last = pe.transpose(aux[:, 2, k * P:(k + 1) * P], z[:, 1, k * P:(k + 1) * P], ident[:, :])
                    last.then_inc(v_turned, 1)
                return go

            def turn_pages(h, p):
                def go():
                    pe.wait_ge(page_loaded[p], page_count(h, p))
                    pe.wait_ge(v_row_made, 4)
                    pe.wait_ge(page_read, 2 * h)
                    for g in range(NPG):
                        for q in range(4):
                            last = pe.transpose(aux[:, 2 + g, q * P:(q + 1) * P],
                                                pages[:, p, g, q * P:(q + 1) * P], ident[:, :])
                        last.then_inc(page_turned, 1)
                return go

            def page_count(h, p):
                return 16 * (h - p + 2)

            x_need = lambda c: CK * (c + 1)

            pe.wait_ge(consts_set, 1)
            pe.wait_ge(consts_loaded, CONSTS)
            pe.matmul(aux[0:NH, 2, 0:512], rb[:, :], oh[:, 0:512], start=True, stop=True)
            pe.matmul(aux[0:NH, 3, 0:NREL - 512], rb[:, :], oh[:, 512:NREL], start=True, stop=True
                      ).then_inc(rel_made, 1)

            for n in range(U_KV):
                unit(straight(n), a_hi, a_lo, a_ready, x_need)
            for j in range(4):
                unit(straight(U_KV + 2 * j), a_hi, a_lo, a_ready, x_need,
                     [None, turn_v(j - 1) if j else None])
                unit(straight(U_KV + 2 * j + 1), a_hi, a_lo, a_ready, x_need,
                     [None, lambda: norm_sum(N_NORM_K + j)])

            unit(straight(U_Q), a_hi, a_lo, a_ready, x_need,
                 [None, turn_v(3), turn_pages(0, 0)])
            unit(straight(U_Q + 1), a_hi, a_lo, a_ready, x_need,
                 [None, lambda: norm_sum(N_NORM_Q), turn_pages(1, 1)])
            with pe.Fori(1, NH // 2) as i:
                for p in range(2):
                    unit((U_Q // 2 + i, p), a_hi, a_lo, a_ready, x_need,
                         [None, lambda: norm_sum(N_NORM_Q - 1 + 2 * i + p), turn_pages(2 * i + p, p)])
            norm_sum(N_NORM_Q + NH - 1)

            def compress(kv):
                for c in range(CMP_LEN // CJ):
                    n = kv * (CMP_LEN // CJ) + c
                    pe.wait_ge(cmp_loaded[n % 2], 16 * (n // 2 + 1))
                    for jj in range(CJ):
                        j = c * CJ + jj
                        last = pe.matmul(aux[:, 2 + kv, 0:NKV * (W_ALL + 1)], w_cmp[:, n % 2, jj, :],
                                         kv_t[:, NKV * kv:NKV * (kv + 1), j:j + STRIDE * W_ALL + 1:STRIDE],
                                         start=j == 0, stop=j == CMP_LEN - 1)
                    last.then_inc(cmp_used, 1)

            pe.wait_ge(page_read, NPG * DEC)
            pe.wait_ge(z_copied, U_KV)
            pe.wait_ge(pos_loaded, 64)
            compress(0)
            pe.wait_ge(wg_split, 1)
            pe.wait_ge(norm_base, N_NORM_Q + NH)
            for tb in range(NCH + 1):
                o = min(P * tb, TOK - P)
                for kt in range(KT):
                    for a, w, part in ((a_hi, wg_hi, 0), (a_hi, wg_lo, 1), (a_lo, wg_hi, 2)):
                        pe.matmul(aux[:, 1, N_GATE * tb:N_GATE * (tb + 1)], a[:, kt, o:o + P], w[:, kt, :],
                                  start=kt == 0 and part == 0, stop=kt == KT - 1 and part == 2)
            for tb in range(NCH + 1):
                o = min(P * tb, TOK - P)
                last = pe.transpose(aux[:, 1, 256 + tb:257 + tb], rstd[0:1, o:o + P], ident[0:1, 0:1])
            last.then_inc(gates_summed, 1)
            compress(1)
            pe.wait_ge(squared, N_NORM_C)
            pe.wait_ge(norm_base, N_NORM_C)
            pe.matmul(aux[:, 0, 0:NKV * W_USED], ones[:, :], sq[:, 0:NKV * W_USED], start=True, stop=True
                      ).then_inc(summed, 1)
            pe.wait_ge(vc_made, 1)
            for g in range(NKV):
                last = pe.transpose(aux[0:W_PROMPT, 2, g * P:(g + 1) * P], vc_t[:, g, 0:W_PROMPT], ident[:, :])
            last.then_inc(vcp_turned, 1)

            def smp_values(b):
                def go():
                    pe.wait_ge(smp_max, b)
                    pe.wait_ge(vcp_made, 1)
                    pe.wait_ge(smp_static, b + 1)
                    for s in range(4):
                        pe.transpose(aux[0:1, 2, s * P:(s + 1) * P], v_new_b[:, s:s + 1], ident[:, :])
                    for g in range(NKV):
                        last = pe.transpose(aux[0:W_SAMPLE, 3, g * P:(g + 1) * P], vc_b[:, g, 0:W_SAMPLE],
                                            ident[:, :])
                    last.then_inc(smp_vturned, 1)
                return go

            def smp_turn_keys(b):
                def go():
                    pe.wait_ge(smp_keys, b + 1)
                    pe.wait_ge(smp_pmade, b)
                    pe.wait_ge(smp_read, b)
                    for br in range(2):
                        for g in range(NKV):
                            for k in range(NPG):
                                last = pe.transpose(aux[:, br, (2 * g + k) * P:(2 * g + k + 1) * P],
                                                    stage[:, 2 * br + k, g * P:(g + 1) * P], ident[:, :])
                        last.then_inc(smp_kturned, 1)
                return go

            def smp_scores(b):
                def go():
                    pe.wait_ge(smp_ks, b + 1)
                    pe.wait_ge(smp_kw, b + 1)
                    pe.wait_ge(smp_vmade, b + 1)
                    for g in range(NKV):
                        pe.matmul(aux[0:NH, 2, 0:PAST + 1], qm[:, g, :], ks_t[:, g, 0:PAST + 1],
                                  start=g == 0, stop=g == NKV - 1)
                    for g in range(NKV):
                        pe.matmul(aux[0:NH, 2, 300:300 + W_SAMPLE], qm[:, g, :],
                                  kc_t[:, g, bass.ds(SEQ // STRIDE + b * (PAST // STRIDE), W_SAMPLE)],
                                  start=g == 0, stop=g == NKV - 1)
                    for g in range(NKV):
                        last = pe.matmul(aux[0:NH, 3, 0:PAST + 1], qm[:, g, :], kw_t[:, g, 0:PAST + 1],
                                         start=g == 0, stop=g == NKV - 1)
                    last.then_inc(smp_scored, 1)
                return go

            def smp_turn_probs(b):
                def go():
                    pe.wait_ge(smp_probs, b + 1)
                    i8 = ident[0:NH, 0:NH]
                    for br in range(2):
                        for k in range(NPG):
                            pe.matmul(aux[:, 0, (2 * br + k) * NH:(2 * br + k + 1) * NH],
                                      sp[:, br, k * P:(k + 1) * P], i8, start=True, stop=True)
                        pe.transpose(aux[0:1, 0, (4 + br) * NH:(5 + br) * NH], sp[:, br, PAST:PAST + 1], i8)
                    pe.transpose(aux[0:W_SAMPLE, 0, 6 * NH:7 * NH], sp[:, 2, 0:W_SAMPLE], i8
                                 ).then_inc(smp_pturned, 1)
                return go

            def smp_attend(b):
                def go():
                    pe.wait_ge(smp_pmade, b + 1)
                    for g in range(NKV):
                        o = aux[:, 1, REP * g:REP * (g + 1)]
                        cut = lambda n, rows: pt_s[0:rows, n * NH + REP * g:n * NH + REP * (g + 1)]
                        vg = slice((NKV + g) * HD, (NKV + g + 1) * HD)
                        for n in range(4):
                            pe.matmul(o, stage[:, n, vg], cut(n, P), start=n == 0, stop=False)
                        for br in range(2):
                            pe.matmul(o, v_new_r[0:1, 2 * br + g, :], cut(4 + br, 1), start=False, stop=False)
                        last = pe.matmul(o, vc_s[0:W_SAMPLE, g, :], cut(6, W_SAMPLE), start=False, stop=True)
                    last.then_inc(smp_out, 1)
                return go

            with pe.Fori(0, DEC) as b:
                unit((U_VU // 2 + b, 0), a_hi, a_lo, a_ready, x_need,
                     [None, None, smp_values(b), smp_turn_keys(b)])
                unit((U_VU // 2 + b, 1), a_hi, a_lo, a_ready, x_need,
                     [smp_scores(b), None, smp_turn_probs(b), smp_attend(b)])
            pe.wait_ge(smp_read, DEC)
            norm_sum(N_NORM_V, acc_v, (v_acc, GRP))

            def scores(g, h, i):
                def go():
                    a = NCH * h + i
                    pe.wait_ge(q_copied, h + 1)
                    pe.wait_ge(pt_sel_made, a)
                    pe.wait_ge(pt_made, a)
                    qi = q_h[:, P * i:P * (i + 1)]
                    pe.matmul(aux[:, 0, 0:P * (i + 1)], qi, k_t[:, g, 0:P * (i + 1)], start=True, stop=True)
                    pe.matmul(aux[:, 1, 0:P * (i + 1)], qi, k_t[:, 2 + g, 0:P * (i + 1)], start=True, stop=True)
                    pe.matmul(aux[:, 2, 0:seen(i)], qi, kc_t[:, g, 0:seen(i)], start=True, stop=True
                              ).then_inc(scored, 1)
                return go

            def turn_probs(g, h, i):
                def go():
                    pe.wait_ge(probs, NCH * h + i + 1)
                    for n, src in enumerate((p_s, p_w)):
                        for k in range(i + 1):
                            pe.transpose(aux[:, n, k * P:(k + 1) * P], src[:, k * P:(k + 1) * P], ident[:, :])
                    pe.transpose(aux[0:seen(i), 2, 0:P], p_c[:, 0:seen(i)], ident[:, :]).then_inc(p_turned, 1)
                return go

            def attend(g, h, i):
                def go():
                    pe.wait_ge(pt_sel_made, NCH * h + i + 1)
                    pe.wait_ge(pt_made, NCH * h + i + 1)
                    pe.wait_ge(b7_read, 6 * h + (1, 3, 4, 5)[i])
                    o = aux[:, 3, 0:P]
                    for k in range(i + 1):
                        pe.matmul(o, v_row[:, g, k, :], pt_sel[:, k, :], start=k == 0, stop=False)
                    for k in range(i + 1):
                        pe.matmul(o, v_row[:, 2 + g, k, :], pt_win[:, k, :], start=False, stop=False)
                    pe.matmul(o, vc_p[0:seen(i), g, :], pt_cmp[0:seen(i), :], start=False, stop=True
                              ).then_inc(b7_made, 1)
                return go

            def turn_group(h):
                def go():
                    pe.wait_ge(q_copied, h + 1)
                    pe.wait_ge(b7_read, 6 * h)
                    for k in range(NCH):
                        last = pe.transpose(aux[:, 3, k * P:(k + 1) * P], v_g[:, k * P:(k + 1) * P], ident[:, :])
                    last.then_inc(b7_made, 1)
                return go

            def mix_group(h):
                def go():
                    pe.wait_ge(w_masked, 1)
                    pe.wait_ge(b7_read, 6 * h + 2)
                    for k in range(NCH):
                        last = pe.matmul(aux[:, 3, k * P:(k + 1) * P], vr_g[:, k, :], wm[:, h, :],
                                         start=True, stop=True)
                    last.then_inc(b7_made, 1)
                return go

            for g in range(NKV):
                with pe.Fori(REP * g, REP * (g + 1)) as h:
                    for i in range(NCH):
                        u = (U_GATE // 2 + 2 * h + i // 2, i % 2)
                        unit(u, a_hi, a_lo, a_ready, x_need,
                             [scores(g, h, i), (turn_group(h), mix_group(h), None, None)[i],
                              turn_probs(g, h, i), attend(g, h, i)])

            with pe.Fori(0, MB // 2) as i:
                for p in range(2):
                    unit((U_PROJ // 2 + i, p), a_hi, a_lo, a_ready, lambda c: KT + CK * (c + 1),
                         projections=True)
            late = lambda u: num(u) + MB - 1
            with pe.Fori(0, MB // 2) as i:
                for p in range(2):
                    unit((U_OUT // 2 + i, p), b_hi, b_lo, b_ready, x_need, before=late)
            norm_sum(N_NORM_X2, acc_x, (x2_squared, MB))
            with pe.Fori(0, FG) as f:
                with pe.Fori(0, MB // 2) as i:
                    for p in range(2):
                        unit((U_FF // 2 + MB * f + i, p), a_hi, a_lo, a_ready,
                             lambda c: 2 * KT + CK * (c + 1), before=late)
                with pe.Fori(0, MB // 2) as i:
                    for p in range(2):
                        unit((U_FF // 2 + MB // 2 + MB * f + i, p), b_hi, b_lo, b_ready,
                             lambda c: KT + KT * f + CK * (c + 1), before=late)

        @block.scalar
        def _(act):
            steps = Steps(act, act_step)
            run = act.activation

            def hi(u, c):
                n = num(u)
                if c % 2 == 0:
                    act.wait_ge(raw_loaded[2 * u[1] + c // 2], 16 * (u[0] + 1))
                if not (type(n) is int and n == 0):
                    act.wait_ge(chunk_done, 4 * n - 3 + c)
                run(w_hi[:, c, :], raw(u, c), ACT.Copy).then_inc(hi_split, 1)

            def beside(u, jobs=()):
                for c in range(CH):
                    hi(after(u), c)
                    if c < len(jobs) and jobs[c]:
                        jobs[c]()

            def guess(n, w=TOK):
                act.wait_ge(norm_base, n + 1)
                steps.did(run(nr[:, 0:w], na[:, 0:w], ACT.Ln))
                steps.did(run(nr[:, 0:w], nr[:, 0:w], ACT.Exp, scale=-0.5))
                run(nq[:, 0:w], nr[:, 0:w], ACT.Square).then_inc(norm_guess, 1)

            act.wait_ge(consts_loaded, CONSTS)
            for c in range(CH):
                hi(straight(0), c)
                act.wait_ge(x_loaded[c], 16)
                for kt in range(CK * c, CK * (c + 1)):
                    run(a_hi[:, kt, :], x_raw[:, kt, :], ACT.Copy, scale=g_mix[:, kt:kt + 1]).then_inc(act_hi, 1)
                    if kt >= 2:
                        act.wait_ge(x_summed, kt - 1)
                    run(z[:, kt % 2, :], x_raw[:, kt, :], ACT.Square).then_inc(x_squared, 1)
            guess(0)

            def store(n):
                act.wait_ge(z_made, n + 1)
                act.dma_start(t["kv_t"][n], z[:, n % 2, :]).then_inc(z_stored[n % 2], 16)

            def square(n, u, src):
                act.wait_ge(z_made, num(u) + 1)
                act.wait_ge(summed, n)
                run(sq[:, :], src, ACT.Square).then_inc(squared, 1)

            def v_rows(j):
                act.wait_ge(v_turned, j + 1)
                run(v_row[:, j, :, :], aux[:, 2, :].rearrange("p (k d) -> p k d", k=NCH), ACT.Copy
                    ).then_inc(v_row_made, 1)

            for n in range(U_KV):
                beside(straight(n))
                store(n)
            for j in range(4):
                beside(straight(U_KV + 2 * j), [None, None, (lambda: v_rows(j - 1)) if j else None])
                store(U_KV + 2 * j)
                square(N_NORM_K + j, straight(U_KV + 2 * j), z[:, 0, :])
                beside(straight(U_KV + 2 * j + 1), [None, lambda: guess(N_NORM_K + j)])
                store(U_KV + 2 * j + 1)
            beside(straight(U_Q), [None, None, lambda: v_rows(3)])
            square(N_NORM_Q, straight(U_Q), z[:, 0, :])
            beside(straight(U_Q + 1), [None, lambda: guess(N_NORM_Q)])
            square(N_NORM_Q + 1, straight(U_Q + 1), z[:, 1, :])
            with steps.loop(1, NH // 2, 4) as i:
                for p in range(2):
                    u = (U_Q // 2 + i, p)
                    beside(u, [None, lambda: guess(N_NORM_Q - 1 + 2 * i + p)])
                    square(N_NORM_Q + 2 * i + p, u, z[:, p, :])
            guess(N_NORM_Q + NH - 1)
            act.wait_ge(wg_loaded, 16)
            run(wg_hi[:, :, :], wg_raw[:, :, :], ACT.Copy).then_inc(wg_hi_made, 1)
            act.wait_ge(kc_made, 1)
            act.wait_ge(summed, N_NORM_C)
            run(sq[:, 0:NKV * W_USED], kc_t[:, :, :].rearrange("p g w -> p (g w)"), ACT.Square).then_inc(squared, 1)
            act.wait_ge(gz_made, 1)
            run(gz[:, :, :], gz[:, :, :], ACT.Tanh, scale=0.5).then_inc(gz_tanh, 1)
            guess(N_NORM_C, NKV * W_USED)

            def smp_norm_guess(b):
                act.wait_ge(smp_base, b + 1)
                steps.did(run(k_r, k_a, ACT.Ln))
                steps.did(run(k_r, k_r, ACT.Exp, scale=-0.5))
                run(k_q, k_r, ACT.Square).then_inc(smp_guess, 1)

            def smp_exps(b):
                act.wait_ge(smp_max, b + 1)
                for n, w in enumerate((PAST + 1, PAST + 1, W_SAMPLE)):
                    last = run(sp[:, n, 0:w], sp[:, n, 0:w], ACT.Exp, bias=mn[0:NH, n:n + 1],
                               accum_out=ls[0:NH, GATE_OF[n]:GATE_OF[n] + 1])
                last.then_inc(smp_exp, 1)

            with steps.loop(0, DEC, 2) as b:
                beside((U_VU // 2 + b, 0), [None, lambda: smp_norm_guess(b)])
                act.wait_ge(smp_kturned, 2 * b + 1)
                run(ks_t[:, :, 0:PAST], aux[:, 0, :].rearrange("p (g k) -> p g k", g=NKV), ACT.Copy,
                    scale=g_k[:, 1:2]).then_inc(smp_ks, 1)
                act.wait_ge(z_made, U_VU + 2 * b + 1)
                run(v_t[:, b, :], z[:, 0, :], ACT.Gelu_apprx_tanh).then_inc(z_read, 1)
                beside((U_VU // 2 + b, 1), [lambda: smp_exps(b)])
                act.wait_ge(z_made, U_VU + 2 * b + 2)
                run(u_t[:, b, :], z[:, 1, :], ACT.Gelu_apprx_tanh).then_inc(z_read, 1)
            guess(N_NORM_V)
            act.wait_ge(v_normed, 1)
            act.dma_start(t["v_t"], v_t[:, :, SEQ - P:TOK]).then_inc(v_stored, 16)
            act.dma_start(t["win"], t["state"]).then_inc(win_stored, 16)

            def exps(a, i):
                act.wait_ge(s_max, a + 1)
                for n, (x, w) in enumerate(((p_s, P * (i + 1)), (p_w, P * (i + 1)), (p_c, seen(i)))):
                    last = run(x[:, 0:w], x[:, 0:w], ACT.Exp, bias=mn[:, n:n + 1],
                               accum_out=ls[:, GATE_OF[n]:GATE_OF[n] + 1])
                last.then_inc(s_exp, 1)

            def probs_out(a, i):
                act.wait_ge(p_turned, a + 1)
                run(pt_sel[:, 0:i + 1, :], aux[:, 0, 0:P * (i + 1)].rearrange("p (k q) -> p k q", k=i + 1),
                    ACT.Copy).then_inc(pt_sel_made, 1)

            act.wait_ge(toep_stored, 16)
            act.wait_ge(smp_read, DEC)
            for g in range(NKV):
                with steps.loop(REP * g, REP * (g + 1), 0) as h:
                    act.wait_ge(s_max, NCH * h)
                    act.dma_start(toep[:, :], toep_d[h]).then_inc(toep_loaded, 16)
                    act.wait_ge(scored, NCH * h)
                    run(q_h[:, :], q_t[:, h, 0:SEQ], ACT.Copy)
                    run(v_g[:, :], v_t[:, h, :], ACT.Copy).then_inc(q_copied, 1)
                    for i in range(NCH):
                        a = NCH * h + i
                        u = (U_GATE // 2 + 2 * h + i // 2, i % 2)
                        beside(u, [lambda: exps(a, i), None, lambda: probs_out(a, i)])
                        act.wait_ge(z_made, num(u) + 1)
                        run(z[:, i % 2, :], z[:, i % 2, :], ACT.Tanh, scale=0.5).then_inc(g_tanh, 1)

            act.wait_ge(b7_read, 6 * NH)
            act.wait_ge(chunk_done, CH * U_PROJ)
            act.wait_ge(v_stored, 16)
            for kt in range(KT):
                src = u_t[:, kt, :] if kt < GRP else q_t[:, kt - GRP, :]
                run(a_hi[:, kt, :], src, ACT.Copy).then_inc(act_hi, 1)

            def split_hi(count, dst, src, func=ACT.Copy):
                act.wait_ge(act_src, count)
                run(dst, src, func).then_inc(act_hi, 1)

            with steps.loop(0, MB // 2, 0) as i:
                for p in range(2):
                    beside((U_PROJ // 2 + i, p))
                    split_hi(1 + 2 * i + p, b_hi[:, 2 * i + p, :], cm[:, :])
            with steps.loop(0, MB // 2, 0) as i:
                for p in range(2):
                    beside((U_OUT // 2 + i, p))
                    split_hi(1 + MB + 2 * i + p, a_hi[:, 2 * i + p, :], na[:, :])
            guess(N_NORM_X2)

            def up(f, i, p):
                beside((U_FF // 2 + MB * f + i, p))
                split_hi(1 + 2 * MB + MB * f + 2 * i + p, b_hi[:, 2 * i + p, :], z[:, p, :], ACT.Square)

            def down(f, i, p):
                u = (U_FF // 2 + MB // 2 + MB * f + i, p)
                if more(u):
                    beside(u)

            ff_loops(act, up, down)
            act.wait_ge(win_stored, 16)
            for p in range(2):
                act.wait_ge(z_stored[p], 16 * (U_Q // 2))

        @block.vector
        def _(dve):
            steps = Steps(dve, dve_step)

            def lo(u, c):
                n = num(u)
                dve.wait_ge(hi_split, 4 * n + c + 1)
                dve.tensor_tensor(w_lo[:, c, :], raw(u, c), w_hi[:, c, :].bitcast(F32), ALU.subtract
                                  ).then_inc(lo_split, 1)

            def beside(u, jobs=()):
                for c in range(CH):
                    lo(after(u), c)
                    if c < len(jobs) and jobs[c]:
                        jobs[c]()

            def mean(n, count, w=None):
                dve.wait_ge(summed, n + 1)
                dst, src = (halves(na[:, :]), aux[:, 0:2, 0:HT]) if w is None else (na[:, 0:w], aux[:, 0, 0:w])
                dve.tensor_scalar(dst, src, 1.0 / count, EPS, ALU.mult, ALU.add).then_inc(norm_base, 1)

            def newton(n, dst, w=TOK):
                dve.wait_ge(norm_guess, n + 1)
                steps.did(dve.scalar_tensor_tensor(nq[:, 0:w], nq[:, 0:w], -0.5, na[:, 0:w], ALU.mult, ALU.mult))
                steps.did(dve.scalar_tensor_tensor(dst, nq[:, 0:w], 1.5, nr[:, 0:w], ALU.add, ALU.mult))

            def scale_out(u, dst):
                dve.wait_ge(chunk_done, CH * num(u) + CH)
                dve.tensor_tensor(halves(dst), pair(u[1]), halves(rstd[:, :]), ALU.mult).then_inc(mm_read, 1)

            dve.wait_ge(consts_loaded, CONSTS)
            steps.did(dve.tensor_scalar(g_qs, g_q, HD ** -0.5, None, ALU.mult))
            dve.wait_ge(rel_made, 1)
            dve.tensor_copy(rel_row[:, 0:512], aux[0:NH, 2, 0:512])
            steps.did(dve.tensor_copy(rel_row[:, 512:NREL], aux[0:NH, 3, 0:NREL - 512]))
            o = SEQ - 1 - PAST
            dve.tensor_copy(rel_s[:, 0:PAST + 1], rel_row[:, o:o + PAST + 1]).then_inc(rel_done, 1)

            for c in range(CH):
                lo(straight(0), c)
                for kt in range(CK * c, CK * (c + 1)):
                    dve.wait_ge(act_hi, kt + 1)
                    dve.scalar_tensor_tensor(a_lo[:, kt, :], x_raw[:, kt, :], g_mix[:, kt:kt + 1],
                                             a_hi[:, kt, :].bitcast(F32), ALU.mult, ALU.subtract).then_inc(a_ready, 1)
            mean(0, D_MODEL)
            newton(0, rstd[:, :])

            def z_free(n):
                if n >= 2:
                    dve.wait_ge(z_stored[n % 2], 16 * min(n // 2, U_Q // 2))
                if 2 <= n < U_KV + 2:
                    dve.wait_ge(z_copied, n - 1)
                if n > U_KV + 1 and n % 2 == 1:
                    dve.wait_ge(v_row_made, min((n - U_KV) // 2, 4))

            for n in range(U_KV):
                beside(straight(n))
                z_free(n)
                scale_out(straight(n), z[:, n % 2, :])

            def key_norm(j):
                newton(N_NORM_K + j, nr[:, :])
                dve.scalar_tensor_tensor(k_t[:, j, :], z[:, 0, :], g_k[:, 1 + j // 2:2 + j // 2], nr[:, :],
                                         ALU.mult, ALU.mult)

            def query_norm(h, p):
                newton(N_NORM_Q + h, nr[:, :])
                dve.scalar_tensor_tensor(q_t[:, h, :], z[:, p, :], g_qs, nr[:, :], ALU.mult, ALU.mult)

            def pages_in(h):
                for k in range(NPG):
                    dve.wait_ge(page_turned, 2 * h + k + 1)
                    dve.tensor_copy(kv_t[:, :, bass.ds(SEQ + PAST * h + PAGE * k, PAGE)],
                                    aux[:, 2 + k, :].rearrange("p (q n) -> p q n", q=4)).then_inc(page_read, 1)

            for j in range(4):
                n = U_KV + 2 * j
                beside(straight(n))
                z_free(n)
                scale_out(straight(n), z[:, 0, :])
                beside(straight(n + 1), [None, lambda: mean(N_NORM_K + j, HD), lambda: key_norm(j)])
                z_free(n + 1)
                scale_out(straight(n + 1), z[:, 1, :])
                dve.wait_ge(mm_read, n + 2)
                dve.tensor_copy(v_new[:, j, :], z[:, 1, SEQ:TOK])
            beside(straight(U_Q), [None, None, lambda: pages_in(0)])
            z_free(U_Q)
            scale_out(straight(U_Q), z[:, 0, :])
            beside(straight(U_Q + 1), [None, lambda: mean(N_NORM_Q, HD), lambda: (pages_in(1), query_norm(0, 0))])
            z_free(U_Q + 1)
            scale_out(straight(U_Q + 1), z[:, 1, :])
            with steps.loop(1, NH // 2, 4) as i:
                for p in range(2):
                    h = 2 * i + p
                    beside((U_Q // 2 + i, p), [None, lambda: mean(N_NORM_Q - 1 + h, HD),
                                               lambda: (pages_in(h), query_norm(h - 1, 1 - p))])
                    scale_out((U_Q // 2 + i, p), z[:, p, :])
            mean(N_NORM_Q + NH - 1, HD)
            query_norm(NH - 1, 1)

            dve.wait_ge(wg_hi_made, 1)
            dve.tensor_tensor(wg_lo[:, :, :], wg_raw[:, :, :], wg_hi[:, :, :].bitcast(F32), ALU.subtract
                              ).then_inc(wg_split, 1)

            def compressed(kv, dst, made):
                dve.wait_ge(cmp_used, (kv + 1) * CMP_LEN // CJ)
                src = aux[:, 2 + kv, 0:NKV * (W_ALL + 1)].rearrange("p (g w) -> p g w", g=NKV)
                steps.did(dve.tensor_copy(vs_tmp[:, kv:kv + 1], src[:, 0, W_ALL:W_ALL + 1]))
                dve.tensor_scalar(dst[:, :, :], src[:, :, 0:W_USED], vs_tmp[:, kv:kv + 1], None, ALU.add
                                  ).then_inc(made, 1)

            compressed(0, kc_t, kc_made)
            dve.wait_ge(gates_summed, 1)
            steps.did(dve.tensor_copy(tok_rstd[:, 0:NCH + 1], aux[:, 1, 256:256 + NCH + 1]))
            for tb in range(NCH + 1):
                last = dve.tensor_scalar(gz[:, tb, :], aux[:, 1, N_GATE * tb:N_GATE * (tb + 1)],
                                         tok_rstd[:, tb:tb + 1], None, ALU.mult)
            last.then_inc(gz_made, 1)
            dve.wait_ge(gz_tanh, 1)
            dve.tensor_scalar(gates[:, :, :], gz[:, :, :], 0.5, 0.5, ALU.mult, ALU.add).then_inc(gates_made, 1)
            compressed(1, vc_t, vc_made)
            mean(N_NORM_C, HD, NKV * W_USED)
            dve.wait_ge(vcp_turned, 1)
            dve.tensor_copy(vc_p[0:W_PROMPT, :, :], aux[0:W_PROMPT, 2, 0:NKV * P].rearrange("p (g d) -> p g d", g=NKV)
                            ).then_inc(vcp_made, 1)
            newton(N_NORM_C, nr[:, 0:NKV * W_USED], NKV * W_USED)
            steps.did(dve.scalar_tensor_tensor(kc_t[:, :, :], kc_t[:, :, :], g_k[:, 0:1],
                                               nr[:, 0:NKV * W_USED].rearrange("p (g w) -> p g w", g=NKV),
                                               ALU.mult, ALU.mult))

            def smp_copies(b):
                dve.tensor_copy(v_new_b, v_new[:, :, bass.ds(b, 1)].rearrange("p s o -> p (s o)"))
                dve.tensor_copy(vc_b[:, :, 0:W_SAMPLE],
                                vc_t[:, :, bass.ds(SEQ // STRIDE + b * (PAST // STRIDE), W_SAMPLE)]
                                ).then_inc(smp_static, 1)

            def smp_norms(b):
                dve.wait_ge(stage_loaded, 48 * b + 48)
                for n in range(4):
                    for g in range(NKV):
                        k = stage[:, n, g * HD:(g + 1) * HD]
                        junk = (na, nr)[n // 2][:, (2 * (n % 2) + g) * HD:(2 * (n % 2) + g + 1) * HD]
                        last = dve.tensor_tensor_reduce(junk, k, k, 1.0, 0.0, ALU.mult, ALU.add,
                                                        k_ss[:, 2 * n + g:2 * n + g + 1])
                steps.did(last)
                dve.tensor_scalar(k_a, k_ss, 1.0 / HD, EPS, ALU.mult, ALU.add).then_inc(smp_base, 1)

            def smp_scale_keys(b):
                dve.wait_ge(smp_guess, b + 1)
                steps.did(dve.scalar_tensor_tensor(k_q, k_q, -0.5, k_a, ALU.mult, ALU.mult))
                steps.did(dve.scalar_tensor_tensor(k_rs, k_q, 1.5, k_r, ALU.add, ALU.mult))
                for n in range(4):
                    for g in range(NKV):
                        k = stage[:, n, g * HD:(g + 1) * HD]
                        last = dve.tensor_scalar(k, k, k_rs[:, 2 * n + g:2 * n + g + 1], None, ALU.mult)
                last.then_inc(smp_keys, 1)
                dve.wait_ge(smp_vturned, b + 1)
                dve.tensor_copy(v_new_r[:, :, :], aux[0:1, 2, :].rearrange("p (s d) -> p s d", s=4))
                dve.tensor_copy(vc_s[0:W_SAMPLE, :, :],
                                aux[0:W_SAMPLE, 3, 0:NKV * P].rearrange("p (g d) -> p g d", g=NKV)
                                ).then_inc(smp_vmade, 1)

            def smp_keys_in(b):
                dve.wait_ge(smp_kturned, 2 * b + 2)
                dve.tensor_scalar(kw_t[:, :, 0:PAST], aux[:, 1, :].rearrange("p (g k) -> p g k", g=NKV),
                                  g_k[:, 2:3], None, ALU.mult)
                for br, dst in enumerate((ks_t, kw_t)):
                    dve.tensor_copy(dst[:, :, PAST:PAST + 1], k_t[:, 2 * br:2 * br + 2, bass.ds(SEQ + b, 1)])
                for g in range(NKV):
                    last = dve.tensor_copy(qm[:, g, REP * g:REP * (g + 1)],
                                           q_t[:, REP * g:REP * (g + 1), bass.ds(SEQ + b, 1)
                                               ].rearrange("p h o -> p (h o)"))
                last.then_inc(smp_kw, 1)

            def smp_softmax(b):
                dve.wait_ge(smp_scored, b + 1)
                carry(nc.vector)
                r = rel_s[:, 0:PAST + 1]
                rc = rel_s[:, CMP_LEN - 1:CMP_LEN - 1 + STRIDE * (W_SAMPLE - 1) + 1:STRIDE]
                for n, (s_, bias, w) in enumerate(((aux[0:NH, 2, 0:PAST + 1], r, PAST + 1),
                                                   (aux[0:NH, 3, 0:PAST + 1], r, PAST + 1),
                                                   (aux[0:NH, 2, 300:300 + W_SAMPLE], rc, W_SAMPLE))):
                    last = dve.tensor_tensor_reduce(sp[:, n, 0:w], s_, bias, 1.0, -3e38, ALU.add, ALU.max,
                                                    mx[0:NH, n:n + 1])
                steps.did(last)
                dve.tensor_scalar(mn[0:NH, :], mx[0:NH, :], -1.0, None, ALU.mult).then_inc(smp_max, 1)

            def smp_divide(b):
                dve.wait_ge(smp_exp, b + 1)
                steps.did(dve.reciprocal(rl[0:NH, :], ls[0:NH, :]))
                steps.did(dve.tensor_tensor(rl[0:NH, :], rl[0:NH, :],
                                            gs_row[:, bass.ds(b, 1), :].rearrange("p o j -> p (o j)"), ALU.mult))
                for n, w in ((0, PAST + 1), (1, PAST + 1), (2, W_SAMPLE)):
                    last = dve.tensor_scalar(sp[:, n, 0:w], sp[:, n, 0:w],
                                             rl[0:NH, GATE_OF[n]:GATE_OF[n] + 1], None, ALU.mult)
                last.then_inc(smp_probs, 1)

            def smp_probs_out(b):
                dve.wait_ge(smp_pturned, b + 1)
                dve.tensor_copy(pt_s[:, 0:4 * NH], aux[:, 0, 0:4 * NH])
                dve.tensor_copy(pt_s[0:1, 4 * NH:6 * NH], aux[0:1, 0, 4 * NH:6 * NH])
                dve.tensor_copy(pt_s[0:W_SAMPLE, 6 * NH:7 * NH], aux[0:W_SAMPLE, 0, 6 * NH:7 * NH]
                                ).then_inc(smp_pmade, 1)

            dve.wait_ge(gate_loaded, 16)
            dve.wait_ge(consts_set, 2)
            with steps.loop(0, DEC, 6) as b:
                dve.wait_ge(z_read, 2 * b)
                beside((U_VU // 2 + b, 0), [lambda: smp_copies(b), lambda: smp_norms(b),
                                            lambda: smp_scale_keys(b), lambda: smp_keys_in(b)])
                scale_out((U_VU // 2 + b, 0), z[:, 0, :])
                dve.wait_ge(z_read, 2 * b + 1)
                beside((U_VU // 2 + b, 1), [lambda: smp_softmax(b), lambda: smp_divide(b),
                                            lambda: smp_probs_out(b)])
                scale_out((U_VU // 2 + b, 1), z[:, 1, :])
                dve.wait_ge(smp_out, b + 1)
                carry(nc.vector)
                dve.tensor_copy(q_t[:, :, bass.ds(SEQ + b, 1)].rearrange("p h o -> p (h o)"), aux[:, 1, 0:NH]
                                ).then_inc(smp_read, 1)

            mean(N_NORM_V, D_GM)
            newton(N_NORM_V, nr[:, :])
            dve.wait_ge(z_read, 2 * GRP)
            for g in range(GRP):
                last = dve.scalar_tensor_tensor(v_t[:, g, :], v_t[:, g, :], g_sgu[:, g:g + 1], nr[:, :],
                                                ALU.mult, ALU.mult)
            last.then_inc(v_normed, 1)
            dve.wait_ge(v_normed, 1)
            dve.wait_ge(gm_loaded, 32)
            for g in range(GRP):
                last = dve.tensor_scalar(na[:, DEC * g:DEC * (g + 1)], v_t[:, g, SEQ:TOK], w00[:, g:g + 1],
                                         b_bc[:, g, 0:1], ALU.mult, ALU.add)
            steps.did(last)
            steps.did(dve.tensor_tensor(u_t[:, :, SEQ:TOK], u_t[:, :, SEQ:TOK],
                                        na[:, 0:DEC * GRP].rearrange("p (g b) -> p g b", g=GRP), ALU.mult))

            def softmax(h, a, i):
                dve.wait_ge(scored, a + 1)
                if i == 0:
                    dve.wait_ge(toep_loaded, 16 * h + 16)
                carry(nc.vector)
                o = SEQ - P * (i + 1)
                w = P * (i + 1)
                oc = o + CMP_LEN - 1
                for n, (x, s_, bias) in enumerate((
                        (p_s[:, 0:w], aux[:, 0, 0:w], toep[:, o:SEQ]),
                        (p_w[:, 0:w], aux[:, 1, 0:w], toep[:, o:SEQ]),
                        (p_c[:, 0:seen(i)], aux[:, 2, 0:seen(i)], toep[:, oc:oc + STRIDE * (seen(i) - 1) + 1:STRIDE]))):
                    last = dve.tensor_tensor_reduce(x, s_, bias, 1.0, -3e38, ALU.add, ALU.max, mx[:, n:n + 1])
                steps.did(last)
                dve.tensor_scalar(mn, mx, -1.0, -0.1 * NEG, ALU.mult, ALU.min).then_inc(s_max, 1)

            def divide(h, a, i):
                dve.wait_ge(s_exp, a + 1)
                steps.did(dve.tensor_scalar(ls, ls, 1e-30, None, ALU.max))
                steps.did(dve.reciprocal(rl, ls))
                steps.did(dve.tensor_tensor(rl, rl, gates[:, i, bass.ds(3 * h, 3)], ALU.mult))
                for n, (x, w) in enumerate(((p_s, P * (i + 1)), (p_w, P * (i + 1)), (p_c, seen(i)))):
                    last = dve.tensor_scalar(x[:, 0:w], x[:, 0:w], rl[:, GATE_OF[n]:GATE_OF[n] + 1], None, ALU.mult)
                last.then_inc(probs, 1)
                if i == 0:
                    dve.wait_ge(b7_made, 6 * h + 1)
                    dve.tensor_copy(vr_g[:, :, :], aux[:, 3, :].rearrange("p (k c) -> p k c", k=NCH)
                                    ).then_inc(b7_read, 1)
                if i == 1:
                    dve.wait_ge(b7_made, 6 * h + 3)
                    dve.tensor_tensor(na[:, 0:SEQ].rearrange("p (k t) -> p k t", k=NCH),
                                      aux[:, 3, :].rearrange("p (k t) -> p k t", k=NCH),
                                      b_bc[:, bass.ds(h, 1), :].to_broadcast([P, NCH, P]), ALU.add
                                      ).then_inc(b7_read, 1)
                    dve.wait_ge(b7_read, 6 * h + 3)
                    dve.tensor_tensor(u_t[:, h, 0:SEQ], u_t[:, h, 0:SEQ], na[:, 0:SEQ], ALU.mult)

            def probs_out(a, i):
                dve.wait_ge(p_turned, a + 1)
                dve.tensor_copy(pt_win[:, 0:i + 1, :], aux[:, 1, 0:P * (i + 1)].rearrange("p (k q) -> p k q", k=i + 1))
                dve.tensor_copy(pt_cmp[0:seen(i), :], aux[0:seen(i), 2, 0:P]).then_inc(pt_made, 1)

            dve.wait_ge(gates_made, 1)
            for g in range(NKV):
                with steps.loop(REP * g, REP * (g + 1), 16) as h:
                    for i in range(NCH):
                        a = NCH * h + i
                        u = (U_GATE // 2 + 2 * h + i // 2, i % 2)
                        beside(u, [lambda: softmax(h, a, i), lambda: divide(h, a, i), lambda: probs_out(a, i)])
                        dve.wait_ge(g_stored[i % 2], 32 * h + 16 * (i // 2))
                        scale_out(u, z[:, i % 2, :])
                        dve.wait_ge(b7_made, 6 * h + (2, 4, 5, 6)[i])
                        dve.tensor_copy(q_t[:, h, P * i:P * (i + 1)], aux[:, 3, 0:P]).then_inc(b7_read, 1)
            dve.wait_ge(chunk_done, CH * U_PROJ)
            for kt in range(KT):
                src = u_t[:, kt, :] if kt < GRP else q_t[:, kt - GRP, :]
                dve.wait_ge(act_hi, KT + kt + 1)
                dve.tensor_tensor(a_lo[:, kt, :], src, a_hi[:, kt, :].bitcast(F32), ALU.subtract).then_inc(a_ready, 1)

            with steps.loop(0, MB // 2, 0) as i:
                for p in range(2):
                    m = 2 * i + p
                    u = (U_PROJ // 2 + i, p)
                    n = num(u)

                    def first():
                        dve.wait_ge(g_loaded[p], 16 * i + 16)
                        dve.tensor_tensor(halves(ca[:, :]), pair(0), halves(g_in[:, p, 0, :]), ALU.mult
                                          ).then_inc(mm_read, 1)

                    beside(u, [None, first])
                    dve.wait_ge(chunk_done, CH * n + CH)
                    dve.tensor_tensor(halves(cb[:, :]), pair(1), halves(g_in[:, p, 1, :]), ALU.mult).then_inc(mm_read, 1)
                    dve.wait_ge(mm_read, 2 * n - U_PROJ + 2)
                    dve.tensor_tensor(cm[:, :], ca[:, :], cb[:, :], ALU.add).then_inc(act_src, 1)
                    dve.wait_ge(act_src, m + 1)
                    dve.wait_ge(act_hi, 2 * KT + m + 1)
                    dve.tensor_tensor(b_lo[:, m, :], cm[:, :], b_hi[:, m, :].bitcast(F32), ALU.subtract
                                      ).then_inc(b_ready, 1)

            with steps.loop(0, MB // 2, 0) as i:
                for p in range(2):
                    m = 2 * i + p
                    u = (U_OUT // 2 + i, p)
                    beside(u)
                    dve.wait_ge(x_in_loaded[p], 16 * i + 16)
                    dve.wait_ge(chunk_done, CH * num(u) + CH)
                    dve.tensor_tensor(halves(x2[:, m, :]), pair(p), halves(z[:, p, :]), ALU.add).then_inc(mm_read, 1)
                    dve.wait_ge(mm_read, num(u) + MB + 1)
                    dve.tensor_scalar(na[:, :], x2[:, m, :], g_mlp[:, bass.ds(m, 1)], None, ALU.mult
                                      ).then_inc(act_src, 1)
                    dve.wait_ge(act_src, 1 + MB + m)
                    dve.wait_ge(act_hi, 3 * KT + m + 1)
                    dve.tensor_tensor(a_lo[:, m, :], na[:, :], a_hi[:, m, :].bitcast(F32), ALU.subtract
                                      ).then_inc(a_ready, 1)
            dve.wait_ge(a_ready, 3 * KT)
            mean(N_NORM_X2, D_MODEL)
            newton(N_NORM_X2, rstd[:, :])

            def up(f, i, p):
                m = 2 * i + p
                u = (U_FF // 2 + MB * f + i, p)
                beside(u)
                dve.wait_ge(chunk_done, CH * num(u) + CH)
                dve.scalar_tensor_tensor(halves(z[:, p, :]), pair(p), 0.0, halves(rstd[:, :]), ALU.max, ALU.mult
                                         ).then_inc(mm_read, 1)
                dve.wait_ge(mm_read, num(u) + MB + 1)
                dve.tensor_tensor(na[:, :], z[:, p, :], z[:, p, :], ALU.mult).then_inc(act_src, 1)
                dve.wait_ge(act_src, 1 + 2 * MB + MB * f + m)
                dve.wait_ge(act_hi, 4 * KT + MB * f + m + 1)
                dve.tensor_tensor(b_lo[:, m, :], na[:, :], b_hi[:, m, :].bitcast(F32), ALU.subtract
                                  ).then_inc(b_ready, 1)

            def down(f, i, p):
                m = 2 * i + p
                u = (U_FF // 2 + MB // 2 + MB * f + i, p)
                if more(u):
                    beside(u)
                dve.wait_ge(chunk_done, CH * num(u) + CH)
                dve.tensor_tensor(halves(x2[:, m, :]), pair(p), halves(x2[:, m, :]), ALU.add).then_inc(mm_read, 1)

            ff_loops(dve, up, down)

        @block.gpsimd
        def _(pool):
            steps = Steps(pool, pool_step)

            pool.dma_start(gains[:, 0:44], t["gains"]).then_inc(consts_loaded, 16)
            pool.dma_start(oh[:, :], t["one_hot"]).then_inc(consts_loaded, 16)
            pool.dma_start(rb[0:NB, :], t["rel_bias"]).then_inc(consts_loaded, 16)
            pool.dma_start(w00, t["w_00"].to_broadcast([P, GRP])).then_inc(consts_loaded, 16)
            pool.dma_start(table[:, :], t["table"]).then_inc(table_loaded, 16)
            steps.did(pool.memset(rb[NB:NB + 1, :], NEG))
            steps.did(pool.memset(ident[:, :], 0.0))
            steps.did(pool.affine_select(out=ident[:, :], in_=ident[:, :], compare_op=ALU.not_equal, fill=1.0,
                                         base=0, pattern=[[-1, P]], channel_multiplier=1))
            pool.memset(ones[:, :], 1.0).then_inc(consts_set, 1)
            pool.wait_ge(consts_set, 1)
            steps.did(pool.memset(acc_v[:, :], 0.0))
            pool.memset(qm[:, :, :], 0.0).then_inc(consts_set, 1)

            pool.wait_ge(rel_done, 1)
            pool.dma_start(rel_d, rel_row[:, :]).then_inc(rel_stored, 16)
            pool.wait_ge(rel_stored, 16)
            pool.dma_start(toep_d, bass.AP(tensor=rel_d.tensor, offset=P - 1,
                                           ap=[[NREL, NH], [-1, P], [1, SEQ]])).then_inc(toep_stored, 16)

            def load_w_cmp(n):
                pool.dma_start(w_cmp[:, n % 2, :, :], t["w_cmp"][n]).then_inc(cmp_loaded[n % 2], 16)

            def load_pages(h, p):
                for k in range(NPG):
                    page = pool.value_load(table[0:1, bass.ds(NPG * h + k, 1)], min_val=0, max_val=N_POOL - 1)
                    pool.dma_start(pages[:, p, k, :], t["cache_cmp"][page]).then_inc(page_loaded[p], 16)

            load_w_cmp(0)
            load_w_cmp(1)
            pool.wait_ge(table_loaded, 16)
            load_pages(0, 0)
            load_pages(1, 1)
            pool.wait_ge(a_ready, KT)
            pool.wait_ge(summed, 1)
            for s in range(4):
                pool.dma_start(kv_t[:, s, L_ALL:KVT_W], t["pos"][s // NKV]).then_inc(pos_loaded, 16)
            for n in range(U_KV):
                pool.wait_ge(z_made, n + 1)
                pool.tensor_copy(kv_t[:, n, 0:SEQ], z[:, n % 2, 0:SEQ]).then_inc(z_copied, 1)
            with pool.Fori(1, DEC // 2) as i:
                for p in range(2):
                    pool.wait_ge(page_turned, 2 * (2 * i + p - 2) + 2)
                    load_pages(2 * i + p, p)
            pool.wait_ge(page_turned, NPG * DEC)
            pool.dma_start(wg_raw[:, :, :], t["w_gates"]).then_inc(wg_loaded, 16)
            for n in range(2, 2 * CMP_LEN // CJ):
                pool.wait_ge(cmp_used, n - 1)
                load_w_cmp(n)
            pool.wait_ge(gates_made, 1)
            pool.dma_start(gate_d, gates[P - DEC:P, NCH, :]).then_inc(gate_stored, 16)
            pool.wait_ge(gate_stored, 16)
            pool.dma_start(gs_row, gate_d.rearrange("b (h j) -> h b j", h=NH)).then_inc(gate_loaded, 16)
            pool.wait_ge(cmp_used, 2 * CMP_LEN // CJ)

            with steps.loop(0, DEC, 1) as b:
                pool.wait_ge(smp_out, b)
                for k in range(NPG):
                    page = pool.value_load(table[0:1, bass.ds(NPG * b + k, 1)], min_val=0, max_val=N_POOL - 1)
                    pool.dma_start(stage[:, k, :], t["cache_sel"][page]).then_inc(stage_loaded, 16)
                pool.dma_start(stage[:, 2:4, :], t["state"][b].rearrange("(c p) n -> p c n", c=2)
                               ).then_inc(stage_loaded, 16)
                pool.wait_ge(z_read, 2 * b + 1)
                pool.wait_ge(v_acc, b)
                steps.did(pool.tensor_tensor(sq[:, :], v_t[:, b, :], v_t[:, b, :], ALU.mult))
                pool.tensor_tensor(acc_v[:, :], acc_v[:, :], sq[:, :], ALU.add).then_inc(v_acc, 1)

            pool.wait_ge(smp_read, DEC)
            pool.dma_start(wm[:, :, :], t["w_mix"]).then_inc(gm_loaded, 16)
            pool.dma_start(b_bc[:, :, :].rearrange("p g t -> p (g t)"), t["b_mix"].to_broadcast([P, GRP * P])
                           ).then_inc(gm_loaded, 16)
            pool.wait_ge(gm_loaded, 32)
            pool.affine_select(out=wm[:, :, :], in_=wm[:, :, :], compare_op=ALU.is_ge, fill=0.0, base=0,
                               pattern=[[0, GRP], [1, P]], channel_multiplier=-1).then_inc(w_masked, 1)

            with steps.loop(0, MB, 2) as m:
                for p in range(2):
                    pool.wait_ge(g_tanh, 2 * m + p + 1)
                    carry(nc.gpsimd)
                    steps.did(pool.tensor_scalar(z[:, p, :], z[:, p, :], 0.5, 0.5, ALU.mult, ALU.add))
                    pool.dma_start(merge_d[2 * m + p], z[:, p, :]).then_inc(g_stored[p], 16)

            pool.wait_ge(b7_read, 6 * NH)
            for p in range(2):
                pool.wait_ge(g_stored[p], 16 * MB)
            with pool.Fori(0, MB // 2) as i:
                for p in range(2):
                    pool.wait_ge(mm_read, U_PROJ + 2 * (2 * i + p) - 2)
                    pool.dma_start(g_in[:, p, :, :], merge_d.rearrange("(m t) p n -> m p t n", t=2)[2 * i + p]
                                   ).then_inc(g_loaded[p], 16)
            steps.did(pool.memset(acc_x[:, :], 0.0))
            with steps.loop(0, MB // 2, 2) as i:
                for p in range(2):
                    m = 2 * i + p
                    pool.wait_ge(mm_read, U_OUT + MB - 1 + m)
                    pool.dma_start(z[:, p, :], t["x_t"][m]).then_inc(x_in_loaded[p], 16)
                    pool.wait_ge(act_src, MB + m + 1)
                    pool.wait_ge(x2_squared, m)
                    steps.did(pool.tensor_tensor(nr[:, :], x2[:, m, :], x2[:, m, :], ALU.mult))
                    pool.tensor_tensor(acc_x[:, :], acc_x[:, :], nr[:, :], ALU.add).then_inc(x2_squared, 1)


_INS = ["x_t", "w", "gains", "one_hot", "rel_bias", "w_00", "table", "w_cmp", "pos", "cache_cmp", "cache_sel",
        "state", "w_gates", "w_mix", "b_mix"]
_OUTS = [("y_t", (MB, P, TOK)), ("kv_t", (U_Q, P, TOK)), ("v_t", (P, GRP, P + DEC)), ("win", (DEC, PAST, 512))]


def _layout(a):
    w_in = a["w_in"][0]
    x = np.concatenate([a["x_prompt"][0], a["x_sample"][:, 0]], 0)
    kvw = 2 * NKV * HD

    def blocks(w, rows=KT):
        n = w.shape[1] // P
        return w.reshape(rows, P, n, P).transpose(2, 1, 0, 3).reshape(n, P, rows * P)

    o = 2 * D_GM
    uv, q = blocks(w_in[:, :o]), blocks(w_in[:, o:o + NH * HD])
    o += NH * HD
    kv = [blocks(w_in[:, o + n * kvw:o + (n + 1) * kvw]) for n in range(3)]
    o += 3 * kvw
    w_gates = w_in[:, o:o + N_GATE].reshape(KT, P, N_GATE).transpose(1, 0, 2)
    o += N_GATE
    ga, gb = blocks(w_in[:, o:o + D_MODEL]), blocks(w_in[:, o + D_MODEL:])
    pairs = lambda f, s: np.stack([f, s], 1).reshape(-1, P, KT * P)
    up, down = a["w_up"][0], a["w_down"][0]
    parts = [kv[0], kv[1][[0, 2, 1, 3]], kv[2][[0, 2, 1, 3]], q, pairs(uv[GRP:], uv[:GRP]), pairs(ga, gb),
             np.concatenate([blocks(a["w_proj_gmlp"][0], GRP), blocks(a["w_proj_nsa"][0], NH)], 2),
             blocks(a["w_out"][0])]
    for f in range(FG):
        cut = slice(f * D_MODEL, (f + 1) * D_MODEL)
        parts += [blocks(up[:, cut]), blocks(down[cut])]
    cols = lambda g: g.reshape(-1, P).T
    rel = SEQ - 1 - np.arange(NREL)
    far = np.maximum(rel, 1).astype(np.float32)
    bucket = NB // 2 + (np.log(far / (NB // 2)) / np.log(128 / (NB // 2)) * (NB // 2)).astype(np.int32)
    bucket = np.where(rel < NB // 2, rel, np.minimum(bucket, NB - 1))
    bucket = np.where(rel < 0, NB, bucket)
    one_hot = (np.arange(NB + 1)[:, None] == bucket[None]).astype(np.float32)
    w_sgu = a["w_sgu"][0]
    w_cmp = np.stack([a["w_cmp_k"][0], a["w_cmp_v"][0]]).reshape(2 * CMP_LEN // CJ, CJ, HD, HD)
    return {
        "x_t": x.T.reshape(KT, P, TOK),
        "w": np.concatenate(parts),
        "gains": np.concatenate([cols(a["g_mix_norm"][0]), cols(a["g_mlp_norm"][0]), cols(a["g_sgu"][0]),
                                 cols(a["g_q"][0]), cols(a["g_k"][0])], 1),
        "one_hot": one_hot,
        "rel_bias": a["rel_bias"],
        "w_00": w_sgu[None, :, 0, 0],
        "table": a["page_table"].reshape(1, DEC * NPG),
        "w_cmp": w_cmp.transpose(0, 2, 1, 3),
        "pos": np.stack([a["pos_cmp_k"][0].T, a["pos_cmp_v"][0].T]),
        "cache_cmp": a["cache_cmp_kv"].reshape(N_POOL, PAGE, kvw),
        "cache_sel": a["cache_sel_kv"].reshape(N_POOL, PAGE, kvw),
        "state": a["state_win_kv"].reshape(DEC, PAST, kvw),
        "w_gates": w_gates,
        "w_mix": w_sgu.transpose(2, 0, 1),
        "b_mix": a["b_sgu"].reshape(1, GRP * P),
    }


def kernel(**inputs):
    import concourse.bacc as bacc
    from concourse.bass_utils import run_bass_kernel_spmd

    nc = bacc.Bacc("TRN2", target_bir_lowering=False, num_devices=1, dynamic_dma_scratch_size=8192)
    arrays = {n: np.ascontiguousarray(x) for n, x in _layout({k: np.asarray(v) for k, v in inputs.items()}).items()}
    t = {n: nc.dram_tensor(f"in_{n}", arrays[n].shape, mybir.dt.from_np(arrays[n].dtype), kind="ExternalInput").ap()
         for n in _INS}
    t |= {n: nc.dram_tensor(f"out_{n}", shape, F32, kind="ExternalOutput").ap() for n, shape in _OUTS}
    build(nc, t)
    r = run_bass_kernel_spmd(nc, [{f"in_{n}": arrays[n] for n in _INS}], core_ids=[0]).results[0]
    y = r["out_y_t"].reshape(D_MODEL, TOK).T
    kv = r["out_kv_t"].transpose(2, 0, 1)
    order = {"cmp": [0, 1, 2, 3], "sel": [4, 6, 5, 7], "win": [8, 10, 9, 11]}
    kv = {n: kv[:, o].reshape(TOK, 2, NKV, HD) for n, o in order.items()}
    v = r["out_v_t"].transpose(2, 1, 0).reshape(P + DEC, D_GM)
    prompt = lambda n: np.ascontiguousarray(kv[n][None, None, :SEQ])
    sample = lambda n: np.ascontiguousarray(kv[n][None, SEQ:, None])
    win = np.concatenate([r["out_win"].reshape(1, DEC, PAST, 2, NKV, HD), sample("win")], 2)
    return (np.ascontiguousarray(y[None, :SEQ]), np.ascontiguousarray(y[SEQ:, None]),
            prompt("cmp"), prompt("sel"), prompt("win"), np.ascontiguousarray(v[None, None, :P]),
            sample("cmp"), sample("sel"), win, np.ascontiguousarray(v[None, P:, None]))
```

```python
from contextlib import ExitStack, contextmanager

import numpy as np

import concourse.bass as bass
from concourse import mybir

F32 = mybir.dt.float32
F32R = mybir.dt.float32r
I32 = mybir.dt.int32
ALU = mybir.AluOpType
ACT = mybir.ActivationFunctionType

P = 128
D_MODEL, SEQ, DEC, PAST, PAGE = 2048, 512, 8, 256, 128
HD, NH, NKV, REP = 128, 8, 2, 4
D_GM, GRP, D_FF = 1024, 8, 8192
CMP_LEN, STRIDE = 32, 16
N_POOL = 20
EPS = 1e-6
NEG = -1e30
NB = 32

TOK = SEQ + DEC
HT = TOK // 2
KT = D_MODEL // P
CH = 4
CK = KT // CH
CW = CK * P
MB = D_MODEL // P
NCH = SEQ // P
NPG = PAST // PAGE

U_CMP, U_KV, U_Q, U_VU, U_GATE = 0, 4, 12, 20, 36
U_PROJ = U_GATE + 2 * MB
U_OUT = U_PROJ + MB
U_FF = U_OUT + MB
FG = D_FF // D_MODEL
UNITS = U_FF + 2 * MB * FG

L_ALL = SEQ + DEC * PAST
W_ALL = L_ALL // STRIDE
KVT_W = L_ALL + CMP_LEN
W_PROMPT = (SEQ - CMP_LEN) // STRIDE + 1
W_SAMPLE = (PAST - CMP_LEN) // STRIDE + 1
W_USED = W_ALL
CJ = 8
NREL = 640
N_GATE = 3 * NH


def seen(i):
    return (P * (i + 1) - CMP_LEN) // STRIDE + 1


class Steps:

    def __init__(self, eng, sem):
        self.eng, self.sem, self.n, self.local = eng, sem, 0, 0

    def did(self, ins):
        ins.then_inc(self.sem, 1)
        self.local += 1
        self.n = self.n + 1
        self.eng.wait_ge(self.sem, self.n)

    @contextmanager
    def loop(self, first, last, per):
        with self.eng.Fori(first, last) as i:
            before, start = self.local, self.n
            self.n = start + (i - first) * per
            yield i
            assert self.local - before == per, (self.local - before, per)
        self.local = before + per * (last - first)
        self.n = start + per * (last - first)


def build(nc, t):
    with ExitStack() as ctx:
        def sem(name):
            return ctx.enter_context(nc.semaphore(name))

        def dram(name, shape):
            return nc.dram_tensor(name, shape, F32).ap()

        base = nc.sbuf_base + (-nc.sbuf_base) % 64
        top = [base]

        def at(name, shape, offset, dt=F32):
            assert offset % 32 == 0, name
            size = 4 * int(np.prod(shape[1:]))
            assert offset + size <= nc.sbuf_usable_end, (name, offset + size - nc.sbuf_usable_end)
            return nc.alloc_sbuf_tensor_at(name, shape, dt, offset=offset)

        def new(name, shape, dt=F32):
            o = top[0]
            size = 4 * int(np.prod(shape[1:]))
            top[0] = o + size + (-size) % 32
            return at(name, shape, o, dt)

        w_raw = new("w_raw", [P, 4, 2 * CW])
        w_hi = new("w_hi", [P, CH, CW], F32R)
        w_lo = new("w_lo", [P, CH, CW], F32R)
        a_hi = new("a_hi", [P, KT, TOK], F32R)
        a_lo = new("a_lo", [P, KT, TOK], F32R)
        ones = new("ones", [P, P])
        ident = new("ident", [P, P])
        gains = new("gains", [P, 48])
        z = new("z", [P, 2, TOK])
        na = new("na", [P, TOK])
        nr = new("nr", [P, TOK])
        nq = new("nq", [P, TOK])
        rstd = new("rstd", [P, TOK])
        small = new("small", [P, 192])

        g_mix = gains[:, 0:16]
        g_mlp = gains[:, 16:32]
        g_sgu = gains[:, 32:40]
        g_q = gains[:, 40:41]
        g_k = gains[:, 41:44]
        g_qs = gains[:, 44:45]
        mx = small[:, 0:3]
        mn = small[:, 4:7]
        ls = small[:, 8:11]
        rl = small[:, 12:15]
        k_ss = small[:, 16:24]
        k_a = small[:, 24:32]
        k_r = small[:, 32:40]
        k_q = small[:, 40:48]
        k_rs = small[:, 48:56]
        tok_rstd = small[:, 56:64]
        w00 = small[:, 64:72]
        v_new = small[:, 80:112].rearrange("p (s b) -> p s b", s=4)
        gs_row = small[0:NH, 112:136].rearrange("p (b j) -> p b j", b=DEC)
        vs_tmp = small[:, 136:144]
        qm = small[:, 144:160].rearrange("p (g h) -> p g h", g=NKV)
        v_new_b = small[:, 160:164]

        zone = top[0]
        q_t = new("q_t", [P, NH, TOK])
        k_t = new("k_t", [P, 4, TOK])
        v_row = new("v_row", [P, 4, NCH, HD])
        kc_t = new("kc_t", [P, NKV, W_USED])
        vc_t = new("vc_t", [P, NKV, W_USED])
        vc_p = new("vc_p", [32, NKV, HD])
        gates = new("gates", [P, NCH + 1, N_GATE])
        r1 = top[0]
        kv_t = new("kv_t", [P, 4, KVT_W])
        r1_end = top[0]
        x_raw = at("x_raw", [P, KT, TOK], r1)
        u_t = at("u_t", [P, GRP, TOK], r1)
        v_t = at("v_t", [P, GRP, TOK], r1 + 4 * GRP * TOK)
        r1b = r1 + 8 * GRP * TOK
        ks_t = at("ks_t", [P, NKV, PAST + 4], r1b)
        kw_t = at("kw_t", [P, NKV, PAST + 4], r1b + 2080)
        sp = at("sp", [NH, 3, PAST + 4], r1b + 4160)
        p_s = at("p_s", [P, SEQ], r1b)
        p_w = at("p_w", [P, SEQ], r1b + 2048)
        p_c = at("p_c", [P, 32], r1b + 4096)
        assert r1b + 8192 <= r1_end
        r2 = top[0]
        w_cmp = new("w_cmp", [P, 2, CJ, HD])
        pages = new("pages", [P, 2, NPG, 512])
        r2_end = top[0]
        stage = at("stage", [P, 4, 512], r2 + 8192)
        v_new_r = at("v_new_r", [1, 4, HD], r2)
        vc_s = at("vc_s", [16, NKV, HD], r2 + 2048)
        pt_s = at("pt_s", [P, 64], r2 + 3072)
        wm = at("wm", [P, GRP, P], r2)
        b_bc = at("b_bc", [P, GRP, P], r2 + 4096)
        pt_sel = at("pt_sel", [P, NCH, P], r2 + 8192)
        pt_win = at("pt_win", [P, NCH, P], r2 + 10240)
        pt_cmp = at("pt_cmp", [32, P], r2 + 12288)
        r3 = top[0]
        sq = new("sq", [P, TOK])
        acc_v = new("acc_v", [P, TOK])
        wg_hi = at("wg_hi", [P, KT, N_GATE], r2 + 8192, F32R)
        wg_lo = at("wg_lo", [P, KT, N_GATE], r2 + 8192 + 1536, F32R)
        wg_raw = at("wg_raw", [P, KT, N_GATE], r2 + 8192 + 3072)
        gz = at("gz", [P, NCH + 1, N_GATE], r2 + 8192 + 4608)
        v_g = at("v_g", [P, TOK], r3)
        vr_g = new("vr_g", [P, NCH, P])
        toep = new("toep", [P, SEQ])
        q_h = new("q_h", [P, SEQ])
        oh = at("oh", [NB + 1, NREL], r2)
        rb = at("rb", [NB + 1, NH], r2 + 4 * NREL)
        rel_row = at("rel_row", [NH, NREL], r2 + 4 * NREL + 64)
        vc_b = new("vc_b", [P, NKV, W_SAMPLE + 1])
        rel_s = new("rel_s", [NH, PAST + 4])
        table = new("table", [1, DEC * NPG], I32)
        b_hi = at("b_hi", [P, KT, TOK], zone, F32R)
        b_lo = at("b_lo", [P, KT, TOK], zone + 4 * KT * TOK, F32R)
        r4 = zone + 8 * KT * TOK
        x2 = at("x2", [P, MB, TOK], r4)
        acc_x = at("acc_x", [P, TOK], r4 + 4 * MB * TOK)
        g_in = at("g_in", [P, 2, 2, TOK], r4)

        ca, cb, cm = na, nr, nq

        mm = nc.alloc_psum_tensor("mm", [P, 4, 512], F32)
        aux = nc.alloc_psum_tensor("aux", [P, 4, 512], F32)


        rel_d = dram("rel_d", [NH, NREL])
        toep_d = dram("toep_d", [NH, P, SEQ])
        gate_d = dram("gate_d", [DEC, N_GATE])
        merge_d = dram("merge_d", [2 * MB, P, TOK])

        raw_loaded = [sem(f"raw_loaded{n}") for n in range(4)]
        hi_split = sem("hi_split")
        lo_split = sem("lo_split")
        chunk_done = sem("chunk_done")
        mm_read = sem("mm_read")
        a_ready = sem("a_ready")
        b_ready = sem("b_ready")
        act_hi = sem("act_hi")
        act_src = sem("act_src")
        x_loaded = [sem(f"x_loaded{n}") for n in range(CH)]
        gains_loaded = sem("gains_loaded")
        consts_loaded = sem("consts_loaded")
        consts_set = sem("consts_set")
        x_squared = sem("x_squared")
        x_added = sem("x_added")
        squared = sem("squared")
        summed = sem("summed")
        norm_base = sem("norm_base")
        norm_guess = sem("norm_guess")
        z_made = mm_read
        z_read = sem("z_read")
        z_stored = [sem(f"z_stored{n}") for n in range(2)]
        z_copied = sem("z_copied")
        pos_loaded = sem("pos_loaded")
        v_turned = sem("v_turned")
        v_row_made = sem("v_row_made")
        rel_made, rel_done = sem("rel_made"), sem("rel_done")
        rel_stored, toep_stored = sem("rel_stored"), sem("toep_stored")
        toep_loaded = sem("toep_loaded")
        table_loaded = sem("table_loaded")
        page_loaded = [sem(f"page_loaded{n}") for n in range(2)]
        page_turned = sem("page_turned")
        page_read = sem("page_read")
        cmp_loaded = [sem(f"cmp_loaded{n}") for n in range(2)]
        cmp_used = sem("cmp_used")
        kc_made, vc_made = sem("kc_made"), sem("vc_made")
        vcp_turned, vcp_made = sem("vcp_turned"), sem("vcp_made")
        wg_loaded, wg_hi_made, wg_split = sem("wg_loaded"), sem("wg_hi_made"), sem("wg_split")
        gates_summed, gz_made, gz_tanh, gates_made = (sem("gates_summed"), sem("gz_made"),
                                                      sem("gz_tanh"), sem("gates_made"))
        gate_stored, gate_loaded = sem("gate_stored"), sem("gate_loaded")
        keys_loaded, values_loaded = sem("keys_loaded"), sem("values_loaded")
        smp_base, smp_guess, smp_keys = sem("smp_base"), sem("smp_guess"), sem("smp_keys")
        smp_vturned, smp_vmade = sem("smp_vturned"), sem("smp_vmade")
        smp_kturned, smp_ks, smp_kw = sem("smp_kturned"), sem("smp_ks"), sem("smp_kw")
        smp_scored, smp_max, smp_exp = sem("smp_scored"), sem("smp_max"), sem("smp_exp")
        smp_probs, smp_pturned, smp_pmade = sem("smp_probs"), sem("smp_pturned"), sem("smp_pmade")
        smp_out, smp_read = sem("smp_out"), sem("smp_read")
        smp_static = sem("smp_static")
        v_acc = sem("v_acc")
        gm_loaded, w_masked, v_normed = sem("gm_loaded"), sem("w_masked"), sem("v_normed")
        v_stored, win_stored = sem("v_stored"), sem("win_stored")
        q_copied, v_copied = sem("q_copied"), sem("v_copied")
        scored, s_max, s_exp, probs = sem("scored"), sem("s_max"), sem("s_exp"), sem("probs")
        p_turned, pt_sel_made, pt_made = sem("p_turned"), sem("pt_sel_made"), sem("pt_made")
        b7_made, b7_read = sem("b7_made"), sem("b7_read")
        g_tanh = sem("g_tanh")
        g_stored = [sem(f"g_stored{n}") for n in range(2)]
        g_loaded = [sem(f"g_loaded{n}") for n in range(2)]
        x_in_loaded = [sem(f"x_in_loaded{n}") for n in range(2)]
        x2_made, x2_squared = sem("x2_made"), sem("x2_squared")
        y_stored = sem("y_stored")
        dve_step, act_step, pool_step = sem("dve_step"), sem("act_step"), sem("pool_step")

        def carry(eng):
            if eng is nc.vector:
                eng.memset(small[:, 170:171], 0.0)
            else:
                eng.tensor_tensor(small[:, 171:172], ones[:, 0:1], ones[:, 0:1], ALU.mult)

        def num(u):
            return 2 * u[0] + u[1]

        def after(u):
            return (u[0], 1) if u[1] == 0 else (u[0] + 1, 0)

        def straight(n):
            return (n // 2, n % 2)

        def raw(u, c):
            return w_raw[:, 2 * u[1] + c // 2, (c % 2) * CW:(c % 2 + 1) * CW]

        def pair(v):
            return mm[:, 2 * v:2 * v + 2, 0:HT]

        def halves(ap):
            return ap.rearrange("p (a b) -> p a b", a=2)

        def mm_use(u):
            return num(u)

        def more(u):
            return not (type(u[0]) is int and num(u) == UNITS - 1)

        def ff_loops(eng, up, down):
            def group(f, pairs):
                with eng.Fori(0, MB // 2) as i:
                    for p in range(2):
                        up(f, i, p)
                with eng.Fori(0, pairs) as i:
                    for p in range(2):
                        down(f, i, p)

            with eng.Fori(0, FG - 1) as f:
                group(f, MB // 2)
            group(FG - 1, MB // 2 - 1)
            for p in range(2):
                down(FG - 1, MB // 2 - 1, p)

        GATE_OF = (1, 2, 0)
        CONSTS = 16 * 3
        N_NORM_K, N_NORM_C, N_NORM_V, N_NORM_X2 = 1, 9, 14, 15

        def n_norm_q(h):
            return 5 + h + (1 if h >= NH // 2 else 0)


        block = ctx.enter_context(nc.Block())

        @block.sync
        def _(sp_):
            for c in range(CH):
                sp_.dma_start(x_raw[:, CK * c:CK * (c + 1), :],
                              t["x_t"][CK * c:CK * (c + 1)].rearrange("k p n -> p k n")
                              ).then_inc(x_loaded[c], 16)
                sp_.dma_start(w_raw[:, c, :], t["w"][c // 2, :, (c % 2) * 2 * CW:(c % 2 + 1) * 2 * CW]
                              ).then_inc(raw_loaded[c], 16)
            with sp_.Fori(1, UNITS // 2) as i:
                for n in range(4):
                    sp_.wait_ge(lo_split, 8 * i - 8 + 2 * n + 2)
                    sp_.dma_start(w_raw[:, n, :], t["w"][2 * i + n // 2, :, (n % 2) * 2 * CW:(n % 2 + 1) * 2 * CW]
                                  ).then_inc(raw_loaded[n], 16)
            with sp_.Fori(0, MB) as m:
                sp_.wait_ge(mm_read, UNITS + m + 1)
                sp_.dma_start(t["y_t"][m], x2[:, m, :]).then_inc(y_stored, 16)
            sp_.wait_ge(y_stored, 16 * MB)

        @block.tensor
        def _(pe):
            def unit(u, ah, al, ready, need, hooks=(), before=None, projections=False,
                     first_hook=None):
                n = num(u)
                if first_hook:
                    first_hook()
                for c in range(CH):
                    pe.wait_ge(lo_split, 4 * n + c + 1)
                    pe.wait_ge(ready, need(c))
                    if projections:
                        v = c // 2
                        if c % 2 == 0:
                            pe.wait_ge(mm_read, 2 * n - U_PROJ - 1 + v)
                    else:
                        v = u[1]
                        if c == 0 and not (type(n) is int and n < 2):
                            pe.wait_ge(mm_read, before(u) if before else mm_use(u) - 1)
                    first = c % 2 == 0 if projections else c == 0
                    final = c % 2 == 1 if projections else c == CH - 1
                    for k in range(CK):
                        kt = CK * c + k
                        wh, wl = w_hi[:, c, k * P:(k + 1) * P], w_lo[:, c, k * P:(k + 1) * P]
                        for w, a, part in ((wh, ah, 0), (wh, al, 1), (wl, ah, 2)):
                            for h in range(2):
                                last = pe.matmul(mm[:, 2 * v + h, 0:HT], w, a[:, kt, h * HT:(h + 1) * HT],
                                                 start=first and k == 0 and part == 0,
                                                 stop=final and k == CK - 1 and part == 2)
                    last.then_inc(chunk_done, 1)
                    if c < len(hooks) and hooks[c]:
                        hooks[c]()

            def norm_sum(n, src=None, made=None):
                src = sq if src is None else src
                pe.wait_ge(*(made or (squared, n)))
                pe.wait_ge(norm_base, n)
                for h in range(2):
                    last = pe.matmul(aux[:, h, 0:HT], ones[:, :], src[:, h * HT:(h + 1) * HT],
                                     start=True, stop=True)
                last.then_inc(summed, 1)

            def turn_v(j):
                def go():
                    pe.wait_ge(z_made, U_KV + 2 * j + 2)
                    pe.wait_ge(v_row_made, j)
                    pe.wait_ge(page_read, 4 * j + 4)
                    for k in range(NCH):
                        last = pe.transpose(aux[:, 2, k * P:(k + 1) * P], z[:, 1, k * P:(k + 1) * P], ident[:, :])
                    last.then_inc(v_turned, 1)
                return go

            def turn_pages(b):
                def go():
                    p = b % 2
                    pe.wait_ge(page_loaded[p], 16 * NPG * (b // 2 + 1))
                    pe.wait_ge(v_row_made, b // 2)
                    pe.wait_ge(page_read, NPG * b)
                    for g in range(NPG):
                        for q in range(4):
                            last = pe.transpose(aux[:, 2 + g, q * P:(q + 1) * P],
                                                pages[:, p, g, q * P:(q + 1) * P], ident[:, :])
                        last.then_inc(page_turned, 1)
                return go

            x_need = lambda c: CK * (c + 1)

            def rel_row_sums():
                pe.wait_ge(consts_loaded, CONSTS)
                pe.matmul(aux[0:NH, 2, 0:512], rb[:, :], oh[:, 0:512], start=True, stop=True)
                pe.matmul(aux[0:NH, 3, 0:NREL - 512], rb[:, :], oh[:, 512:NREL], start=True, stop=True
                          ).then_inc(rel_made, 1)

            def x_sum():
                pe.wait_ge(consts_set, 1)
                pe.wait_ge(x_added, KT)
                for h in range(2):
                    last = pe.matmul(aux[:, h, 0:HT], ones[:, :], acc_v[:, h * HT:(h + 1) * HT],
                                     start=True, stop=True)
                last.then_inc(summed, 1)

            unit(straight(0), a_hi, a_lo, a_ready, x_need, [None, None, None, x_sum])
            unit(straight(1), a_hi, a_lo, a_ready, x_need, [None, rel_row_sums])
            for n in range(2, U_KV):
                unit(straight(n), a_hi, a_lo, a_ready, x_need)
            pe.wait_ge(rel_done, 1)
            for j in range(4):
                unit(straight(U_KV + 2 * j), a_hi, a_lo, a_ready, x_need,
                     [None, turn_v(j - 1) if j else None, turn_pages(2 * j)])
                unit(straight(U_KV + 2 * j + 1), a_hi, a_lo, a_ready, x_need,
                     [None, lambda: norm_sum(N_NORM_K + j), turn_pages(2 * j + 1)])

            def compress(n):
                def go():
                    kv, part = divmod(n, CMP_LEN // CJ)
                    if n == 0:
                        pe.wait_ge(page_read, NPG * DEC)
                        pe.wait_ge(z_copied, U_KV)
                        pe.wait_ge(pos_loaded, 64)
                        pe.wait_ge(v_row_made, 4)
                    if part == 0 and kv == 1:
                        pe.wait_ge(gz_made, 1)
                    pe.wait_ge(cmp_loaded[n % 2], 16 * (n // 2 + 1))
                    for jj in range(CJ):
                        j = part * CJ + jj
                        last = pe.matmul(aux[:, 2 + kv, 0:NKV * (W_ALL + 1)], w_cmp[:, n % 2, jj, :],
                                         kv_t[:, NKV * kv:NKV * (kv + 1), j:j + STRIDE * W_ALL + 1:STRIDE],
                                         start=j == 0, stop=j == CMP_LEN - 1)
                    last.then_inc(cmp_used, 1)
                return go

            def gate_sums():
                pe.wait_ge(wg_split, 1)
                pe.wait_ge(page_read, NPG * DEC)
                for tb in range(NCH + 1):
                    o = min(P * tb, TOK - P)
                    for kt in range(KT):
                        for a, w, part in ((a_hi, wg_hi, 0), (a_hi, wg_lo, 1), (a_lo, wg_hi, 2)):
                            pe.matmul(aux[:, 3, N_GATE * tb:N_GATE * (tb + 1)], a[:, kt, o:o + P], w[:, kt, :],
                                      start=kt == 0 and part == 0, stop=kt == KT - 1 and part == 2)
                for tb in range(NCH + 1):
                    o = min(P * tb, TOK - P)
                    last = pe.transpose(aux[:, 3, 256 + tb:257 + tb], rstd[0:1, o:o + P], ident[0:1, 0:1])
                last.then_inc(gates_summed, 1)

            def key_windows_sum():
                pe.wait_ge(squared, N_NORM_C)
                pe.wait_ge(norm_base, N_NORM_C)
                pe.matmul(aux[:, 0, 0:NKV * W_USED], ones[:, :], sq[:, 0:NKV * W_USED], start=True, stop=True
                          ).then_inc(summed, 1)

            def turn_windows():
                pe.wait_ge(vc_made, 1)
                for g in range(NKV):
                    last = pe.transpose(aux[0:W_PROMPT, 2, g * P:(g + 1) * P], vc_t[:, g, 0:W_PROMPT], ident[:, :])
                last.then_inc(vcp_turned, 1)

            for h in range(NH):
                unit(straight(U_Q + h), a_hi, a_lo, a_ready, x_need,
                     [None, turn_v(3) if h == 0 else (lambda: norm_sum(n_norm_q(h - 1))),
                      gate_sums if h == 1 else None,
                      (lambda: (key_windows_sum(), compress(h)())) if h == NH // 2 else compress(h)])

            def smp_values(b):
                def go():
                    pe.wait_ge(smp_max, b)
                    pe.wait_ge(vcp_made, 1)
                    pe.wait_ge(smp_static, b + 1)
                    for s in range(4):
                        pe.transpose(aux[0:1, 2, s * P:(s + 1) * P], v_new_b[:, s:s + 1], ident[:, :])
                    for g in range(NKV):
                        last = pe.transpose(aux[0:W_SAMPLE, 3, g * P:(g + 1) * P], vc_b[:, g, 0:W_SAMPLE],
                                            ident[:, :])
                    last.then_inc(smp_vturned, 1)
                return go

            def smp_turn_keys(b):
                def go():
                    pe.wait_ge(smp_keys, b + 1)
                    pe.wait_ge(smp_pmade, b)
                    pe.wait_ge(smp_read, b)
                    for br in range(2):
                        for g in range(NKV):
                            for k in range(NPG):
                                last = pe.transpose(aux[:, br, (2 * g + k) * P:(2 * g + k + 1) * P],
                                                    stage[:, 2 * br + k, g * P:(g + 1) * P], ident[:, :])
                        last.then_inc(smp_kturned, 1)
                return go

            def smp_scores(b):
                def go():
                    pe.wait_ge(smp_ks, b + 1)
                    pe.wait_ge(smp_kw, b + 1)
                    pe.wait_ge(smp_vmade, b + 1)
                    for g in range(NKV):
                        pe.matmul(aux[0:NH, 2, 0:PAST + 1], qm[:, g, :], ks_t[:, g, 0:PAST + 1],
                                  start=g == 0, stop=g == NKV - 1)
                    for g in range(NKV):
                        pe.matmul(aux[0:NH, 2, 300:300 + W_SAMPLE], qm[:, g, :],
                                  kc_t[:, g, bass.ds(SEQ // STRIDE + b * (PAST // STRIDE), W_SAMPLE)],
                                  start=g == 0, stop=g == NKV - 1)
                    for g in range(NKV):
                        last = pe.matmul(aux[0:NH, 3, 0:PAST + 1], qm[:, g, :], kw_t[:, g, 0:PAST + 1],
                                         start=g == 0, stop=g == NKV - 1)
                    last.then_inc(smp_scored, 1)
                return go

            def smp_turn_probs(b):
                def go():
                    pe.wait_ge(smp_probs, b + 1)
                    i8 = ident[0:NH, 0:NH]
                    for br in range(2):
                        for k in range(NPG):
                            pe.matmul(aux[:, 0, (2 * br + k) * NH:(2 * br + k + 1) * NH],
                                      sp[:, br, k * P:(k + 1) * P], i8, start=True, stop=True)
                        pe.transpose(aux[0:1, 0, (4 + br) * NH:(5 + br) * NH], sp[:, br, PAST:PAST + 1], i8)
                    pe.transpose(aux[0:W_SAMPLE, 0, 6 * NH:7 * NH], sp[:, 2, 0:W_SAMPLE], i8
                                 ).then_inc(smp_pturned, 1)
                return go

            def smp_attend(b):
                def go():
                    pe.wait_ge(smp_pmade, b + 1)
                    pe.wait_ge(values_loaded, 48 * b + 48)
                    for g in range(NKV):
                        o = aux[:, 1, REP * g:REP * (g + 1)]
                        cut = lambda n, rows: pt_s[0:rows, n * NH + REP * g:n * NH + REP * (g + 1)]
                        vg = slice((NKV + g) * HD, (NKV + g + 1) * HD)
                        for n in range(4):
                            pe.matmul(o, stage[:, n, vg], cut(n, P), start=n == 0, stop=False)
                        for br in range(2):
                            pe.matmul(o, v_new_r[0:1, 2 * br + g, :], cut(4 + br, 1), start=False, stop=False)
                        last = pe.matmul(o, vc_s[0:W_SAMPLE, g, :], cut(6, W_SAMPLE), start=False, stop=True)
                    last.then_inc(smp_out, 1)
                return go

            unit((U_VU // 2, 0), a_hi, a_lo, a_ready, x_need,
                 [lambda: norm_sum(n_norm_q(NH - 1)), turn_windows, smp_values(0), smp_turn_keys(0)])
            unit((U_VU // 2, 1), a_hi, a_lo, a_ready, x_need, [None, smp_turn_probs(0), smp_attend(0)],
                 first_hook=smp_scores(0))
            with pe.Fori(1, DEC) as b:
                unit((U_VU // 2 + b, 0), a_hi, a_lo, a_ready, x_need,
                     [None, smp_values(b), smp_turn_keys(b)])
                unit((U_VU // 2 + b, 1), a_hi, a_lo, a_ready, x_need, [None, smp_turn_probs(b), smp_attend(b)],
                     first_hook=smp_scores(b))
            pe.wait_ge(smp_read, DEC)
            norm_sum(N_NORM_V, acc_v, (v_acc, GRP))
            pe.wait_ge(norm_base, N_NORM_V + 1)

            def scores(g, h, i):
                def go():
                    a = NCH * h + i
                    pe.wait_ge(q_copied, h + 1)
                    pe.wait_ge(pt_sel_made, a)
                    pe.wait_ge(pt_made, a)
                    qi = q_h[:, P * i:P * (i + 1)]
                    pe.matmul(aux[:, 0, 0:P * (i + 1)], qi, k_t[:, g, 0:P * (i + 1)], start=True, stop=True)
                    pe.matmul(aux[:, 1, 0:P * (i + 1)], qi, k_t[:, 2 + g, 0:P * (i + 1)], start=True, stop=True)
                    pe.matmul(aux[:, 2, 0:seen(i)], qi, kc_t[:, g, 0:seen(i)], start=True, stop=True
                              ).then_inc(scored, 1)
                return go

            def turn_probs(g, h, i):
                def go():
                    pe.wait_ge(probs, NCH * h + i + 1)
                    for n, src in enumerate((p_s, p_w)):
                        for k in range(i + 1):
                            pe.transpose(aux[:, n, k * P:(k + 1) * P], src[:, k * P:(k + 1) * P], ident[:, :])
                    pe.transpose(aux[0:seen(i), 2, 0:P], p_c[:, 0:seen(i)], ident[:, :]).then_inc(p_turned, 1)
                return go

            def attend(g, h, i):
                def go():
                    pe.wait_ge(pt_sel_made, NCH * h + i + 1)
                    pe.wait_ge(pt_made, NCH * h + i + 1)
                    pe.wait_ge(b7_read, 6 * h + (0, 1, 3, 5)[i])
                    o = aux[:, 3, 0:P]
                    for k in range(i + 1):
                        pe.matmul(o, v_row[:, g, k, :], pt_sel[:, k, :], start=k == 0, stop=False)
                    for k in range(i + 1):
                        pe.matmul(o, v_row[:, 2 + g, k, :], pt_win[:, k, :], start=False, stop=False)
                    pe.matmul(o, vc_p[0:seen(i), g, :], pt_cmp[0:seen(i), :], start=False, stop=True
                              ).then_inc(b7_made, 1)
                return go

            def turn_group(h):
                def go():
                    pe.wait_ge(v_copied, h + 1)
                    pe.wait_ge(b7_read, 6 * h + 2)
                    for k in range(NCH):
                        last = pe.transpose(aux[:, 3, k * P:(k + 1) * P], v_g[:, k * P:(k + 1) * P], ident[:, :])
                    last.then_inc(b7_made, 1)
                return go

            def mix_group(h):
                def go():
                    pe.wait_ge(w_masked, 1)
                    pe.wait_ge(b7_read, 6 * h + 4)
                    for k in range(NCH):
                        last = pe.matmul(aux[:, 3, k * P:(k + 1) * P], vr_g[:, k, :], wm[:, h, :],
                                         start=True, stop=True)
                    last.then_inc(b7_made, 1)
                return go

            for g in range(NKV):
                with pe.Fori(REP * g, REP * (g + 1)) as h:
                    for i in range(NCH):
                        u = (U_GATE // 2 + 2 * h + i // 2, i % 2)
                        unit(u, a_hi, a_lo, a_ready, x_need,
                             [None, (None, None, turn_group(h), mix_group(h))[i],
                              turn_probs(g, h, i), attend(g, h, i)], first_hook=scores(g, h, i))

            with pe.Fori(0, MB // 2) as i:
                for p in range(2):
                    unit((U_PROJ // 2 + i, p), a_hi, a_lo, a_ready, lambda c: KT + CK * (c + 1),
                         projections=True)
            late = lambda u: num(u) + MB - 1
            with pe.Fori(0, MB // 2) as i:
                for p in range(2):
                    unit((U_OUT // 2 + i, p), b_hi, b_lo, b_ready, x_need, before=late)
            norm_sum(N_NORM_X2, acc_x, (x2_squared, MB))
            with pe.Fori(0, FG) as f:
                with pe.Fori(0, MB // 2) as i:
                    for p in range(2):
                        unit((U_FF // 2 + MB * f + i, p), a_hi, a_lo, a_ready,
                             lambda c: 2 * KT + CK * (c + 1), before=late)
                with pe.Fori(0, MB // 2) as i:
                    for p in range(2):
                        unit((U_FF // 2 + MB // 2 + MB * f + i, p), b_hi, b_lo, b_ready,
                             lambda c: KT + KT * f + CK * (c + 1), before=late)

        @block.scalar
        def _(act):
            steps = Steps(act, act_step)
            run = act.activation

            def hi(u, c):
                n = num(u)
                if c % 2 == 0:
                    act.wait_ge(raw_loaded[2 * u[1] + c // 2], 16 * (u[0] + 1))
                if not (type(n) is int and n == 0):
                    act.wait_ge(chunk_done, 4 * n - 3 + c)
                run(w_hi[:, c, :], raw(u, c), ACT.Copy).then_inc(hi_split, 1)

            def beside(u, jobs=(), first=None):
                if first:
                    first()
                for c in range(CH):
                    hi(after(u), c)
                    if c < len(jobs) and jobs[c]:
                        jobs[c]()

            def guess(n, w=TOK):
                act.wait_ge(norm_base, n + 1)
                steps.did(run(nr[:, 0:w], na[:, 0:w], ACT.Ln))
                steps.did(run(nr[:, 0:w], nr[:, 0:w], ACT.Exp, scale=-0.5))
                run(nq[:, 0:w], nr[:, 0:w], ACT.Square).then_inc(norm_guess, 1)

            act.dma_start(gains[:, 0:44], t["gains"]).then_inc(gains_loaded, 16)
            act.wait_ge(gains_loaded, 16)
            for c in range(CH):
                hi(straight(0), c)
                act.wait_ge(x_loaded[c], 16)
                for kt in range(CK * c, CK * (c + 1)):
                    run(a_hi[:, kt, :], x_raw[:, kt, :], ACT.Copy, scale=g_mix[:, kt:kt + 1]).then_inc(act_hi, 1)
                    if kt >= 2:
                        act.wait_ge(x_added, kt - 1)
                    run(z[:, kt % 2, :], x_raw[:, kt, :], ACT.Square).then_inc(x_squared, 1)

            def store(n):
                act.wait_ge(z_made, n + 1)
                act.dma_start(t["kv_t"][n], z[:, n % 2, :]).then_inc(z_stored[n % 2], 16)

            def square(n, u, src):
                act.wait_ge(z_made, num(u) + 1)
                act.wait_ge(summed, n)
                run(sq[:, :], src, ACT.Square).then_inc(squared, 1)

            def v_rows(j):
                act.wait_ge(v_turned, j + 1)
                run(v_row[:, j, :, :], aux[:, 2, :].rearrange("p (k d) -> p k d", k=NCH), ACT.Copy
                    ).then_inc(v_row_made, 1)

            for n in range(U_KV):
                beside(straight(n))
                if n == 0:
                    guess(0)
                store(n)
            for j in range(4):
                beside(straight(U_KV + 2 * j), [None, None, (lambda: v_rows(j - 1)) if j else None])
                store(U_KV + 2 * j)
                square(N_NORM_K + j, straight(U_KV + 2 * j), z[:, 0, :])
                beside(straight(U_KV + 2 * j + 1), [None, lambda: guess(N_NORM_K + j)])
                store(U_KV + 2 * j + 1)

            def wg_parts():
                act.wait_ge(wg_loaded, 16)
                run(wg_hi[:, :, :], wg_raw[:, :, :], ACT.Copy).then_inc(wg_hi_made, 1)

            def gates_tanh():
                act.wait_ge(gz_made, 1)
                run(gz[:, :, :], gz[:, :, :], ACT.Tanh, scale=0.5).then_inc(gz_tanh, 1)

            def square_windows():
                act.wait_ge(kc_made, 1)
                act.wait_ge(summed, N_NORM_C)
                run(sq[:, 0:NKV * W_USED], kc_t[:, :, :].rearrange("p g w -> p (g w)"), ACT.Square
                    ).then_inc(squared, 1)

            for h in range(NH):
                n = U_Q + h
                jobs = [None, (lambda: guess(n_norm_q(h - 1))) if h else wg_parts, None, None]
                if h == 0:
                    jobs[2] = lambda: v_rows(3)
                if h == 2:
                    jobs[2] = gates_tanh
                if h == NH // 2:
                    jobs[2:] = [square_windows, lambda: guess(N_NORM_C, NKV * W_USED)]
                beside(straight(n), jobs)
                square(n_norm_q(h), straight(n), z[:, n % 2, :])

            def smp_norm_guess(b):
                act.wait_ge(smp_base, b + 1)
                steps.did(run(k_r, k_a, ACT.Ln))
                steps.did(run(k_r, k_r, ACT.Exp, scale=-0.5))
                run(k_q, k_r, ACT.Square).then_inc(smp_guess, 1)

            def smp_exps(b):
                act.wait_ge(smp_max, b + 1)
                for n, w in enumerate((PAST + 1, PAST + 1, W_SAMPLE)):
                    last = run(sp[:, n, 0:w], sp[:, n, 0:w], ACT.Exp, bias=mn[0:NH, n:n + 1],
                               accum_out=ls[0:NH, GATE_OF[n]:GATE_OF[n] + 1])
                last.then_inc(smp_exp, 1)

            def smp_ks_in(b):
                act.wait_ge(smp_kturned, 2 * b + 1)
                run(ks_t[:, :, 0:PAST], aux[:, 0, :].rearrange("p (g k) -> p g k", g=NKV), ACT.Copy,
                    scale=g_k[:, 1:2]).then_inc(smp_ks, 1)

            def gelu(b, p, dst):
                act.wait_ge(z_made, U_VU + 2 * b + p + 1)
                run(dst[:, b, :], z[:, p, :], ACT.Gelu_apprx_tanh).then_inc(z_read, 1)

            beside((U_VU // 2, 0), [lambda: guess(n_norm_q(NH - 1)), lambda: smp_norm_guess(0), None,
                                    lambda: smp_ks_in(0)])
            gelu(0, 0, v_t)
            beside((U_VU // 2, 1), first=lambda: smp_exps(0))
            gelu(0, 1, u_t)
            with steps.loop(1, DEC, 2) as b:
                beside((U_VU // 2 + b, 0), [None, None, lambda: smp_ks_in(b)], first=lambda: smp_norm_guess(b))
                gelu(b, 0, v_t)
                beside((U_VU // 2 + b, 1), first=lambda: smp_exps(b))
                gelu(b, 1, u_t)
            guess(N_NORM_V)

            def exps(a, i):
                act.wait_ge(s_max, a + 1)
                for n, (x, w) in enumerate(((p_s, P * (i + 1)), (p_w, P * (i + 1)), (p_c, seen(i)))):
                    last = run(x[:, 0:w], x[:, 0:w], ACT.Exp, bias=mn[:, n:n + 1],
                               accum_out=ls[:, GATE_OF[n]:GATE_OF[n] + 1])
                last.then_inc(s_exp, 1)

            def probs_out(a, i):
                act.wait_ge(p_turned, a + 1)
                run(pt_sel[:, 0:i + 1, :], aux[:, 0, 0:P * (i + 1)].rearrange("p (k q) -> p k q", k=i + 1),
                    ACT.Copy).then_inc(pt_sel_made, 1)

            def load_bias(h):
                act.wait_ge(s_max, NCH * h)
                act.dma_start(toep[:, :], toep_d[h]).then_inc(toep_loaded, 16)

            def copy_queries(h):
                act.wait_ge(scored, NCH * h)
                run(q_h[:, :], q_t[:, h, 0:SEQ], ACT.Copy).then_inc(q_copied, 1)

            def copy_values(h):
                act.wait_ge(v_normed, 1)
                act.wait_ge(b7_read, 6 * h)
                run(v_g[:, :], v_t[:, h, :], ACT.Copy).then_inc(v_copied, 1)

            def mixed(kt):
                act.wait_ge(chunk_done, CH * (U_PROJ - 1) + kt // CK + 1)
                src = u_t[:, kt, :] if kt < GRP else q_t[:, kt - GRP, :]
                run(a_hi[:, kt, :], src, ACT.Copy).then_inc(act_hi, 1)

            def mixed_chunk(c):
                for kt in range(CK * c, CK * (c + 1)):
                    mixed(kt)

            def head(h, ahead):
                for i in range(NCH):
                    a = NCH * h + i
                    u = (U_GATE // 2 + 2 * h + i // 2, i % 2)
                    jobs = [None, None, lambda: probs_out(a, i), None]
                    if i == 2:
                        jobs[0] = lambda: copy_values(h)
                    if i == NCH - 1 and ahead:
                        jobs[:2] = [lambda: load_bias(h + 1), lambda: copy_queries(h + 1)]
                    if i == NCH - 1 and not ahead:
                        jobs = [lambda: mixed_chunk(0), None, jobs[2], None]
                    beside(u, jobs, first=lambda: exps(a, i))
                    act.wait_ge(z_made, num(u) + 1)
                    run(z[:, i % 2, :], z[:, i % 2, :], ACT.Tanh, scale=0.5).then_inc(g_tanh, 1)

            act.wait_ge(toep_stored, 16)
            load_bias(0)
            copy_queries(0)
            for g in range(NKV):
                with steps.loop(REP * g, REP * (g + 1) - g, 0) as h:
                    head(h, True)
            head(NH - 1, False)
            act.wait_ge(b7_read, 6 * NH)
            for c in range(1, CH):
                mixed_chunk(c)

            def split_hi(count, dst, src, func=ACT.Copy):
                act.wait_ge(act_src, count)
                run(dst, src, func).then_inc(act_hi, 1)

            with steps.loop(0, MB // 2, 0) as i:
                for p in range(2):
                    beside((U_PROJ // 2 + i, p))
                    split_hi(1 + 2 * i + p, b_hi[:, 2 * i + p, :], cm[:, :])
            with steps.loop(0, MB // 2, 0) as i:
                for p in range(2):
                    beside((U_OUT // 2 + i, p))
                    split_hi(1 + MB + 2 * i + p, a_hi[:, 2 * i + p, :], na[:, :])
            guess(N_NORM_X2)

            def up(f, i, p):
                beside((U_FF // 2 + MB * f + i, p))
                split_hi(1 + 2 * MB + MB * f + 2 * i + p, b_hi[:, 2 * i + p, :], z[:, p, :], ACT.Square)

            def down(f, i, p):
                u = (U_FF // 2 + MB // 2 + MB * f + i, p)
                if more(u):
                    beside(u)

            ff_loops(act, up, down)
            for p in range(2):
                act.wait_ge(z_stored[p], 16 * (U_Q // 2))

        @block.vector
        def _(dve):
            steps = Steps(dve, dve_step)

            def lo(u, c):
                n = num(u)
                dve.wait_ge(hi_split, 4 * n + c + 1)
                dve.tensor_tensor(w_lo[:, c, :], raw(u, c), w_hi[:, c, :].bitcast(F32), ALU.subtract
                                  ).then_inc(lo_split, 1)

            def beside(u, jobs=(), first=None):
                if first:
                    first()
                for c in range(CH):
                    lo(after(u), c)
                    if c < len(jobs) and jobs[c]:
                        jobs[c]()

            def mean(n, count, w=None):
                dve.wait_ge(summed, n + 1)
                dst, src = (halves(na[:, :]), aux[:, 0:2, 0:HT]) if w is None else (na[:, 0:w], aux[:, 0, 0:w])
                dve.tensor_scalar(dst, src, 1.0 / count, EPS, ALU.mult, ALU.add).then_inc(norm_base, 1)

            def newton(n, dst, w=TOK):
                dve.wait_ge(norm_guess, n + 1)
                steps.did(dve.scalar_tensor_tensor(nq[:, 0:w], nq[:, 0:w], -0.5, na[:, 0:w], ALU.mult, ALU.mult))
                steps.did(dve.scalar_tensor_tensor(dst, nq[:, 0:w], 1.5, nr[:, 0:w], ALU.add, ALU.mult))

            def scale_out(u, dst):
                dve.wait_ge(chunk_done, CH * num(u) + CH)
                dve.tensor_tensor(halves(dst), pair(u[1]), halves(rstd[:, :]), ALU.mult).then_inc(mm_read, 1)

            def rel_rows():
                dve.wait_ge(rel_made, 1)
                dve.tensor_copy(rel_row[:, 0:512], aux[0:NH, 2, 0:512])
                steps.did(dve.tensor_copy(rel_row[:, 512:NREL], aux[0:NH, 3, 0:NREL - 512]))
                o = SEQ - 1 - PAST
                dve.tensor_copy(rel_s[:, 0:PAST + 1], rel_row[:, o:o + PAST + 1]).then_inc(rel_done, 1)

            dve.wait_ge(gains_loaded, 16)
            steps.did(dve.tensor_scalar(g_qs, g_q, HD ** -0.5, None, ALU.mult))
            for c in range(CH):
                lo(straight(0), c)
                for kt in range(CK * c, CK * (c + 1)):
                    dve.wait_ge(act_hi, kt + 1)
                    dve.scalar_tensor_tensor(a_lo[:, kt, :], x_raw[:, kt, :], g_mix[:, kt:kt + 1],
                                             a_hi[:, kt, :].bitcast(F32), ALU.mult, ALU.subtract).then_inc(a_ready, 1)

            def z_free(n):
                if 2 <= n < U_Q + 2:
                    dve.wait_ge(z_stored[n % 2], 16 * min(n // 2, U_Q // 2))
                if 2 <= n < U_KV + 2:
                    dve.wait_ge(z_copied, n - 1)
                if n > U_KV + 1 and n % 2 == 1:
                    dve.wait_ge(v_row_made, min((n - U_KV) // 2, 4))

            for n in range(U_KV):
                beside(straight(n), [None, rel_rows if n == 1 else None])
                if n == 0:
                    mean(0, D_MODEL)
                    newton(0, rstd[:, :])
                z_free(n)
                scale_out(straight(n), z[:, n % 2, :])

            def key_norm(j):
                newton(N_NORM_K + j, nr[:, :])
                dve.scalar_tensor_tensor(k_t[:, j, :], z[:, 0, :], g_k[:, 1 + j // 2:2 + j // 2], nr[:, :],
                                         ALU.mult, ALU.mult)

            def query_norm(h, p):
                newton(n_norm_q(h), nr[:, :])
                dve.scalar_tensor_tensor(q_t[:, h, :], z[:, p, :], g_qs, nr[:, :], ALU.mult, ALU.mult)

            def pages_in(h):
                for k in range(NPG):
                    dve.wait_ge(page_turned, 2 * h + k + 1)
                    dve.tensor_copy(kv_t[:, :, bass.ds(SEQ + PAST * h + PAGE * k, PAGE)],
                                    aux[:, 2 + k, :].rearrange("p (q n) -> p q n", q=4)).then_inc(page_read, 1)

            for j in range(4):
                n = U_KV + 2 * j
                beside(straight(n), [None, None, lambda: pages_in(2 * j)])
                z_free(n)
                scale_out(straight(n), z[:, 0, :])
                beside(straight(n + 1), [None, lambda: mean(N_NORM_K + j, HD),
                                         lambda: (key_norm(j), pages_in(2 * j + 1))])
                z_free(n + 1)
                scale_out(straight(n + 1), z[:, 1, :])
                dve.wait_ge(mm_read, n + 2)
                dve.tensor_copy(v_new[:, j, :], z[:, 1, SEQ:TOK])

            def wg_parts():
                dve.wait_ge(wg_hi_made, 1)
                dve.tensor_tensor(wg_lo[:, :, :], wg_raw[:, :, :], wg_hi[:, :, :].bitcast(F32), ALU.subtract
                                  ).then_inc(wg_split, 1)

            def compressed(kv, dst, made):
                dve.wait_ge(cmp_used, (kv + 1) * CMP_LEN // CJ)
                src = aux[:, 2 + kv, 0:NKV * (W_ALL + 1)].rearrange("p (g w) -> p g w", g=NKV)
                steps.did(dve.tensor_copy(vs_tmp[:, kv:kv + 1], src[:, 0, W_ALL:W_ALL + 1]))
                dve.tensor_scalar(dst[:, :, :], src[:, :, 0:W_USED], vs_tmp[:, kv:kv + 1], None, ALU.add
                                  ).then_inc(made, 1)

            def gates_in():
                dve.wait_ge(gates_summed, 1)
                steps.did(dve.tensor_copy(tok_rstd[:, 0:NCH + 1], aux[:, 3, 256:256 + NCH + 1]))
                for tb in range(NCH + 1):
                    last = dve.tensor_scalar(gz[:, tb, :], aux[:, 3, N_GATE * tb:N_GATE * (tb + 1)],
                                             tok_rstd[:, tb:tb + 1], None, ALU.mult)
                last.then_inc(gz_made, 1)

            def gates_out():
                dve.wait_ge(gz_tanh, 1)
                dve.tensor_scalar(gates[:, :, :], gz[:, :, :], 0.5, 0.5, ALU.mult, ALU.add).then_inc(gates_made, 1)

            def key_windows_norm():
                newton(N_NORM_C, nr[:, 0:NKV * W_USED], NKV * W_USED)
                steps.did(dve.scalar_tensor_tensor(kc_t[:, :, :], kc_t[:, :, :], g_k[:, 0:1],
                                                   nr[:, 0:NKV * W_USED].rearrange("p (g w) -> p g w", g=NKV),
                                                   ALU.mult, ALU.mult))

            def windows_turned():
                dve.wait_ge(vcp_turned, 1)
                dve.tensor_copy(vc_p[0:W_PROMPT, :, :],
                                aux[0:W_PROMPT, 2, 0:NKV * P].rearrange("p (g d) -> p g d", g=NKV)
                                ).then_inc(vcp_made, 1)

            for h in range(NH):
                n = U_Q + h
                jobs = [None, None, None, None]
                if h:
                    jobs[1:3] = [lambda: mean(n_norm_q(h - 1), HD), lambda: query_norm(h - 1, 1 - h % 2)]
                if h == 0:
                    jobs[2] = wg_parts
                if h == 2:
                    jobs[0] = gates_in
                if h == 3:
                    jobs[0] = gates_out
                if h == NH // 2:
                    jobs[0] = lambda: compressed(0, kc_t, kc_made)
                    jobs[3] = lambda: mean(N_NORM_C, HD, NKV * W_USED)
                if h == NH // 2 + 1:
                    jobs[0] = key_windows_norm
                beside(straight(n), jobs)
                z_free(n)
                scale_out(straight(n), z[:, n % 2, :])

            def smp_copies(b):
                dve.tensor_copy(v_new_b, v_new[:, :, bass.ds(b, 1)].rearrange("p s o -> p (s o)"))
                dve.tensor_copy(vc_b[:, :, 0:W_SAMPLE],
                                vc_t[:, :, bass.ds(SEQ // STRIDE + b * (PAST // STRIDE), W_SAMPLE)]
                                ).then_inc(smp_static, 1)

            def smp_norms(b):
                dve.wait_ge(keys_loaded, 48 * b + 48)
                dve.wait_ge(smp_static, b + 1)
                for n in range(4):
                    for g in range(NKV):
                        k = stage[:, n, g * HD:(g + 1) * HD]
                        junk = (na, nr)[n // 2][:, (2 * (n % 2) + g) * HD:(2 * (n % 2) + g + 1) * HD]
                        last = dve.tensor_tensor_reduce(junk, k, k, 1.0, 0.0, ALU.mult, ALU.add,
                                                        k_ss[:, 2 * n + g:2 * n + g + 1])
                steps.did(last)
                dve.tensor_scalar(k_a, k_ss, 1.0 / HD, EPS, ALU.mult, ALU.add).then_inc(smp_base, 1)

            def smp_scale_keys(b):
                dve.wait_ge(smp_guess, b + 1)
                steps.did(dve.scalar_tensor_tensor(k_q, k_q, -0.5, k_a, ALU.mult, ALU.mult))
                steps.did(dve.scalar_tensor_tensor(k_rs, k_q, 1.5, k_r, ALU.add, ALU.mult))
                for n in range(4):
                    for g in range(NKV):
                        k = stage[:, n, g * HD:(g + 1) * HD]
                        last = dve.tensor_scalar(k, k, k_rs[:, 2 * n + g:2 * n + g + 1], None, ALU.mult)
                last.then_inc(smp_keys, 1)
                dve.wait_ge(smp_vturned, b + 1)
                dve.tensor_copy(v_new_r[:, :, :], aux[0:1, 2, :].rearrange("p (s d) -> p s d", s=4))
                dve.tensor_copy(vc_s[0:W_SAMPLE, :, :],
                                aux[0:W_SAMPLE, 3, 0:NKV * P].rearrange("p (g d) -> p g d", g=NKV)
                                ).then_inc(smp_vmade, 1)

            def smp_keys_in(b):
                dve.wait_ge(smp_kturned, 2 * b + 2)
                dve.tensor_scalar(kw_t[:, :, 0:PAST], aux[:, 1, :].rearrange("p (g k) -> p g k", g=NKV),
                                  g_k[:, 2:3], None, ALU.mult)
                for br, dst in enumerate((ks_t, kw_t)):
                    dve.tensor_copy(dst[:, :, PAST:PAST + 1], k_t[:, 2 * br:2 * br + 2, bass.ds(SEQ + b, 1)])
                for g in range(NKV):
                    last = dve.tensor_copy(qm[:, g, REP * g:REP * (g + 1)],
                                           q_t[:, REP * g:REP * (g + 1), bass.ds(SEQ + b, 1)
                                               ].rearrange("p h o -> p (h o)"))
                last.then_inc(smp_kw, 1)

            def smp_softmax(b):
                dve.wait_ge(smp_scored, b + 1)
                carry(nc.vector)
                r = rel_s[:, 0:PAST + 1]
                rc = rel_s[:, CMP_LEN - 1:CMP_LEN - 1 + STRIDE * (W_SAMPLE - 1) + 1:STRIDE]
                for n, (s_, bias, w) in enumerate(((aux[0:NH, 2, 0:PAST + 1], r, PAST + 1),
                                                   (aux[0:NH, 3, 0:PAST + 1], r, PAST + 1),
                                                   (aux[0:NH, 2, 300:300 + W_SAMPLE], rc, W_SAMPLE))):
                    last = dve.tensor_tensor_reduce(sp[:, n, 0:w], s_, bias, 1.0, -3e38, ALU.add, ALU.max,
                                                    mx[0:NH, n:n + 1])
                steps.did(last)
                dve.tensor_scalar(mn[0:NH, :], mx[0:NH, :], -1.0, None, ALU.mult).then_inc(smp_max, 1)

            def smp_divide(b):
                dve.wait_ge(smp_exp, b + 1)
                steps.did(dve.reciprocal(rl[0:NH, :], ls[0:NH, :]))
                steps.did(dve.tensor_tensor(rl[0:NH, :], rl[0:NH, :],
                                            gs_row[:, bass.ds(b, 1), :].rearrange("p o j -> p (o j)"), ALU.mult))
                for n, w in ((0, PAST + 1), (1, PAST + 1), (2, W_SAMPLE)):
                    last = dve.tensor_scalar(sp[:, n, 0:w], sp[:, n, 0:w],
                                             rl[0:NH, GATE_OF[n]:GATE_OF[n] + 1], None, ALU.mult)
                last.then_inc(smp_probs, 1)

            def smp_probs_out(b):
                dve.wait_ge(smp_pturned, b + 1)
                dve.tensor_copy(pt_s[:, 0:4 * NH], aux[:, 0, 0:4 * NH])
                dve.tensor_copy(pt_s[0:1, 4 * NH:6 * NH], aux[0:1, 0, 4 * NH:6 * NH])
                dve.tensor_copy(pt_s[0:W_SAMPLE, 6 * NH:7 * NH], aux[0:W_SAMPLE, 0, 6 * NH:7 * NH]
                                ).then_inc(smp_pmade, 1)

            def smp_result(b):
                dve.wait_ge(smp_out, b + 1)
                carry(nc.vector)
                dve.tensor_copy(q_t[:, :, bass.ds(SEQ + b, 1)].rearrange("p h o -> p (h o)"), aux[:, 1, 0:NH]
                                ).then_inc(smp_read, 1)

            def smp_pair(b):
                scale_out((U_VU // 2 + b, 0), z[:, 0, :])
                beside((U_VU // 2 + b, 1), [lambda: smp_divide(b), lambda: smp_probs_out(b), None,
                                            lambda: smp_result(b)], first=lambda: smp_softmax(b))
                dve.wait_ge(z_read, 2 * b)
                scale_out((U_VU // 2 + b, 1), z[:, 1, :])

            beside((U_VU // 2, 0), [lambda: (compressed(1, vc_t, vc_made), mean(n_norm_q(NH - 1), HD)),
                                    lambda: (query_norm(NH - 1, 1), smp_copies(0), smp_norms(0)),
                                    lambda: (windows_turned(), smp_scale_keys(0)), lambda: smp_keys_in(0)])
            dve.wait_ge(gate_loaded, 16)
            dve.wait_ge(consts_set, 2)
            smp_pair(0)
            with steps.loop(1, DEC, 6) as b:
                beside((U_VU // 2 + b, 0), [None, lambda: smp_scale_keys(b), lambda: smp_keys_in(b)],
                       first=lambda: (smp_copies(b), smp_norms(b)))
                dve.wait_ge(z_read, 2 * b - 1)
                smp_pair(b)

            mean(N_NORM_V, D_GM)

            def v_scaled(first, last):
                for g in range(first, last):
                    dve.scalar_tensor_tensor(v_t[:, g, :], v_t[:, g, :], g_sgu[:, g:g + 1], nr[:, :],
                                             ALU.mult, ALU.mult)

            def v_norm():
                newton(N_NORM_V, nr[:, :])
                dve.wait_ge(z_read, 2 * GRP)
                v_scaled(0, 1)

            def v_norm_end():
                v_scaled(GRP - 2, GRP - 1)
                dve.scalar_tensor_tensor(v_t[:, GRP - 1, :], v_t[:, GRP - 1, :], g_sgu[:, GRP - 1:GRP], nr[:, :],
                                         ALU.mult, ALU.mult).then_inc(v_normed, 1)

            def smp_gating():
                dve.wait_ge(v_normed, 1)
                dve.wait_ge(gm_loaded, 32)
                for g in range(GRP):
                    last = dve.tensor_scalar(na[:, DEC * g:DEC * (g + 1)], v_t[:, g, SEQ:TOK], w00[:, g:g + 1],
                                             b_bc[:, g, 0:1], ALU.mult, ALU.add)
                steps.did(last)
                steps.did(dve.tensor_tensor(u_t[:, :, SEQ:TOK], u_t[:, :, SEQ:TOK],
                                            na[:, 0:DEC * GRP].rearrange("p (g b) -> p g b", g=GRP), ALU.mult))

            def softmax(h, a, i):
                dve.wait_ge(scored, a + 1)
                if i == 0:
                    dve.wait_ge(toep_loaded, 16 * h + 16)
                carry(nc.vector)
                o = SEQ - P * (i + 1)
                w = P * (i + 1)
                oc = o + CMP_LEN - 1
                for n, (x, s_, bias) in enumerate((
                        (p_s[:, 0:w], aux[:, 0, 0:w], toep[:, o:SEQ]),
                        (p_w[:, 0:w], aux[:, 1, 0:w], toep[:, o:SEQ]),
                        (p_c[:, 0:seen(i)], aux[:, 2, 0:seen(i)], toep[:, oc:oc + STRIDE * (seen(i) - 1) + 1:STRIDE]))):
                    last = dve.tensor_tensor_reduce(x, s_, bias, 1.0, -3e38, ALU.add, ALU.max, mx[:, n:n + 1])
                steps.did(last)
                dve.tensor_scalar(mn, mx, -1.0, -0.1 * NEG, ALU.mult, ALU.min).then_inc(s_max, 1)

            def divide(h, a, i):
                dve.wait_ge(s_exp, a + 1)
                steps.did(dve.tensor_scalar(ls, ls, 1e-30, None, ALU.max))
                steps.did(dve.reciprocal(rl, ls))
                steps.did(dve.tensor_tensor(rl, rl, gates[:, i, bass.ds(3 * h, 3)], ALU.mult))
                for n, (x, w) in enumerate(((p_s, P * (i + 1)), (p_w, P * (i + 1)), (p_c, seen(i)))):
                    last = dve.tensor_scalar(x[:, 0:w], x[:, 0:w], rl[:, GATE_OF[n]:GATE_OF[n] + 1], None, ALU.mult)
                last.then_inc(probs, 1)

            def group(h, i):
                if i == 2:
                    dve.wait_ge(b7_made, 6 * h + 3)
                    dve.tensor_copy(vr_g[:, :, :], aux[:, 3, :].rearrange("p (k c) -> p k c", k=NCH)
                                    ).then_inc(b7_read, 1)
                if i == 3:
                    dve.wait_ge(b7_made, 6 * h + 5)
                    dve.tensor_tensor(na[:, 0:SEQ].rearrange("p (k t) -> p k t", k=NCH),
                                      aux[:, 3, :].rearrange("p (k t) -> p k t", k=NCH),
                                      b_bc[:, bass.ds(h, 1), :].to_broadcast([P, NCH, P]), ALU.add
                                      ).then_inc(b7_read, 1)
                    dve.wait_ge(b7_read, 6 * h + 5)
                    dve.tensor_tensor(u_t[:, h, 0:SEQ], u_t[:, h, 0:SEQ], na[:, 0:SEQ], ALU.mult)

            def probs_out(a, i):
                dve.wait_ge(p_turned, a + 1)
                dve.tensor_copy(pt_win[:, 0:i + 1, :], aux[:, 1, 0:P * (i + 1)].rearrange("p (k q) -> p k q", k=i + 1))
                dve.tensor_copy(pt_cmp[0:seen(i), :], aux[0:seen(i), 2, 0:P]).then_inc(pt_made, 1)

            def mixed_chunk(c):
                for kt in range(CK * c, CK * (c + 1)):
                    src = u_t[:, kt, :] if kt < GRP else q_t[:, kt - GRP, :]
                    dve.wait_ge(act_hi, KT + kt + 1)
                    dve.tensor_tensor(a_lo[:, kt, :], src, a_hi[:, kt, :].bitcast(F32), ALU.subtract
                                      ).then_inc(a_ready, 1)

            def head(h, extra=()):
                for i in range(NCH):
                    a = NCH * h + i
                    u = (U_GATE // 2 + 2 * h + i // 2, i % 2)
                    more_jobs = extra[i] if i < len(extra) else [None] * CH
                    jobs = [[lambda: divide(h, a, i)], [lambda: group(h, i)] if i >= 2 else [],
                            [lambda: probs_out(a, i)], []]
                    for c in range(CH):
                        if more_jobs[c]:
                            jobs[c].append(more_jobs[c])
                    together = lambda fs: (lambda: [f() for f in fs])
                    beside(u, [together(fs) for fs in jobs], first=lambda: softmax(h, a, i))
                    dve.wait_ge(g_stored[i % 2], 32 * h + 16 * (i // 2))
                    scale_out(u, z[:, i % 2, :])
                    dve.wait_ge(b7_made, 6 * h + (1, 2, 4, 6)[i])
                    dve.tensor_copy(q_t[:, h, P * i:P * (i + 1)], aux[:, 3, 0:P]).then_inc(b7_read, 1)

            dve.wait_ge(gates_made, 1)
            head(0, [[None, v_norm, lambda: v_scaled(1, 2), lambda: v_scaled(2, 3)],
                     [lambda: v_scaled(3, 4), lambda: v_scaled(4, 6), None, v_norm_end],
                     [None, None, None, smp_gating]])
            with steps.loop(1, REP, 16) as h:
                head(h)
            with steps.loop(REP, NH - 1, 16) as h:
                head(h)
            head(NH - 1, [[None] * CH] * 3 + [[lambda: mixed_chunk(0), None, None, None]])
            dve.wait_ge(b7_read, 6 * NH)
            for c in range(1, CH):
                mixed_chunk(c)

            with steps.loop(0, MB // 2, 0) as i:
                for p in range(2):
                    m = 2 * i + p
                    u = (U_PROJ // 2 + i, p)
                    n = num(u)

                    def first():
                        dve.wait_ge(g_loaded[p], 16 * i + 16)
                        dve.tensor_tensor(halves(ca[:, :]), pair(0), halves(g_in[:, p, 0, :]), ALU.mult
                                          ).then_inc(mm_read, 1)

                    beside(u, [None, first])
                    dve.wait_ge(chunk_done, CH * n + CH)
                    dve.tensor_tensor(halves(cb[:, :]), pair(1), halves(g_in[:, p, 1, :]), ALU.mult).then_inc(mm_read, 1)
                    dve.wait_ge(mm_read, 2 * n - U_PROJ + 2)
                    dve.tensor_tensor(cm[:, :], ca[:, :], cb[:, :], ALU.add).then_inc(act_src, 1)
                    dve.wait_ge(act_src, m + 1)
                    dve.wait_ge(act_hi, 2 * KT + m + 1)
                    dve.tensor_tensor(b_lo[:, m, :], cm[:, :], b_hi[:, m, :].bitcast(F32), ALU.subtract
                                      ).then_inc(b_ready, 1)

            with steps.loop(0, MB // 2, 0) as i:
                for p in range(2):
                    m = 2 * i + p
                    u = (U_OUT // 2 + i, p)
                    beside(u)
                    dve.wait_ge(x_in_loaded[p], 16 * i + 16)
                    dve.wait_ge(chunk_done, CH * num(u) + CH)
                    dve.tensor_tensor(halves(x2[:, m, :]), pair(p), halves(z[:, p, :]), ALU.add).then_inc(mm_read, 1)
                    dve.wait_ge(mm_read, num(u) + MB + 1)
                    dve.tensor_scalar(na[:, :], x2[:, m, :], g_mlp[:, bass.ds(m, 1)], None, ALU.mult
                                      ).then_inc(act_src, 1)
                    dve.wait_ge(act_src, 1 + MB + m)
                    dve.wait_ge(act_hi, 3 * KT + m + 1)
                    dve.tensor_tensor(a_lo[:, m, :], na[:, :], a_hi[:, m, :].bitcast(F32), ALU.subtract
                                      ).then_inc(a_ready, 1)
            dve.wait_ge(a_ready, 3 * KT)
            mean(N_NORM_X2, D_MODEL)
            newton(N_NORM_X2, rstd[:, :])

            def up(f, i, p):
                m = 2 * i + p
                u = (U_FF // 2 + MB * f + i, p)
                beside(u)
                dve.wait_ge(chunk_done, CH * num(u) + CH)
                dve.scalar_tensor_tensor(halves(z[:, p, :]), pair(p), 0.0, halves(rstd[:, :]), ALU.max, ALU.mult
                                         ).then_inc(mm_read, 1)
                dve.wait_ge(mm_read, num(u) + MB + 1)
                dve.tensor_tensor(na[:, :], z[:, p, :], z[:, p, :], ALU.mult).then_inc(act_src, 1)
                dve.wait_ge(act_src, 1 + 2 * MB + MB * f + m)
                dve.wait_ge(act_hi, 4 * KT + MB * f + m + 1)
                dve.tensor_tensor(b_lo[:, m, :], na[:, :], b_hi[:, m, :].bitcast(F32), ALU.subtract
                                  ).then_inc(b_ready, 1)

            def down(f, i, p):
                m = 2 * i + p
                u = (U_FF // 2 + MB // 2 + MB * f + i, p)
                if more(u):
                    beside(u)
                dve.wait_ge(chunk_done, CH * num(u) + CH)
                dve.tensor_tensor(halves(x2[:, m, :]), pair(p), halves(x2[:, m, :]), ALU.add).then_inc(mm_read, 1)

            ff_loops(dve, up, down)

        @block.gpsimd
        def _(pool):
            steps = Steps(pool, pool_step)

            pool.dma_start(oh[:, :], t["one_hot"]).then_inc(consts_loaded, 16)
            pool.dma_start(rb[0:NB, :], t["rel_bias"]).then_inc(consts_loaded, 16)
            pool.dma_start(w00, t["w_00"].to_broadcast([P, GRP])).then_inc(consts_loaded, 16)
            pool.dma_start(table[:, :], t["table"]).then_inc(table_loaded, 16)
            steps.did(pool.memset(rb[NB:NB + 1, :], NEG))
            steps.did(pool.memset(ident[:, :], 0.0))
            steps.did(pool.affine_select(out=ident[:, :], in_=ident[:, :], compare_op=ALU.not_equal, fill=1.0,
                                         base=0, pattern=[[-1, P]], channel_multiplier=1))
            pool.memset(ones[:, :], 1.0).then_inc(consts_set, 1)
            pool.wait_ge(consts_set, 1)
            steps.did(pool.memset(acc_v[:, :], 0.0))
            for kt in range(KT):
                pool.wait_ge(x_squared, kt + 1)
                pool.wait_ge(x_added, kt)
                pool.tensor_tensor(acc_v[:, :], acc_v[:, :], z[:, kt % 2, :], ALU.add).then_inc(x_added, 1)
            pool.memset(qm[:, :, :], 0.0).then_inc(consts_set, 1)

            def load_w_cmp(n):
                pool.dma_start(w_cmp[:, n % 2, :, :], t["w_cmp"][n]).then_inc(cmp_loaded[n % 2], 16)

            def load_pages(h, p):
                for k in range(NPG):
                    page = pool.value_load(table[0:1, bass.ds(NPG * h + k, 1)], min_val=0, max_val=N_POOL - 1)
                    pool.dma_start(pages[:, p, k, :], t["cache_cmp"][page]).then_inc(page_loaded[p], 16)

            pool.wait_ge(table_loaded, 16)
            load_pages(0, 0)
            load_pages(1, 1)
            pool.wait_ge(a_ready, KT)
            pool.wait_ge(summed, 1)
            for s in range(4):
                pool.dma_start(kv_t[:, s, L_ALL:KVT_W], t["pos"][s // NKV]).then_inc(pos_loaded, 16)
            for n in range(U_KV):
                pool.wait_ge(z_made, n + 1)
                pool.tensor_copy(kv_t[:, n, 0:SEQ], z[:, n % 2, 0:SEQ]).then_inc(z_copied, 1)
            pool.wait_ge(z_copied, 1)
            steps.did(pool.memset(acc_v[:, :], 0.0))

            pool.wait_ge(rel_done, 1)
            pool.dma_start(rel_d, rel_row[:, :]).then_inc(rel_stored, 16)
            pool.wait_ge(rel_stored, 16)
            pool.dma_start(toep_d, bass.AP(tensor=rel_d.tensor, offset=P - 1,
                                           ap=[[NREL, NH], [-1, P], [1, SEQ]])).then_inc(toep_stored, 16)
            load_w_cmp(0)
            load_w_cmp(1)
            with pool.Fori(1, DEC // 2) as i:
                for p in range(2):
                    pool.wait_ge(page_turned, 2 * (2 * i + p - 2) + 2)
                    load_pages(2 * i + p, p)
            pool.wait_ge(page_turned, NPG * DEC)
            pool.dma_start(wg_raw[:, :, :], t["w_gates"]).then_inc(wg_loaded, 16)

            def load_keys(b):
                load_stage(b, 0, keys_loaded)

            def load_values(b):
                load_stage(b, 1, values_loaded)

            def load_stage(b, kv, loaded):
                cut = slice(kv * NKV * HD, (kv + 1) * NKV * HD)
                for k in range(NPG):
                    page = pool.value_load(table[0:1, bass.ds(NPG * b + k, 1)], min_val=0, max_val=N_POOL - 1)
                    pool.dma_start(stage[:, k, cut], t["cache_sel"][page][:, cut]).then_inc(loaded, 16)
                pool.dma_start(stage[:, 2:4, cut], t["state"][b].rearrange("(c p) n -> p c n", c=2)[:, :, cut]
                               ).then_inc(loaded, 16)

            for n in range(2, 2 * CMP_LEN // CJ):
                pool.wait_ge(cmp_used, n - 1)
                load_w_cmp(n)
                if n == 2 * CMP_LEN // CJ - 2:
                    pool.wait_ge(gates_made, 1)
                    pool.dma_start(gate_d, gates[P - DEC:P, NCH, :]).then_inc(gate_stored, 16)
                    pool.wait_ge(gate_stored, 16)
                    pool.dma_start(gs_row, gate_d.rearrange("b (h j) -> h b j", h=NH)).then_inc(gate_loaded, 16)
                    load_keys(0)

            def smp_pair(b, ahead):
                pool.wait_ge(smp_out, b)
                load_values(b)
                if ahead:
                    pool.wait_ge(smp_kturned, 2 * b + 2)
                    load_keys(b + 1)
                pool.wait_ge(z_read, 2 * b + 1)
                pool.wait_ge(v_acc, b)
                steps.did(pool.tensor_tensor(sq[:, :], v_t[:, b, :], v_t[:, b, :], ALU.mult))
                pool.tensor_tensor(acc_v[:, :], acc_v[:, :], sq[:, :], ALU.add).then_inc(v_acc, 1)

            with steps.loop(0, DEC - 1, 1) as b:
                smp_pair(b, True)
            smp_pair(DEC - 1, False)

            pool.wait_ge(smp_read, DEC)
            pool.dma_start(wm[:, :, :], t["w_mix"]).then_inc(gm_loaded, 16)
            pool.dma_start(b_bc[:, :, :].rearrange("p g t -> p (g t)"), t["b_mix"].to_broadcast([P, GRP * P])
                           ).then_inc(gm_loaded, 16)
            pool.wait_ge(gm_loaded, 32)
            pool.affine_select(out=wm[:, :, :], in_=wm[:, :, :], compare_op=ALU.is_ge, fill=0.0, base=0,
                               pattern=[[0, GRP], [1, P]], channel_multiplier=-1).then_inc(w_masked, 1)

            pool.wait_ge(v_normed, 1)
            pool.dma_start(t["v_t"], v_t[:, :, SEQ - P:TOK]).then_inc(v_stored, 16)
            pool.dma_start(t["win"], t["state"]).then_inc(win_stored, 16)

            with steps.loop(0, MB, 2) as m:
                for p in range(2):
                    pool.wait_ge(g_tanh, 2 * m + p + 1)
                    carry(nc.gpsimd)
                    steps.did(pool.tensor_scalar(z[:, p, :], z[:, p, :], 0.5, 0.5, ALU.mult, ALU.add))
                    pool.dma_start(merge_d[2 * m + p], z[:, p, :]).then_inc(g_stored[p], 16)

            pool.wait_ge(b7_read, 6 * NH)
            pool.wait_ge(v_stored, 16)
            pool.wait_ge(win_stored, 16)
            for p in range(2):
                pool.wait_ge(g_stored[p], 16 * MB)
            with pool.Fori(0, MB // 2) as i:
                for p in range(2):
                    pool.wait_ge(mm_read, U_PROJ + 2 * (2 * i + p) - 2)
                    pool.dma_start(g_in[:, p, :, :], merge_d.rearrange("(m t) p n -> m p t n", t=2)[2 * i + p]
                                   ).then_inc(g_loaded[p], 16)
            steps.did(pool.memset(acc_x[:, :], 0.0))
            with steps.loop(0, MB // 2, 2) as i:
                for p in range(2):
                    m = 2 * i + p
                    pool.wait_ge(mm_read, U_OUT + MB - 1 + m)
                    pool.dma_start(z[:, p, :], t["x_t"][m]).then_inc(x_in_loaded[p], 16)
                    pool.wait_ge(act_src, MB + m + 1)
                    pool.wait_ge(x2_squared, m)
                    steps.did(pool.tensor_tensor(nr[:, :], x2[:, m, :], x2[:, m, :], ALU.mult))
                    pool.tensor_tensor(acc_x[:, :], acc_x[:, :], nr[:, :], ALU.add).then_inc(x2_squared, 1)


_INS = ["x_t", "w", "gains", "one_hot", "rel_bias", "w_00", "table", "w_cmp", "pos", "cache_cmp", "cache_sel",
        "state", "w_gates", "w_mix", "b_mix"]
_OUTS = [("y_t", (MB, P, TOK)), ("kv_t", (U_Q, P, TOK)), ("v_t", (P, GRP, P + DEC)), ("win", (DEC, PAST, 512))]


def _layout(a):
    w_in = a["w_in"][0]
    x = np.concatenate([a["x_prompt"][0], a["x_sample"][:, 0]], 0)
    kvw = 2 * NKV * HD

    def blocks(w, rows=KT):
        n = w.shape[1] // P
        return w.reshape(rows, P, n, P).transpose(2, 1, 0, 3).reshape(n, P, rows * P)

    o = 2 * D_GM
    uv, q = blocks(w_in[:, :o]), blocks(w_in[:, o:o + NH * HD])
    o += NH * HD
    kv = [blocks(w_in[:, o + n * kvw:o + (n + 1) * kvw]) for n in range(3)]
    o += 3 * kvw
    w_gates = w_in[:, o:o + N_GATE].reshape(KT, P, N_GATE).transpose(1, 0, 2)
    o += N_GATE
    ga, gb = blocks(w_in[:, o:o + D_MODEL]), blocks(w_in[:, o + D_MODEL:])
    pairs = lambda f, s: np.stack([f, s], 1).reshape(-1, P, KT * P)
    up, down = a["w_up"][0], a["w_down"][0]
    parts = [kv[0], kv[1][[0, 2, 1, 3]], kv[2][[0, 2, 1, 3]], q, pairs(uv[GRP:], uv[:GRP]), pairs(ga, gb),
             np.concatenate([blocks(a["w_proj_gmlp"][0], GRP), blocks(a["w_proj_nsa"][0], NH)], 2),
             blocks(a["w_out"][0])]
    for f in range(FG):
        cut = slice(f * D_MODEL, (f + 1) * D_MODEL)
        parts += [blocks(up[:, cut]), blocks(down[cut])]
    cols = lambda g: g.reshape(-1, P).T
    rel = SEQ - 1 - np.arange(NREL)
    far = np.maximum(rel, 1).astype(np.float32)
    bucket = NB // 2 + (np.log(far / (NB // 2)) / np.log(128 / (NB // 2)) * (NB // 2)).astype(np.int32)
    bucket = np.where(rel < NB // 2, rel, np.minimum(bucket, NB - 1))
    bucket = np.where(rel < 0, NB, bucket)
    one_hot = (np.arange(NB + 1)[:, None] == bucket[None]).astype(np.float32)
    w_sgu = a["w_sgu"][0]
    w_cmp = np.stack([a["w_cmp_k"][0], a["w_cmp_v"][0]]).reshape(2 * CMP_LEN // CJ, CJ, HD, HD)
    return {
        "x_t": x.T.reshape(KT, P, TOK),
        "w": np.concatenate(parts),
        "gains": np.concatenate([cols(a["g_mix_norm"][0]), cols(a["g_mlp_norm"][0]), cols(a["g_sgu"][0]),
                                 cols(a["g_q"][0]), cols(a["g_k"][0])], 1),
        "one_hot": one_hot,
        "rel_bias": a["rel_bias"],
        "w_00": w_sgu[None, :, 0, 0],
        "table": a["page_table"].reshape(1, DEC * NPG),
        "w_cmp": w_cmp.transpose(0, 2, 1, 3),
        "pos": np.stack([a["pos_cmp_k"][0].T, a["pos_cmp_v"][0].T]),
        "cache_cmp": a["cache_cmp_kv"].reshape(N_POOL, PAGE, kvw),
        "cache_sel": a["cache_sel_kv"].reshape(N_POOL, PAGE, kvw),
        "state": a["state_win_kv"].reshape(DEC, PAST, kvw),
        "w_gates": w_gates,
        "w_mix": w_sgu.transpose(2, 0, 1),
        "b_mix": a["b_sgu"].reshape(1, GRP * P),
    }


def kernel(**inputs):
    import concourse.bacc as bacc
    from concourse.bass_utils import run_bass_kernel_spmd

    nc = bacc.Bacc("TRN2", target_bir_lowering=False, num_devices=1, dynamic_dma_scratch_size=8192)
    arrays = {n: np.ascontiguousarray(x) for n, x in _layout({k: np.asarray(v) for k, v in inputs.items()}).items()}
    t = {n: nc.dram_tensor(f"in_{n}", arrays[n].shape, mybir.dt.from_np(arrays[n].dtype), kind="ExternalInput").ap()
         for n in _INS}
    t |= {n: nc.dram_tensor(f"out_{n}", shape, F32, kind="ExternalOutput").ap() for n, shape in _OUTS}
    build(nc, t)
    r = run_bass_kernel_spmd(nc, [{f"in_{n}": arrays[n] for n in _INS}], core_ids=[0]).results[0]
    y = r["out_y_t"].reshape(D_MODEL, TOK).T
    kv = r["out_kv_t"].transpose(2, 0, 1)
    order = {"cmp": [0, 1, 2, 3], "sel": [4, 6, 5, 7], "win": [8, 10, 9, 11]}
    kv = {n: kv[:, o].reshape(TOK, 2, NKV, HD) for n, o in order.items()}
    v = r["out_v_t"].transpose(2, 1, 0).reshape(P + DEC, D_GM)
    prompt = lambda n: np.ascontiguousarray(kv[n][None, None, :SEQ])
    sample = lambda n: np.ascontiguousarray(kv[n][None, SEQ:, None])
    win = np.concatenate([r["out_win"].reshape(1, DEC, PAST, 2, NKV, HD), sample("win")], 2)
    return (np.ascontiguousarray(y[None, :SEQ]), np.ascontiguousarray(y[SEQ:, None]),
            prompt("cmp"), prompt("sel"), prompt("win"), np.ascontiguousarray(v[None, None, :P]),
            sample("cmp"), sample("sel"), win, np.ascontiguousarray(v[None, P:, None]))
```

```python
from contextlib import ExitStack, contextmanager

import numpy as np

import concourse.bass as bass
from concourse import mybir

F32 = mybir.dt.float32
F32R = mybir.dt.float32r
I32 = mybir.dt.int32
ALU = mybir.AluOpType
ACT = mybir.ActivationFunctionType

P = 128
D_MODEL, SEQ, DEC, PAST, PAGE = 2048, 512, 8, 256, 128
HD, NH, NKV, REP = 128, 8, 2, 4
D_GM, GRP, D_FF = 1024, 8, 8192
CMP_LEN, STRIDE = 32, 16
N_POOL = 20
EPS = 1e-6
NEG = -1e30
NB = 32

TOK = SEQ + DEC
HT = TOK // 2
KT = D_MODEL // P
CH = 4
CK = KT // CH
CW = CK * P
MB = D_MODEL // P
NCH = SEQ // P
NPG = PAST // PAGE

U_CMP, U_KV, U_Q, U_VU, U_GATE = 0, 4, 12, 20, 36
U_PROJ = U_GATE + 2 * MB
U_OUT = U_PROJ + MB
U_FF = U_OUT + MB
FG = D_FF // D_MODEL
UNITS = U_FF + 2 * MB * FG

L_ALL = SEQ + DEC * PAST
W_ALL = L_ALL // STRIDE
KVT_W = L_ALL + CMP_LEN
W_PROMPT = (SEQ - CMP_LEN) // STRIDE + 1
W_SAMPLE = (PAST - CMP_LEN) // STRIDE + 1
W_USED = W_ALL
CJ = 8
NREL = 640
N_GATE = 3 * NH
X_SEL, X_WIN = 32, 64
X_ROWS = X_WIN + 1


def seen(i):
    return (P * (i + 1) - CMP_LEN) // STRIDE + 1


class Steps:

    def __init__(self, eng, sem):
        self.eng, self.sem, self.n, self.local = eng, sem, 0, 0

    def did(self, ins):
        ins.then_inc(self.sem, 1)
        self.local += 1
        self.n = self.n + 1
        self.eng.wait_ge(self.sem, self.n)

    @contextmanager
    def loop(self, first, last, per):
        with self.eng.Fori(first, last) as i:
            before, start = self.local, self.n
            self.n = start + (i - first) * per
            yield i
            assert self.local - before == per, (self.local - before, per)
        self.local = before + per * (last - first)
        self.n = start + per * (last - first)


def build(nc, t):
    with ExitStack() as ctx:
        def sem(name):
            return ctx.enter_context(nc.semaphore(name))

        def dram(name, shape):
            return nc.dram_tensor(name, shape, F32).ap()

        base = nc.sbuf_base + (-nc.sbuf_base) % 64
        top = [base]

        def at(name, shape, offset, dt=F32):
            assert offset % 32 == 0, name
            size = 4 * int(np.prod(shape[1:]))
            assert offset + size <= nc.sbuf_usable_end, (name, offset + size - nc.sbuf_usable_end)
            return nc.alloc_sbuf_tensor_at(name, shape, dt, offset=offset)

        def new(name, shape, dt=F32):
            o = top[0]
            size = 4 * int(np.prod(shape[1:]))
            top[0] = o + size + (-size) % 32
            return at(name, shape, o, dt)

        w_raw = new("w_raw", [P, 4, 2 * CW])
        w_hi = new("w_hi", [P, CH, CW], F32R)
        w_lo = new("w_lo", [P, CH, CW], F32R)
        a_hi = new("a_hi", [P, KT, TOK], F32R)
        a_lo = new("a_lo", [P, KT, TOK], F32R)
        ones = new("ones", [P, P])
        ident = new("ident", [P, P])
        gains = new("gains", [P, 48])
        z = new("z", [P, 2, TOK])
        na = new("na", [P, TOK])
        nr = new("nr", [P, TOK])
        nq = new("nq", [P, TOK])
        rstd = new("rstd", [P, TOK])
        small = new("small", [P, 192])

        g_mix = gains[:, 0:16]
        g_mlp = gains[:, 16:32]
        g_sgu = gains[:, 32:40]
        g_q = gains[:, 40:41]
        g_k = gains[:, 41:44]
        g_qs = gains[:, 44:45]
        mx = small[:, 0:3]
        mn = small[:, 4:7]
        ls = small[:, 8:11]
        rl = small[:, 12:15]
        k_ss = small[:, 16:24]
        k_a = small[:, 24:32]
        k_r = small[:, 32:40]
        k_q = small[:, 40:48]
        k_rs = small[:, 48:56]
        minus_half = small[:, 56:64]
        w00 = small[:, 64:72]
        v_new = small[:, 80:112].rearrange("p (s b) -> p s b", s=4)
        gs_row = small[0:NH, 112:136].rearrange("p (b j) -> p b j", b=DEC)
        vs_tmp = small[:, 136:144]
        qm = small[:, 144:160].rearrange("p (g h) -> p g h", g=NKV)

        zone = top[0]
        q_t = new("q_t", [P, NH, TOK])
        k_t = new("k_t", [P, 4, TOK])
        v_row = new("v_row", [P, 4, NCH, HD])
        kc_t = new("kc_t", [P, NKV, W_USED])
        vc_t = new("vc_t", [P, NKV, W_USED])
        vc_p = new("vc_p", [32, NKV, HD])
        gates = new("gates", [P, NCH + 1, N_GATE])
        r1 = top[0]
        kv_t = new("kv_t", [P, 4, KVT_W])
        r1_end = top[0]
        x_raw = at("x_raw", [P, KT, TOK], r1)
        u_t = at("u_t", [P, GRP, TOK], r1)
        v_t = at("v_t", [P, GRP, TOK], r1 + 4 * GRP * TOK)
        r1b = r1 + 8 * GRP * TOK
        ks_t = at("ks_t", [P, NKV, PAST + 4], r1b)
        kw_t = at("kw_t", [P, NKV, PAST + 4], r1b + 2080)
        sp = at("sp", [NH, 3, PAST + 4], r1b + 4160)
        p_s = at("p_s", [P, SEQ], r1b)
        p_w = at("p_w", [P, SEQ], r1b + 2048)
        p_c = at("p_c", [P, 32], r1b + 4096)
        assert r1b + 8192 <= r1_end
        r2 = top[0]
        w_cmp = new("w_cmp", [P, 2, CJ, HD])
        pages = new("pages", [P, 2, NPG, 512])
        r2_end = top[0]
        stage = at("stage", [P, 4, 512], r2 + 8192)
        vx_s = at("vx_s", [X_ROWS, NKV, HD], r2)
        pt_s = at("pt_s", [P, 64], r2 + 3072)
        junk = at("junk", [P, 8, HD], r2 + 4096)
        wm = at("wm", [P, GRP, P], r2)
        b_bc = at("b_bc", [P, GRP, P], r2 + 4096)
        pt_sel = at("pt_sel", [P, NCH, P], r2 + 8192)
        pt_win = at("pt_win", [P, NCH, P], r2 + 10240)
        pt_cmp = at("pt_cmp", [32, P], r2 + 12288)
        r3 = top[0]
        sq = new("sq", [P, TOK])
        acc_v = new("acc_v", [P, TOK])
        wg_parts = at("wg_parts", [P, KT, 2 * N_GATE], r2 + 8192, F32R)
        wg_raw = at("wg_raw", [P, KT, N_GATE], r2 + 8192 + 3072)
        gz = at("gz", [P, NCH + 1, N_GATE], r2 + 8192 + 4608)
        g_t = at("g_t", [2 * N_GATE, TOK], r2 + 8192 + 5120)
        v_g = at("v_g", [P, TOK], r3)
        vr_g = new("vr_g", [P, NCH, P])
        toep = new("toep", [P, SEQ])
        q_h = new("q_h", [P, SEQ])
        oh = at("oh", [NB + 1, NREL], r2)
        rb = at("rb", [NB + 1, NH], r2 + 4 * NREL)
        rel_row = at("rel_row", [NH, NREL], r2 + 4 * NREL + 64)
        vx_t = new("vx_t", [P, NKV, X_ROWS])
        rel_s = new("rel_s", [NH, PAST + 4])
        table = new("table", [1, DEC * NPG], I32)
        b_hi = at("b_hi", [P, KT, TOK], zone, F32R)
        b_lo = at("b_lo", [P, KT, TOK], zone + 4 * KT * TOK, F32R)
        r4 = zone + 8 * KT * TOK
        x2 = at("x2", [P, MB, TOK], r4)
        acc_x = at("acc_x", [P, TOK], r4 + 4 * MB * TOK)
        g_in = at("g_in", [P, 2, 2, TOK], r4)

        ca, cb, cm = na, nr, nq

        mm = nc.alloc_psum_tensor("mm", [P, 4, 512], F32)
        aux = nc.alloc_psum_tensor("aux", [P, 4, 512], F32)

        rel_d = dram("rel_d", [NH, NREL])
        toep_d = dram("toep_d", [NH, P, SEQ])
        gate_d = dram("gate_d", [DEC, N_GATE])
        merge_d = dram("merge_d", [2 * MB, P, TOK])

        raw_loaded = [sem(f"raw_loaded{n}") for n in range(4)]
        hi_split = sem("hi_split")
        lo_split = sem("lo_split")
        chunk_done = sem("chunk_done")
        mm_read = sem("mm_read")
        a_ready = sem("a_ready")
        b_ready = sem("b_ready")
        act_hi = sem("act_hi")
        act_src = sem("act_src")
        x_loaded = [sem(f"x_loaded{n}") for n in range(CH)]
        gains_loaded = sem("gains_loaded")
        consts_loaded = sem("consts_loaded")
        consts_set = sem("consts_set")
        cell_set = sem("cell_set")
        x_squared = sem("x_squared")
        x_odd_squared = sem("x_odd_squared")
        x_summed = sem("x_summed")
        x_added = sem("x_added")
        squared = sem("squared")
        summed = sem("summed")
        norm_base = sem("norm_base")
        norm_guess = sem("norm_guess")
        z_made = mm_read
        z_read = sem("z_read")
        z_stored = [sem(f"z_stored{n}") for n in range(2)]
        z_copied = sem("z_copied")
        pos_loaded = sem("pos_loaded")
        v_turned = sem("v_turned")
        v_row_made = sem("v_row_made")
        rel_made, rel_done = sem("rel_made"), sem("rel_done")
        rel_stored, toep_stored = sem("rel_stored"), sem("toep_stored")
        toep_loaded = sem("toep_loaded")
        table_loaded = sem("table_loaded")
        page_loaded = [sem(f"page_loaded{n}") for n in range(2)]
        page_turned = sem("page_turned")
        page_read = sem("page_read")
        cmp_loaded = [sem(f"cmp_loaded{n}") for n in range(2)]
        cmp_used = sem("cmp_used")
        kc_made, vc_made = sem("kc_made"), sem("vc_made")
        vcp_turned, vcp_made = sem("vcp_turned"), sem("vcp_made")
        wg_loaded, wg_hi_made, wg_split = sem("wg_loaded"), sem("wg_hi_made"), sem("wg_split")
        gates_summed, g_t_made, gates_turned, gz_made, gz_tanh, gates_made = (
            sem("gates_summed"), sem("g_t_made"), sem("gates_turned"), sem("gz_made"), sem("gz_tanh"),
            sem("gates_made"))
        gate_stored, gate_loaded = sem("gate_stored"), sem("gate_loaded")
        keys_loaded, values_loaded = sem("keys_loaded"), sem("values_loaded")
        smp_static = sem("smp_static")
        smp_vturned, smp_vmade = sem("smp_vturned"), sem("smp_vmade")
        smp_base, smp_guess = sem("smp_base"), sem("smp_guess")
        smp_keys = sem("smp_keys")
        smp_kturned, smp_ks, smp_kw = sem("smp_kturned"), sem("smp_ks"), sem("smp_kw")
        smp_scored, smp_max, smp_exp = sem("smp_scored"), sem("smp_max"), sem("smp_exp")
        smp_probs, smp_pturned, smp_pmade = sem("smp_probs"), sem("smp_pturned"), sem("smp_pmade")
        smp_out, smp_read = sem("smp_out"), sem("smp_read")
        v_acc = sem("v_acc")
        gm_loaded, w_masked, v_normed = sem("gm_loaded"), sem("w_masked"), sem("v_normed")
        v_stored, win_stored = sem("v_stored"), sem("win_stored")
        q_copied, v_copied = sem("q_copied"), sem("v_copied")
        scored, s_max, s_exp, probs = sem("scored"), sem("s_max"), sem("s_exp"), sem("probs")
        p_turned, pt_sel_made, pt_made = sem("p_turned"), sem("pt_sel_made"), sem("pt_made")
        aux3_made, aux3_read = sem("aux3_made"), sem("aux3_read")
        g_tanh = sem("g_tanh")
        g_stored = [sem(f"g_stored{n}") for n in range(2)]
        g_loaded = [sem(f"g_loaded{n}") for n in range(2)]
        x_in_loaded = [sem(f"x_in_loaded{n}") for n in range(2)]
        x2_squared = sem("x2_squared")
        y_stored = sem("y_stored")
        dve_step, act_step, pool_step = sem("dve_step"), sem("act_step"), sem("pool_step")

        def carry(eng):
            if eng is nc.vector:
                eng.memset(small[:, 170:171], 0.0)
            else:
                eng.tensor_tensor(small[:, 171:172], ones[:, 0:1], ones[:, 0:1], ALU.mult)

        def num(u):
            return 2 * u[0] + u[1]

        def after(u):
            return (u[0], 1) if u[1] == 0 else (u[0] + 1, 0)

        def straight(n):
            return (n // 2, n % 2)

        def raw(u, c):
            return w_raw[:, 2 * u[1] + c // 2, (c % 2) * CW:(c % 2 + 1) * CW]

        def pair(v):
            return mm[:, 2 * v:2 * v + 2, 0:HT]

        def halves(ap):
            return ap.rearrange("p (a b) -> p a b", a=2)

        def more(u):
            return not (type(u[0]) is int and num(u) == UNITS - 1)

        def ff_loops(eng, up, down):
            def group(f, first, pairs):
                with eng.Fori(first, MB // 2) as i:
                    for p in range(2):
                        up(f, i, p)
                with eng.Fori(0, pairs) as i:
                    for p in range(2):
                        down(f, i, p)

            for p in range(2):
                up(0, 0, p)
            group(0, 1, MB // 2)
            with eng.Fori(1, FG - 1) as f:
                group(f, 0, MB // 2)
            group(FG - 1, 0, MB // 2 - 1)
            for p in range(2):
                down(FG - 1, MB // 2 - 1, p)

        GATE_OF = (1, 2, 0)
        CONSTS = 16 * 3
        N_NORM_K, N_NORM_C, N_NORM_V, N_NORM_X2 = 1, 9, 14, 15

        def n_norm_q(h):
            return 5 + h + (1 if h >= NH // 2 else 0)


        block = ctx.enter_context(nc.Block())

        @block.sync
        def _(sp_):
            for c in range(CH):
                sp_.dma_start(x_raw[:, CK * c:CK * (c + 1), :],
                              t["x_t"][CK * c:CK * (c + 1)].rearrange("k p n -> p k n")
                              ).then_inc(x_loaded[c], 16)
                sp_.dma_start(w_raw[:, c, :], t["w"][c // 2, :, (c % 2) * 2 * CW:(c % 2 + 1) * 2 * CW]
                              ).then_inc(raw_loaded[c], 16)
            with sp_.Fori(1, UNITS // 2) as i:
                for n in range(4):
                    sp_.wait_ge(lo_split, 8 * i - 8 + 2 * n + 2)
                    sp_.dma_start(w_raw[:, n, :], t["w"][2 * i + n // 2, :, (n % 2) * 2 * CW:(n % 2 + 1) * 2 * CW]
                                  ).then_inc(raw_loaded[n], 16)
            with sp_.Fori(0, MB) as m:
                sp_.wait_ge(mm_read, UNITS + m + 1)
                sp_.dma_start(t["y_t"][m], x2[:, m, :]).then_inc(y_stored, 16)
            sp_.wait_ge(y_stored, 16 * MB)

        @block.tensor
        def _(pe):
            def unit(u, ah, al, ready, need, hooks=(), before=None, projections=False,
                     first_hook=None):
                n = num(u)
                if first_hook:
                    first_hook()
                for c in range(CH):
                    pe.wait_ge(lo_split, 4 * n + c + 1)
                    pe.wait_ge(ready, need(c))
                    if projections:
                        v = c // 2
                        if c % 2 == 0:
                            pe.wait_ge(mm_read, 2 * n - U_PROJ - 1 + v)
                    else:
                        v = u[1]
                        if c == 0 and not (type(n) is int and n < 2):
                            pe.wait_ge(mm_read, before(u) if before else n - 1)
                    first = c % 2 == 0 if projections else c == 0
                    final = c % 2 == 1 if projections else c == CH - 1
                    for k in range(CK):
                        kt = CK * c + k
                        wh, wl = w_hi[:, c, k * P:(k + 1) * P], w_lo[:, c, k * P:(k + 1) * P]
                        for w, a, part in ((wh, ah, 0), (wh, al, 1), (wl, ah, 2)):
                            for h in range(2):
                                last = pe.matmul(mm[:, 2 * v + h, 0:HT], w, a[:, kt, h * HT:(h + 1) * HT],
                                                 start=first and k == 0 and part == 0,
                                                 stop=final and k == CK - 1 and part == 2)
                    last.then_inc(chunk_done, 1)
                    if c < len(hooks) and hooks[c]:
                        hooks[c]()

            def norm_sum(n, src=None, made=None):
                src = sq if src is None else src
                pe.wait_ge(*(made or (squared, n)))
                pe.wait_ge(norm_base, n)
                for h in range(2):
                    last = pe.matmul(aux[:, h, 0:HT], ones[:, :], src[:, h * HT:(h + 1) * HT],
                                     start=True, stop=True)
                last.then_inc(summed, 1)

            def turn_v(j):
                def go():
                    pe.wait_ge(z_made, U_KV + 2 * j + 2)
                    pe.wait_ge(v_row_made, j)
                    pe.wait_ge(page_read, 4 * j + 4)
                    for k in range(NCH):
                        last = pe.transpose(aux[:, 2, k * P:(k + 1) * P], z[:, 1, k * P:(k + 1) * P], ident[:, :])
                    last.then_inc(v_turned, 1)
                return go

            def turn_pages(b):
                def go():
                    p = b % 2
                    pe.wait_ge(page_loaded[p], 16 * NPG * (b // 2 + 1))
                    pe.wait_ge(v_row_made, b // 2)
                    pe.wait_ge(page_read, NPG * b)
                    for g in range(NPG):
                        for q in range(4):
                            last = pe.transpose(aux[:, 2 + g, q * P:(q + 1) * P],
                                                pages[:, p, g, q * P:(q + 1) * P], ident[:, :])
                        last.then_inc(page_turned, 1)
                return go

            x_need = lambda c: CK * (c + 1)

            def rel_row_sums():
                pe.wait_ge(consts_loaded, CONSTS)
                pe.matmul(aux[0:NH, 2, 0:512], rb[:, :], oh[:, 0:512], start=True, stop=True)
                pe.matmul(aux[0:NH, 3, 0:NREL - 512], rb[:, :], oh[:, 512:NREL], start=True, stop=True
                          ).then_inc(rel_made, 1)

            def x_sum(c):
                def go():
                    pe.wait_ge(consts_set, 1)
                    pe.wait_ge(x_odd_squared, CK // 2 * (c + 1))
                    for n in range(CK // 2):
                        for h in range(2):
                            last = pe.matmul(aux[:, h, 0:HT], ones[:, :], (z[:, 1, :], sq[:, :])[n][:, h * HT:(h + 1) * HT],
                                             start=c == 0 and n == 0, stop=False)
                    last.then_inc(x_summed, 1)
                    if c == CH - 1:
                        pe.wait_ge(x_added, KT // 2)
                        for h in range(2):
                            last = pe.matmul(aux[:, h, 0:HT], ones[:, :], acc_v[:, h * HT:(h + 1) * HT],
                                             start=False, stop=True)
                        last.then_inc(summed, 1)
                return go

            unit(straight(0), a_hi, a_lo, a_ready, x_need, [x_sum(c) for c in range(CH)])
            unit(straight(1), a_hi, a_lo, a_ready, x_need, [None, rel_row_sums])
            for n in range(2, U_KV):
                unit(straight(n), a_hi, a_lo, a_ready, x_need)
            pe.wait_ge(rel_done, 1)
            for j in range(4):
                unit(straight(U_KV + 2 * j), a_hi, a_lo, a_ready, x_need,
                     [None, turn_v(j - 1) if j else None, turn_pages(2 * j)])
                unit(straight(U_KV + 2 * j + 1), a_hi, a_lo, a_ready, x_need,
                     [None, lambda: norm_sum(N_NORM_K + j), turn_pages(2 * j + 1)])

            def compress(n):
                def go():
                    kv, part = divmod(n, CMP_LEN // CJ)
                    if n == 0:
                        pe.wait_ge(page_read, NPG * DEC)
                        pe.wait_ge(z_copied, U_KV)
                        pe.wait_ge(pos_loaded, 64)
                        pe.wait_ge(g_t_made, 1)
                    if part == 0 and kv == 1:
                        pe.wait_ge(gz_made, 1)
                    pe.wait_ge(cmp_loaded[n % 2], 16 * (n // 2 + 1))
                    for jj in range(CJ):
                        j = part * CJ + jj
                        last = pe.matmul(aux[:, 2 + kv, 0:NKV * (W_ALL + 1)], w_cmp[:, n % 2, jj, :],
                                         kv_t[:, NKV * kv:NKV * (kv + 1), j:j + STRIDE * W_ALL + 1:STRIDE],
                                         start=j == 0, stop=j == CMP_LEN - 1)
                    last.then_inc(cmp_used, 1)
                return go

            def gate_sums():
                pe.wait_ge(wg_split, 1)
                pe.wait_ge(page_read, NPG * DEC)
                pe.wait_ge(v_row_made, 4)
                for kt in range(KT):
                    for part, a in enumerate((a_hi, a_lo)):
                        for h in range(2):
                            last = pe.matmul(aux[0:2 * N_GATE, 2 + h, 0:HT], wg_parts[:, kt, :],
                                             a[:, kt, h * HT:(h + 1) * HT],
                                             start=kt == 0 and part == 0, stop=kt == KT - 1 and part == 1)
                last.then_inc(gates_summed, 1)

            def turn_gates():
                pe.wait_ge(g_t_made, 1)
                for tb in range(NCH + 1):
                    o = min(P * tb, TOK - P)
                    last = pe.transpose(aux[:, 3, 2 * N_GATE * tb:2 * N_GATE * (tb + 1)], g_t[:, o:o + P],
                                        ident[0:2 * N_GATE, 0:2 * N_GATE])
                last.then_inc(gates_turned, 1)

            def key_windows_sum():
                pe.wait_ge(squared, N_NORM_C)
                pe.wait_ge(norm_base, N_NORM_C)
                pe.matmul(aux[:, 0, 0:NKV * W_USED], ones[:, :], sq[:, 0:NKV * W_USED], start=True, stop=True
                          ).then_inc(summed, 1)

            def turn_windows():
                pe.wait_ge(vc_made, 1)
                for g in range(NKV):
                    last = pe.transpose(aux[0:W_PROMPT, 2, g * P:(g + 1) * P], vc_t[:, g, 0:W_PROMPT], ident[:, :])
                last.then_inc(vcp_turned, 1)

            for h in range(NH):
                unit(straight(U_Q + h), a_hi, a_lo, a_ready, x_need,
                     [None, turn_v(3) if h == 0 else (lambda: norm_sum(n_norm_q(h - 1))),
                      (lambda: (turn_gates(), compress(0)())) if h == 1 else None,
                      (gate_sums if h == 0 else
                       (lambda: (key_windows_sum(), compress(h)())) if h == NH // 2 else compress(h))])

            def smp_values(b):
                def go():
                    pe.wait_ge(smp_max, b)
                    pe.wait_ge(vcp_made, 1)
                    pe.wait_ge(smp_static, b + 1)
                    for g in range(NKV):
                        last = pe.transpose(aux[0:X_ROWS, 3, g * P:(g + 1) * P], vx_t[:, g, :], ident[:, :])
                    last.then_inc(smp_vturned, 1)
                return go

            def smp_turn_keys(b):
                def go():
                    pe.wait_ge(smp_keys, b + 1)
                    pe.wait_ge(smp_pmade, b)
                    pe.wait_ge(smp_read, b)
                    for br in range(2):
                        for g in range(NKV):
                            for k in range(NPG):
                                last = pe.transpose(aux[:, br, (2 * g + k) * P:(2 * g + k + 1) * P],
                                                    stage[:, 2 * br + k, g * P:(g + 1) * P], ident[:, :])
                        last.then_inc(smp_kturned, 1)
                return go

            def smp_scores(b):
                def go():
                    pe.wait_ge(smp_ks, b + 1)
                    pe.wait_ge(smp_kw, b + 1)
                    pe.wait_ge(smp_vmade, b + 1)
                    for g in range(NKV):
                        pe.matmul(aux[0:NH, 2, 0:PAST + 1], qm[:, g, :], ks_t[:, g, 0:PAST + 1],
                                  start=g == 0, stop=g == NKV - 1)
                    for g in range(NKV):
                        pe.matmul(aux[0:NH, 2, 300:300 + W_SAMPLE], qm[:, g, :],
                                  kc_t[:, g, bass.ds(SEQ // STRIDE + b * (PAST // STRIDE), W_SAMPLE)],
                                  start=g == 0, stop=g == NKV - 1)
                    for g in range(NKV):
                        last = pe.matmul(aux[0:NH, 3, 0:PAST + 1], qm[:, g, :], kw_t[:, g, 0:PAST + 1],
                                         start=g == 0, stop=g == NKV - 1)
                    last.then_inc(smp_scored, 1)
                return go

            def smp_turn_probs(b):
                def go():
                    pe.wait_ge(smp_probs, b + 1)
                    i8 = ident[0:NH, 0:NH]
                    for br in range(2):
                        for k in range(NPG):
                            pe.matmul(aux[:, 0, (2 * br + k) * NH:(2 * br + k + 1) * NH],
                                      sp[:, br, k * P:(k + 1) * P], i8, start=True, stop=True)
                    pe.transpose(aux[0:X_ROWS, 0, 4 * NH:5 * NH], sp[:, 2, 0:X_ROWS], i8).then_inc(smp_pturned, 1)
                return go

            def smp_attend(b):
                def go():
                    pe.wait_ge(smp_pmade, b + 1)
                    pe.wait_ge(values_loaded, 48 * b + 48)
                    for g in range(NKV):
                        o = aux[:, 1, REP * g:REP * (g + 1)]
                        cut = lambda n, rows: pt_s[0:rows, n * NH + REP * g:n * NH + REP * (g + 1)]
                        vg = slice((NKV + g) * HD, (NKV + g + 1) * HD)
                        for n in range(4):
                            pe.matmul(o, stage[:, n, vg], cut(n, P), start=n == 0, stop=False)
                        last = pe.matmul(o, vx_s[:, g, :], cut(4, X_ROWS), start=False, stop=True)
                    last.then_inc(smp_out, 1)
                return go

            def smp_pair(b, hooks):
                unit((U_VU // 2 + b, 0), a_hi, a_lo, a_ready, x_need, hooks)
                unit((U_VU // 2 + b, 1), a_hi, a_lo, a_ready, x_need,
                     [smp_scores(b), None, smp_turn_probs(b), smp_attend(b)])

            smp_pair(0, [lambda: norm_sum(n_norm_q(NH - 1)), turn_windows,
                         lambda: (smp_values(0)(), smp_turn_keys(0)())])
            with pe.Fori(1, DEC) as b:
                smp_pair(b, [smp_values(b), None, smp_turn_keys(b)])
            pe.wait_ge(smp_read, DEC)
            norm_sum(N_NORM_V, acc_v, (v_acc, GRP))
            pe.wait_ge(norm_base, N_NORM_V + 1)

            def scores(g, h, i):
                def go():
                    a = NCH * h + i
                    pe.wait_ge(q_copied, h + 1)
                    pe.wait_ge(pt_sel_made, a)
                    pe.wait_ge(pt_made, a)
                    qi = q_h[:, P * i:P * (i + 1)]
                    pe.matmul(aux[:, 0, 0:P * (i + 1)], qi, k_t[:, g, 0:P * (i + 1)], start=True, stop=True)
                    pe.matmul(aux[:, 1, 0:P * (i + 1)], qi, k_t[:, 2 + g, 0:P * (i + 1)], start=True, stop=True)
                    pe.matmul(aux[:, 2, 0:seen(i)], qi, kc_t[:, g, 0:seen(i)], start=True, stop=True
                              ).then_inc(scored, 1)
                return go

            def turn_probs(g, h, i):
                def go():
                    pe.wait_ge(probs, NCH * h + i + 1)
                    for n, src in enumerate((p_s, p_w)):
                        for k in range(i + 1):
                            pe.transpose(aux[:, n, k * P:(k + 1) * P], src[:, k * P:(k + 1) * P], ident[:, :])
                    pe.transpose(aux[0:seen(i), 2, 0:P], p_c[:, 0:seen(i)], ident[:, :]).then_inc(p_turned, 1)
                return go

            def attend(g, h, i):
                def go():
                    pe.wait_ge(pt_sel_made, NCH * h + i + 1)
                    pe.wait_ge(pt_made, NCH * h + i + 1)
                    pe.wait_ge(aux3_read, 6 * h + (0, 1, 3, 5)[i])
                    o = aux[:, 3, 0:P]
                    for k in range(i + 1):
                        pe.matmul(o, v_row[:, g, k, :], pt_sel[:, k, :], start=k == 0, stop=False)
                    for k in range(i + 1):
                        pe.matmul(o, v_row[:, 2 + g, k, :], pt_win[:, k, :], start=False, stop=False)
                    pe.matmul(o, vc_p[0:seen(i), g, :], pt_cmp[0:seen(i), :], start=False, stop=True
                              ).then_inc(aux3_made, 1)
                return go

            def turn_group(h):
                def go():
                    pe.wait_ge(v_copied, h + 1)
                    pe.wait_ge(aux3_read, 6 * h + 2)
                    for k in range(NCH):
                        last = pe.transpose(aux[:, 3, k * P:(k + 1) * P], v_g[:, k * P:(k + 1) * P], ident[:, :])
                    last.then_inc(aux3_made, 1)
                return go

            def mix_group(h):
                def go():
                    pe.wait_ge(w_masked, 1)
                    pe.wait_ge(aux3_read, 6 * h + 4)
                    for k in range(NCH):
                        last = pe.matmul(aux[:, 3, k * P:(k + 1) * P], vr_g[:, k, :], wm[:, h, :],
                                         start=True, stop=True)
                    last.then_inc(aux3_made, 1)
                return go

            for g in range(NKV):
                with pe.Fori(REP * g, REP * (g + 1)) as h:
                    for i in range(NCH):
                        u = (U_GATE // 2 + 2 * h + i // 2, i % 2)
                        unit(u, a_hi, a_lo, a_ready, x_need,
                             [None, (None, None, turn_group(h), mix_group(h))[i],
                              turn_probs(g, h, i), attend(g, h, i)], first_hook=scores(g, h, i))

            with pe.Fori(0, MB // 2) as i:
                for p in range(2):
                    unit((U_PROJ // 2 + i, p), a_hi, a_lo, a_ready, lambda c: KT + CK * (c + 1),
                         projections=True)
            late = lambda u: num(u) + MB - 1
            with pe.Fori(0, MB // 2) as i:
                for p in range(2):
                    unit((U_OUT // 2 + i, p), b_hi, b_lo, b_ready, x_need, before=late)

            def up(f, i, p):
                unit((U_FF // 2 + MB * f + i, p), a_hi, a_lo, a_ready, lambda c: 2 * KT + CK * (c + 1), before=late)

            def down(f, i, p):
                unit((U_FF // 2 + MB // 2 + MB * f + i, p), b_hi, b_lo, b_ready,
                     lambda c: KT + KT * f + CK * (c + 1), before=late)

            up(0, 0, 0)
            norm_sum(N_NORM_X2, acc_x, (x2_squared, MB))
            up(0, 0, 1)
            for first, groups in ((1, (0, 1)), (0, (1, FG))):
                with pe.Fori(*groups) as f:
                    with pe.Fori(first, MB // 2) as i:
                        for p in range(2):
                            up(f, i, p)
                    with pe.Fori(0, MB // 2) as i:
                        for p in range(2):
                            down(f, i, p)

        @block.scalar
        def _(act):
            steps = Steps(act, act_step)
            run = act.activation

            def hi(u, c):
                n = num(u)
                if c % 2 == 0:
                    act.wait_ge(raw_loaded[2 * u[1] + c // 2], 16 * (u[0] + 1))
                if not (type(n) is int and n == 0):
                    act.wait_ge(chunk_done, 4 * n - 3 + c)
                run(w_hi[:, c, :], raw(u, c), ACT.Copy).then_inc(hi_split, 1)

            def beside(u, jobs=(), first=None):
                if first:
                    first()
                for c in range(CH):
                    hi(after(u), c)
                    if c < len(jobs) and jobs[c]:
                        jobs[c]()

            def guess(n, w=TOK):
                act.wait_ge(norm_base, n + 1)
                steps.did(run(nr[:, 0:w], na[:, 0:w], ACT.Ln))
                steps.did(run(nr[:, 0:w], nr[:, 0:w], ACT.Exp, scale=-0.5))
                run(nq[:, 0:w], nr[:, 0:w], ACT.Square).then_inc(norm_guess, 1)

            act.dma_start(gains[:, 0:44], t["gains"]).then_inc(gains_loaded, 16)
            act.wait_ge(cell_set, 1)
            run(small[:, 172:173], small[:, 173:174], ACT.Copy)
            act.wait_ge(gains_loaded, 16)
            for c in range(CH):
                hi(straight(0), c)
                act.wait_ge(x_loaded[c], 16)
                for kt in range(CK * c, CK * (c + 1)):
                    run(a_hi[:, kt, :], x_raw[:, kt, :], ACT.Copy, scale=g_mix[:, kt:kt + 1]).then_inc(act_hi, 1)
                    if kt % 2 == 0:
                        act.wait_ge(x_added, kt // 2)
                        run(z[:, 0, :], x_raw[:, kt, :], ACT.Square).then_inc(x_squared, 1)

            def store(n):
                act.wait_ge(z_made, n + 1)
                act.dma_start(t["kv_t"][n], z[:, n % 2, :]).then_inc(z_stored[n % 2], 16)

            def square(n, u, src):
                act.wait_ge(z_made, num(u) + 1)
                act.wait_ge(summed, n)
                run(sq[:, :], src, ACT.Square).then_inc(squared, 1)

            def v_rows(j):
                act.wait_ge(v_turned, j + 1)
                run(v_row[:, j, :, :], aux[:, 2, :].rearrange("p (k d) -> p k d", k=NCH), ACT.Copy
                    ).then_inc(v_row_made, 1)

            for n in range(U_KV):
                beside(straight(n))
                if n == 0:
                    guess(0)
                store(n)
            for j in range(4):
                beside(straight(U_KV + 2 * j), [None, (lambda: v_rows(j - 1)) if j else None])
                store(U_KV + 2 * j)
                square(N_NORM_K + j, straight(U_KV + 2 * j), z[:, 0, :])
                beside(straight(U_KV + 2 * j + 1), [None, lambda: guess(N_NORM_K + j)])
                store(U_KV + 2 * j + 1)

            def wg_hi():
                act.wait_ge(wg_loaded, 16)
                run(wg_parts[:, :, 0:N_GATE], wg_raw[:, :, :], ACT.Copy).then_inc(wg_hi_made, 1)

            def gates_tanh():
                act.wait_ge(gz_made, 1)
                run(gz[:, :, :], gz[:, :, :], ACT.Tanh, scale=0.5).then_inc(gz_tanh, 1)

            def square_windows():
                act.wait_ge(kc_made, 1)
                act.wait_ge(summed, N_NORM_C)
                run(sq[:, 0:NKV * W_USED], kc_t[:, :, :].rearrange("p g w -> p (g w)"), ACT.Square
                    ).then_inc(squared, 1)

            for h in range(NH):
                n = U_Q + h
                jobs = [None, (lambda: guess(n_norm_q(h - 1))) if h else (lambda: (wg_hi(), v_rows(3))), None, None]
                if h == 2:
                    jobs[0] = gates_tanh
                if h == NH // 2:
                    jobs[2:] = [square_windows, lambda: guess(N_NORM_C, NKV * W_USED)]
                beside(straight(n), jobs)
                square(n_norm_q(h), straight(n), z[:, n % 2, :])

            def smp_exps(b):
                act.wait_ge(smp_max, b + 1)
                for n, w in enumerate((PAST + 1, PAST + 1, W_SAMPLE)):
                    last = run(sp[:, n, 0:w], sp[:, n, 0:w], ACT.Exp, bias=mn[0:NH, n:n + 1],
                               accum_out=ls[0:NH, GATE_OF[n]:GATE_OF[n] + 1])
                last.then_inc(smp_exp, 1)

            def smp_ks_in(b):
                act.wait_ge(smp_kturned, 2 * b + 1)
                run(ks_t[:, :, 0:PAST], aux[:, 0, :].rearrange("p (g k) -> p g k", g=NKV), ACT.Copy,
                    scale=g_k[:, 1:2]).then_inc(smp_ks, 1)

            def gelu(b, p, dst):
                act.wait_ge(z_made, U_VU + 2 * b + p + 1)
                run(dst[:, b, :], z[:, p, :], ACT.Gelu_apprx_tanh).then_inc(z_read, 1)

            def load_bias(h):
                act.wait_ge(s_max, NCH * h)
                act.dma_start(toep[:, :], toep_d[h]).then_inc(toep_loaded, 16)

            def copy_queries(h):
                act.wait_ge(scored, NCH * h)
                run(q_h[:, :], q_t[:, h, 0:SEQ], ACT.Copy).then_inc(q_copied, 1)

            def smp_pair(b):
                gelu(b, 0, v_t)
                beside((U_VU // 2 + b, 1), [lambda: smp_exps(b)])
                gelu(b, 1, u_t)

            beside((U_VU // 2, 0), [lambda: guess(n_norm_q(NH - 1)), None, lambda: smp_ks_in(0)])
            smp_pair(0)
            with act.Fori(1, DEC - 1) as b:
                beside((U_VU // 2 + b, 0), [None, None, lambda: smp_ks_in(b)])
                smp_pair(b)
            act.wait_ge(toep_stored, 16)
            load_bias(0)
            beside((U_VU // 2 + DEC - 1, 0), [None, lambda: copy_queries(0), lambda: smp_ks_in(DEC - 1)])
            smp_pair(DEC - 1)

            def exps(a, i):
                act.wait_ge(s_max, a + 1)
                for n, (x, w) in enumerate(((p_s, P * (i + 1)), (p_w, P * (i + 1)), (p_c, seen(i)))):
                    last = run(x[:, 0:w], x[:, 0:w], ACT.Exp, bias=mn[:, n:n + 1],
                               accum_out=ls[:, GATE_OF[n]:GATE_OF[n] + 1])
                last.then_inc(s_exp, 1)

            def probs_out(a, i):
                act.wait_ge(p_turned, a + 1)
                run(pt_sel[:, 0:i + 1, :], aux[:, 0, 0:P * (i + 1)].rearrange("p (k q) -> p k q", k=i + 1),
                    ACT.Copy).then_inc(pt_sel_made, 1)

            def copy_values(h):
                act.wait_ge(v_normed, 1)
                act.wait_ge(aux3_read, 6 * h)
                run(v_g[:, :], v_t[:, h, :], ACT.Copy).then_inc(v_copied, 1)

            def mixed(kt):
                act.wait_ge(chunk_done, CH * (U_PROJ - 1) + kt // CK + 1)
                src = u_t[:, kt, :] if kt < GRP else q_t[:, kt - GRP, :]
                run(a_hi[:, kt, :], src, ACT.Copy).then_inc(act_hi, 1)

            def mixed_chunk(c):
                for kt in range(CK * c, CK * (c + 1)):
                    mixed(kt)

            def head(h, ahead, extra=None):
                for i in range(NCH):
                    a = NCH * h + i
                    u = (U_GATE // 2 + 2 * h + i // 2, i % 2)
                    jobs = [extra if i == 0 else None, None, lambda: probs_out(a, i), None]
                    if i == 2:
                        jobs[0] = lambda: copy_values(h)
                    if i == NCH - 1 and ahead:
                        jobs[:2] = [lambda: load_bias(h + 1), lambda: copy_queries(h + 1)]
                    if i == NCH - 1 and not ahead:
                        jobs = [lambda: mixed_chunk(0), None, jobs[2], None]
                    beside(u, jobs, first=lambda: exps(a, i))
                    act.wait_ge(z_made, num(u) + 1)
                    run(z[:, i % 2, :], z[:, i % 2, :], ACT.Tanh, scale=0.5).then_inc(g_tanh, 1)

            head(0, True, lambda: guess(N_NORM_V))
            with act.Fori(1, REP) as h:
                head(h, True)
            with act.Fori(REP, NH - 1) as h:
                head(h, True)
            head(NH - 1, False)
            act.wait_ge(aux3_read, 6 * NH)
            for c in range(1, CH):
                mixed_chunk(c)

            def split_hi(count, dst, src, func=ACT.Copy):
                act.wait_ge(act_src, count)
                run(dst, src, func).then_inc(act_hi, 1)

            with act.Fori(0, MB // 2) as i:
                for p in range(2):
                    beside((U_PROJ // 2 + i, p))
                    split_hi(1 + 2 * i + p, b_hi[:, 2 * i + p, :], cm[:, :])
            with act.Fori(0, MB // 2) as i:
                for p in range(2):
                    beside((U_OUT // 2 + i, p))
                    split_hi(1 + MB + 2 * i + p, a_hi[:, 2 * i + p, :], na[:, :])

            def up(f, i, p):
                beside((U_FF // 2 + MB * f + i, p))
                if type(f) is int and f == 0 and type(i) is int:
                    guess(N_NORM_X2) if p == 0 else None
                split_hi(1 + 2 * MB + MB * f + 2 * i + p, b_hi[:, 2 * i + p, :], z[:, p, :], ACT.Square)

            def down(f, i, p):
                u = (U_FF // 2 + MB // 2 + MB * f + i, p)
                if more(u):
                    beside(u)

            ff_loops(act, up, down)
            for p in range(2):
                act.wait_ge(z_stored[p], 16 * (U_Q // 2))

        @block.vector
        def _(dve):
            steps = Steps(dve, dve_step)

            def lo(u, c):
                n = num(u)
                dve.wait_ge(hi_split, 4 * n + c + 1)
                dve.tensor_tensor(w_lo[:, c, :], raw(u, c), w_hi[:, c, :].bitcast(F32), ALU.subtract
                                  ).then_inc(lo_split, 1)

            def beside(u, jobs=(), first=None):
                if first:
                    first()
                for c in range(CH):
                    lo(after(u), c)
                    if c < len(jobs) and jobs[c]:
                        jobs[c]()

            def mean(n, count, w=None):
                dve.wait_ge(summed, n + 1)
                dst, src = (halves(na[:, :]), aux[:, 0:2, 0:HT]) if w is None else (na[:, 0:w], aux[:, 0, 0:w])
                dve.tensor_scalar(dst, src, 1.0 / count, EPS, ALU.mult, ALU.add).then_inc(norm_base, 1)

            def newton(n, dst, w=TOK):
                dve.wait_ge(norm_guess, n + 1)
                steps.did(dve.scalar_tensor_tensor(nq[:, 0:w], nq[:, 0:w], -0.5, na[:, 0:w], ALU.mult, ALU.mult))
                steps.did(dve.scalar_tensor_tensor(dst, nq[:, 0:w], 1.5, nr[:, 0:w], ALU.add, ALU.mult))

            def scale_out(u, dst):
                dve.wait_ge(chunk_done, CH * num(u) + CH)
                dve.tensor_tensor(halves(dst), pair(u[1]), halves(rstd[:, :]), ALU.mult).then_inc(mm_read, 1)

            def rel_rows():
                dve.wait_ge(rel_made, 1)
                dve.tensor_copy(rel_row[:, 0:512], aux[0:NH, 2, 0:512])
                steps.did(dve.tensor_copy(rel_row[:, 512:NREL], aux[0:NH, 3, 0:NREL - 512]))
                o = SEQ - 1 - PAST
                dve.tensor_copy(rel_s[:, 0:PAST + 1], rel_row[:, o:o + PAST + 1]).then_inc(rel_done, 1)

            dve.wait_ge(gains_loaded, 16)
            steps.did(dve.tensor_scalar(g_qs, g_q, HD ** -0.5, None, ALU.mult))
            for c in range(CH):
                lo(straight(0), c)
                for kt in range(CK * c, CK * (c + 1)):
                    dve.wait_ge(act_hi, kt + 1)
                    dve.scalar_tensor_tensor(a_lo[:, kt, :], x_raw[:, kt, :], g_mix[:, kt:kt + 1],
                                             a_hi[:, kt, :].bitcast(F32), ALU.mult, ALU.subtract).then_inc(a_ready, 1)
                dve.wait_ge(x_summed, c)
                for n, kt in enumerate(range(CK * c + 1, CK * (c + 1), 2)):
                    dve.tensor_tensor((z[:, 1, :], sq[:, :])[n], x_raw[:, kt, :], x_raw[:, kt, :], ALU.mult
                                      ).then_inc(x_odd_squared, 1)

            def z_free(n):
                if 2 <= n < U_Q + 2:
                    dve.wait_ge(z_stored[n % 2], 16 * min(n // 2, U_Q // 2))
                if 2 <= n < U_KV + 2:
                    dve.wait_ge(z_copied, n - 1)
                if n > U_KV + 1 and n % 2 == 1:
                    dve.wait_ge(v_row_made, min((n - U_KV) // 2, 4))

            for n in range(U_KV):
                beside(straight(n), [None, rel_rows if n == 1 else None])
                if n == 0:
                    mean(0, D_MODEL)
                    newton(0, rstd[:, :])
                z_free(n)
                scale_out(straight(n), z[:, n % 2, :])

            def key_norm(j):
                newton(N_NORM_K + j, nr[:, :])
                dve.scalar_tensor_tensor(k_t[:, j, :], z[:, 0, :], g_k[:, 1 + j // 2:2 + j // 2], nr[:, :],
                                         ALU.mult, ALU.mult)

            def query_norm(h, p):
                newton(n_norm_q(h), nr[:, :])
                steps.did(dve.scalar_tensor_tensor(q_t[:, h, :], z[:, p, :], g_qs, nr[:, :], ALU.mult, ALU.mult))

            def pages_in(h):
                for k in range(NPG):
                    dve.wait_ge(page_turned, 2 * h + k + 1)
                    dve.tensor_copy(kv_t[:, :, bass.ds(SEQ + PAST * h + PAGE * k, PAGE)],
                                    aux[:, 2 + k, :].rearrange("p (q n) -> p q n", q=4)).then_inc(page_read, 1)

            for j in range(4):
                n = U_KV + 2 * j
                beside(straight(n), [None, None, lambda: pages_in(2 * j)])
                z_free(n)
                scale_out(straight(n), z[:, 0, :])
                beside(straight(n + 1), [None, lambda: mean(N_NORM_K + j, HD),
                                         lambda: (key_norm(j), pages_in(2 * j + 1))])
                z_free(n + 1)
                scale_out(straight(n + 1), z[:, 1, :])
                dve.wait_ge(mm_read, n + 2)
                dve.tensor_copy(v_new[:, j, :], z[:, 1, SEQ:TOK])

            def wg_lo():
                dve.wait_ge(wg_hi_made, 1)
                dve.tensor_tensor(wg_parts[:, :, N_GATE:2 * N_GATE], wg_raw[:, :, :],
                                  wg_parts[:, :, 0:N_GATE].bitcast(F32), ALU.subtract).then_inc(wg_split, 1)

            def compressed(kv, dst, made):
                dve.wait_ge(cmp_used, (kv + 1) * CMP_LEN // CJ)
                src = aux[:, 2 + kv, 0:NKV * (W_ALL + 1)].rearrange("p (g w) -> p g w", g=NKV)
                steps.did(dve.tensor_copy(vs_tmp[:, kv:kv + 1], src[:, 0, W_ALL:W_ALL + 1]))
                dve.tensor_scalar(dst[:, :, :], src[:, :, 0:W_USED], vs_tmp[:, kv:kv + 1], None, ALU.add
                                  ).then_inc(made, 1)

            def gates_in():
                dve.wait_ge(gates_summed, 1)
                dve.tensor_tensor(halves(g_t[:, :]), aux[0:2 * N_GATE, 2:4, 0:HT],
                                  halves(rstd[0:2 * N_GATE, :]), ALU.mult).then_inc(g_t_made, 1)

            def gates_added():
                dve.wait_ge(gates_turned, 1)
                parts = aux[:, 3, 0:2 * N_GATE * (NCH + 1)].rearrange("p (t n) -> p t n", n=2 * N_GATE)
                steps.did(dve.tensor_copy(gz[:, :, :], parts[:, :, 0:N_GATE]))
                dve.tensor_tensor(gz[:, :, :], gz[:, :, :], parts[:, :, N_GATE:2 * N_GATE], ALU.add
                                  ).then_inc(gz_made, 1)

            def gates_out():
                dve.wait_ge(gz_tanh, 1)
                dve.tensor_scalar(gates[:, :, :], gz[:, :, :], 0.5, 0.5, ALU.mult, ALU.add).then_inc(gates_made, 1)

            def key_windows_norm():
                newton(N_NORM_C, nr[:, 0:NKV * W_USED], NKV * W_USED)
                steps.did(dve.scalar_tensor_tensor(kc_t[:, :, :], kc_t[:, :, :], g_k[:, 0:1],
                                                   nr[:, 0:NKV * W_USED].rearrange("p (g w) -> p g w", g=NKV),
                                                   ALU.mult, ALU.mult))

            def windows_turned():
                dve.wait_ge(vcp_turned, 1)
                dve.tensor_copy(vc_p[0:W_PROMPT, :, :],
                                aux[0:W_PROMPT, 2, 0:NKV * P].rearrange("p (g d) -> p g d", g=NKV)
                                ).then_inc(vcp_made, 1)

            for h in range(NH):
                n = U_Q + h
                jobs = [None, None, None, None]
                if h:
                    jobs[1:3] = [lambda: mean(n_norm_q(h - 1), HD), lambda: query_norm(h - 1, 1 - h % 2)]
                if h == 0:
                    jobs[2] = wg_lo
                if h == 1:
                    jobs[0] = gates_in
                    jobs[3] = gates_added
                if h == 2:
                    jobs[3] = gates_out
                if h == NH // 2:
                    jobs[0] = lambda: compressed(0, kc_t, kc_made)
                    jobs[3] = lambda: mean(N_NORM_C, HD, NKV * W_USED)
                if h == NH // 2 + 1:
                    jobs[0] = key_windows_norm
                beside(straight(n), jobs)
                z_free(n)
                scale_out(straight(n), z[:, n % 2, :])

            def smp_copies(b):
                for br, x in ((0, X_SEL), (1, X_WIN)):
                    dve.tensor_copy(vx_t[:, :, x:x + 1], v_new[:, 2 * br:2 * br + 2, bass.ds(b, 1)])
                dve.tensor_copy(vx_t[:, :, 0:W_SAMPLE],
                                vc_t[:, :, bass.ds(SEQ // STRIDE + b * (PAST // STRIDE), W_SAMPLE)]
                                ).then_inc(smp_static, 1)

            def smp_norms(b):
                dve.wait_ge(keys_loaded, 48 * b + 48)
                for n in range(4):
                    for g in range(NKV):
                        k = stage[:, n, g * HD:(g + 1) * HD]
                        last = dve.tensor_tensor_reduce(junk[:, 2 * n + g, :], k, k, 1.0, 0.0, ALU.mult, ALU.add,
                                                        k_ss[:, 2 * n + g:2 * n + g + 1])
                steps.did(last)
                dve.tensor_scalar(k_a, k_ss, 1.0 / HD, EPS, ALU.mult, ALU.add).then_inc(smp_base, 1)

            def smp_scale_keys(b):
                dve.wait_ge(smp_guess, b + 1)
                steps.did(dve.tensor_tensor(k_q, k_r, k_r, ALU.mult))
                steps.did(dve.scalar_tensor_tensor(k_q, k_q, -0.5, k_a, ALU.mult, ALU.mult))
                steps.did(dve.scalar_tensor_tensor(k_rs, k_q, 1.5, k_r, ALU.add, ALU.mult))
                for n in range(4):
                    for g in range(NKV):
                        k = stage[:, n, g * HD:(g + 1) * HD]
                        last = dve.tensor_scalar(k, k, k_rs[:, 2 * n + g:2 * n + g + 1], None, ALU.mult)
                last.then_inc(smp_keys, 1)

            def smp_values_in(b):
                dve.wait_ge(smp_vturned, b + 1)
                dve.tensor_copy(vx_s[:, :, :], aux[0:X_ROWS, 3, 0:NKV * P].rearrange("p (g d) -> p g d", g=NKV)
                                ).then_inc(smp_vmade, 1)

            def smp_keys_in(b):
                dve.wait_ge(smp_kturned, 2 * b + 2)
                dve.tensor_scalar(kw_t[:, :, 0:PAST], aux[:, 1, :].rearrange("p (g k) -> p g k", g=NKV),
                                  g_k[:, 2:3], None, ALU.mult)
                for br, dst in enumerate((ks_t, kw_t)):
                    dve.tensor_copy(dst[:, :, PAST:PAST + 1], k_t[:, 2 * br:2 * br + 2, bass.ds(SEQ + b, 1)])
                for g in range(NKV):
                    last = dve.tensor_copy(qm[:, g, REP * g:REP * (g + 1)],
                                           q_t[:, REP * g:REP * (g + 1), bass.ds(SEQ + b, 1)
                                               ].rearrange("p h o -> p (h o)"))
                last.then_inc(smp_kw, 1)

            def smp_softmax(b):
                dve.wait_ge(smp_scored, b + 1)
                carry(nc.vector)
                r = rel_s[:, 0:PAST + 1]
                rc = rel_s[:, CMP_LEN - 1:CMP_LEN - 1 + STRIDE * (W_SAMPLE - 1) + 1:STRIDE]
                for n, (s_, bias, w) in enumerate(((aux[0:NH, 2, 0:PAST + 1], r, PAST + 1),
                                                   (aux[0:NH, 3, 0:PAST + 1], r, PAST + 1),
                                                   (aux[0:NH, 2, 300:300 + W_SAMPLE], rc, W_SAMPLE))):
                    last = dve.tensor_tensor_reduce(sp[:, n, 0:w], s_, bias, 1.0, -3e38, ALU.add, ALU.max,
                                                    mx[0:NH, n:n + 1])
                steps.did(last)
                dve.tensor_scalar(mn[0:NH, :], mx[0:NH, :], -1.0, None, ALU.mult).then_inc(smp_max, 1)

            def smp_divide(b):
                dve.wait_ge(smp_exp, b + 1)
                steps.did(dve.reciprocal(rl[0:NH, :], ls[0:NH, :]))
                steps.did(dve.tensor_tensor(rl[0:NH, :], rl[0:NH, :],
                                            gs_row[:, bass.ds(b, 1), :].rearrange("p o j -> p (o j)"), ALU.mult))
                for n, cut, dst in ((0, slice(0, PAST), None), (1, slice(0, PAST), None), (2, slice(0, W_SAMPLE), None),
                                    (0, slice(PAST, PAST + 1), X_SEL), (1, slice(PAST, PAST + 1), X_WIN)):
                    out = sp[:, n, cut] if dst is None else sp[:, 2, dst:dst + 1]
                    last = dve.tensor_scalar(out, sp[:, n, cut], rl[0:NH, GATE_OF[n]:GATE_OF[n] + 1], None, ALU.mult)
                last.then_inc(smp_probs, 1)

            def smp_probs_out(b):
                dve.wait_ge(smp_pturned, b + 1)
                dve.tensor_copy(pt_s[:, 0:4 * NH], aux[:, 0, 0:4 * NH])
                dve.tensor_copy(pt_s[0:X_ROWS, 4 * NH:5 * NH], aux[0:X_ROWS, 0, 4 * NH:5 * NH]
                                ).then_inc(smp_pmade, 1)

            def smp_result(b):
                dve.wait_ge(smp_out, b + 1)
                carry(nc.vector)
                dve.tensor_copy(q_t[:, :, bass.ds(SEQ + b, 1)].rearrange("p h o -> p (h o)"), aux[:, 1, 0:NH]
                                ).then_inc(smp_read, 1)

            dve.wait_ge(consts_set, 2)
            def smp_pair(b):
                scale_out((U_VU // 2 + b, 0), z[:, 0, :])
                beside((U_VU // 2 + b, 1), [lambda: smp_softmax(b), lambda: smp_divide(b), lambda: smp_probs_out(b)])
                dve.wait_ge(z_read, 2 * b)
                scale_out((U_VU // 2 + b, 1), z[:, 1, :])
                smp_result(b)

            beside((U_VU // 2, 0), [lambda: (smp_scale_keys(0), mean(n_norm_q(NH - 1), HD)),
                                    lambda: (windows_turned(), query_norm(NH - 1, 1)),
                                    lambda: (smp_values_in(0), smp_keys_in(0))],
                   first=lambda: (compressed(1, vc_t, vc_made), dve.wait_ge(vc_made, 1),
                                  dve.memset(sp[:, 2, 0:X_ROWS], 0.0), smp_copies(0), smp_norms(0)))
            dve.wait_ge(gate_loaded, 16)
            smp_pair(0)
            with steps.loop(1, DEC, 7) as b:
                beside((U_VU // 2 + b, 0), [lambda: smp_scale_keys(b), lambda: smp_values_in(b),
                                            lambda: smp_keys_in(b)],
                       first=lambda: (smp_copies(b), smp_norms(b)))
                dve.wait_ge(z_read, 2 * b - 1)
                smp_pair(b)

            mean(N_NORM_V, D_GM)

            def v_scaled(first, last):
                for g in range(first, last):
                    dve.scalar_tensor_tensor(v_t[:, g, :], v_t[:, g, :], g_sgu[:, g:g + 1], nr[:, :],
                                             ALU.mult, ALU.mult)

            def v_norm():
                newton(N_NORM_V, nr[:, :])
                dve.wait_ge(z_read, 2 * GRP)
                v_scaled(0, 1)

            def v_norm_end():
                v_scaled(GRP - 2, GRP - 1)
                dve.scalar_tensor_tensor(v_t[:, GRP - 1, :], v_t[:, GRP - 1, :], g_sgu[:, GRP - 1:GRP], nr[:, :],
                                         ALU.mult, ALU.mult).then_inc(v_normed, 1)

            def smp_gating():
                dve.wait_ge(v_normed, 1)
                dve.wait_ge(gm_loaded, 32)
                for g in range(GRP):
                    last = dve.tensor_scalar(na[:, DEC * g:DEC * (g + 1)], v_t[:, g, SEQ:TOK], w00[:, g:g + 1],
                                             b_bc[:, g, 0:1], ALU.mult, ALU.add)
                steps.did(last)
                steps.did(dve.tensor_tensor(u_t[:, :, SEQ:TOK], u_t[:, :, SEQ:TOK],
                                            na[:, 0:DEC * GRP].rearrange("p (g b) -> p g b", g=GRP), ALU.mult))

            def softmax(h, a, i):
                dve.wait_ge(scored, a + 1)
                if i == 0:
                    dve.wait_ge(toep_loaded, 16 * h + 16)
                carry(nc.vector)
                o = SEQ - P * (i + 1)
                w = P * (i + 1)
                oc = o + CMP_LEN - 1
                for n, (x, s_, bias) in enumerate((
                        (p_s[:, 0:w], aux[:, 0, 0:w], toep[:, o:SEQ]),
                        (p_w[:, 0:w], aux[:, 1, 0:w], toep[:, o:SEQ]),
                        (p_c[:, 0:seen(i)], aux[:, 2, 0:seen(i)], toep[:, oc:oc + STRIDE * (seen(i) - 1) + 1:STRIDE]))):
                    last = dve.tensor_tensor_reduce(x, s_, bias, 1.0, -3e38, ALU.add, ALU.max, mx[:, n:n + 1])
                steps.did(last)
                dve.tensor_scalar(mn, mx, -1.0, -0.1 * NEG, ALU.mult, ALU.min).then_inc(s_max, 1)

            def divide(h, a, i):
                dve.wait_ge(s_exp, a + 1)
                steps.did(dve.tensor_scalar(ls, ls, 1e-30, None, ALU.max))
                steps.did(dve.reciprocal(rl, ls))
                steps.did(dve.tensor_tensor(rl, rl, gates[:, i, bass.ds(3 * h, 3)], ALU.mult))
                for n, (x, w) in enumerate(((p_s, P * (i + 1)), (p_w, P * (i + 1)), (p_c, seen(i)))):
                    last = dve.tensor_scalar(x[:, 0:w], x[:, 0:w], rl[:, GATE_OF[n]:GATE_OF[n] + 1], None, ALU.mult)
                last.then_inc(probs, 1)

            def group(h, i):
                if i == 2:
                    dve.wait_ge(aux3_made, 6 * h + 3)
                    dve.tensor_copy(vr_g[:, :, :], aux[:, 3, :].rearrange("p (k c) -> p k c", k=NCH)
                                    ).then_inc(aux3_read, 1)
                if i == 3:
                    dve.wait_ge(aux3_made, 6 * h + 5)
                    dve.tensor_tensor(na[:, 0:SEQ].rearrange("p (k t) -> p k t", k=NCH),
                                      aux[:, 3, :].rearrange("p (k t) -> p k t", k=NCH),
                                      b_bc[:, bass.ds(h, 1), :].to_broadcast([P, NCH, P]), ALU.add
                                      ).then_inc(aux3_read, 1)
                    dve.wait_ge(aux3_read, 6 * h + 5)
                    dve.tensor_tensor(u_t[:, h, 0:SEQ], u_t[:, h, 0:SEQ], na[:, 0:SEQ], ALU.mult)

            def probs_out(a, i):
                dve.wait_ge(p_turned, a + 1)
                dve.tensor_copy(pt_win[:, 0:i + 1, :], aux[:, 1, 0:P * (i + 1)].rearrange("p (k q) -> p k q", k=i + 1))
                dve.tensor_copy(pt_cmp[0:seen(i), :], aux[0:seen(i), 2, 0:P]).then_inc(pt_made, 1)

            def mixed_chunk(c):
                for kt in range(CK * c, CK * (c + 1)):
                    src = u_t[:, kt, :] if kt < GRP else q_t[:, kt - GRP, :]
                    dve.wait_ge(act_hi, KT + kt + 1)
                    dve.tensor_tensor(a_lo[:, kt, :], src, a_hi[:, kt, :].bitcast(F32), ALU.subtract
                                      ).then_inc(a_ready, 1)

            def head(h, extra=()):
                for i in range(NCH):
                    a = NCH * h + i
                    u = (U_GATE // 2 + 2 * h + i // 2, i % 2)
                    more_jobs = extra[i] if i < len(extra) else [None] * CH
                    jobs = [[lambda: divide(h, a, i)], [lambda: group(h, i)] if i >= 2 else [],
                            [lambda: probs_out(a, i)], []]
                    for c in range(CH):
                        if more_jobs[c]:
                            jobs[c].append(more_jobs[c])
                    together = lambda fs: (lambda: [f() for f in fs])
                    beside(u, [together(fs) for fs in jobs], first=lambda: softmax(h, a, i))
                    dve.wait_ge(g_stored[i % 2], 32 * h + 16 * (i // 2))
                    scale_out(u, z[:, i % 2, :])
                    dve.wait_ge(aux3_made, 6 * h + (1, 2, 4, 6)[i])
                    dve.tensor_copy(q_t[:, h, P * i:P * (i + 1)], aux[:, 3, 0:P]).then_inc(aux3_read, 1)

            dve.wait_ge(gates_made, 1)
            head(0, [[None, None, v_norm, lambda: v_scaled(1, 2)],
                     [lambda: v_scaled(2, 3), lambda: v_scaled(3, 5), lambda: v_scaled(5, 6), v_norm_end],
                     [None, None, None, smp_gating]])
            with steps.loop(1, REP, 16) as h:
                head(h)
            with steps.loop(REP, NH - 1, 16) as h:
                head(h)
            head(NH - 1, [[None] * CH] * 3 + [[lambda: mixed_chunk(0), None, None, None]])
            dve.wait_ge(aux3_read, 6 * NH)
            for c in range(1, CH):
                mixed_chunk(c)

            with dve.Fori(0, MB // 2) as i:
                for p in range(2):
                    m = 2 * i + p
                    u = (U_PROJ // 2 + i, p)
                    n = num(u)

                    def first():
                        dve.wait_ge(g_loaded[p], 16 * i + 16)
                        dve.tensor_tensor(halves(ca[:, :]), pair(0), halves(g_in[:, p, 0, :]), ALU.mult
                                          ).then_inc(mm_read, 1)

                    beside(u, [None, first])
                    dve.wait_ge(chunk_done, CH * n + CH)
                    dve.tensor_tensor(halves(cb[:, :]), pair(1), halves(g_in[:, p, 1, :]), ALU.mult).then_inc(mm_read, 1)
                    dve.wait_ge(mm_read, 2 * n - U_PROJ + 2)
                    dve.tensor_tensor(cm[:, :], ca[:, :], cb[:, :], ALU.add).then_inc(act_src, 1)
                    dve.wait_ge(act_src, m + 1)
                    dve.wait_ge(act_hi, 2 * KT + m + 1)
                    dve.tensor_tensor(b_lo[:, m, :], cm[:, :], b_hi[:, m, :].bitcast(F32), ALU.subtract
                                      ).then_inc(b_ready, 1)

            with dve.Fori(0, MB // 2) as i:
                for p in range(2):
                    m = 2 * i + p
                    u = (U_OUT // 2 + i, p)
                    beside(u)
                    dve.wait_ge(x_in_loaded[p], 16 * i + 16)
                    dve.wait_ge(chunk_done, CH * num(u) + CH)
                    dve.tensor_tensor(halves(x2[:, m, :]), pair(p), halves(z[:, p, :]), ALU.add).then_inc(mm_read, 1)
                    dve.wait_ge(mm_read, num(u) + MB + 1)
                    dve.tensor_scalar(na[:, :], x2[:, m, :], g_mlp[:, bass.ds(m, 1)], None, ALU.mult
                                      ).then_inc(act_src, 1)
                    dve.wait_ge(act_src, 1 + MB + m)
                    dve.wait_ge(act_hi, 3 * KT + m + 1)
                    dve.tensor_tensor(a_lo[:, m, :], na[:, :], a_hi[:, m, :].bitcast(F32), ALU.subtract
                                      ).then_inc(a_ready, 1)

            def up(f, i, p):
                m = 2 * i + p
                u = (U_FF // 2 + MB * f + i, p)
                beside(u)
                if type(f) is int and f == 0 and type(i) is int and p == 0:
                    dve.wait_ge(a_ready, 3 * KT)
                    mean(N_NORM_X2, D_MODEL)
                    newton(N_NORM_X2, rstd[:, :])
                dve.wait_ge(chunk_done, CH * num(u) + CH)
                dve.scalar_tensor_tensor(halves(z[:, p, :]), pair(p), 0.0, halves(rstd[:, :]), ALU.max, ALU.mult
                                         ).then_inc(mm_read, 1)
                dve.wait_ge(mm_read, num(u) + MB + 1)
                dve.tensor_tensor(na[:, :], z[:, p, :], z[:, p, :], ALU.mult).then_inc(act_src, 1)
                dve.wait_ge(act_src, 1 + 2 * MB + MB * f + m)
                dve.wait_ge(act_hi, 4 * KT + MB * f + m + 1)
                dve.tensor_tensor(b_lo[:, m, :], na[:, :], b_hi[:, m, :].bitcast(F32), ALU.subtract
                                  ).then_inc(b_ready, 1)

            def down(f, i, p):
                m = 2 * i + p
                u = (U_FF // 2 + MB // 2 + MB * f + i, p)
                if more(u):
                    beside(u)
                dve.wait_ge(chunk_done, CH * num(u) + CH)
                dve.tensor_tensor(halves(x2[:, m, :]), pair(p), halves(x2[:, m, :]), ALU.add).then_inc(mm_read, 1)

            ff_loops(dve, up, down)

        @block.gpsimd
        def _(pool):
            steps = Steps(pool, pool_step)

            pool.memset(small[:, 173:174], 0.0).then_inc(cell_set, 1)
            pool.wait_ge(cell_set, 1)
            pool.dma_start(oh[:, :], t["one_hot"]).then_inc(consts_loaded, 16)
            pool.dma_start(rb[0:NB, :], t["rel_bias"]).then_inc(consts_loaded, 16)
            pool.dma_start(w00, t["w_00"].to_broadcast([P, GRP])).then_inc(consts_loaded, 16)
            pool.dma_start(table[:, :], t["table"]).then_inc(table_loaded, 16)
            steps.did(pool.memset(rb[NB:NB + 1, :], NEG))
            steps.did(pool.memset(ident[:, :], 0.0))
            steps.did(pool.affine_select(out=ident[:, :], in_=ident[:, :], compare_op=ALU.not_equal, fill=1.0,
                                         base=0, pattern=[[-1, P]], channel_multiplier=1))
            pool.memset(ones[:, :], 1.0).then_inc(consts_set, 1)
            pool.wait_ge(consts_set, 1)
            steps.did(pool.memset(acc_v[:, :], 0.0))
            for n in range(KT // 2):
                pool.wait_ge(x_squared, n + 1)
                pool.wait_ge(x_added, n)
                pool.tensor_tensor(acc_v[:, :], acc_v[:, :], z[:, 0, :], ALU.add).then_inc(x_added, 1)
            steps.did(pool.memset(minus_half, -0.5))
            steps.did(pool.memset(vx_t[:, :, :], 0.0))
            pool.memset(qm[:, :, :], 0.0).then_inc(consts_set, 1)

            def load_w_cmp(n):
                pool.dma_start(w_cmp[:, n % 2, :, :], t["w_cmp"][n]).then_inc(cmp_loaded[n % 2], 16)

            def load_pages(h, p):
                for k in range(NPG):
                    page = pool.value_load(table[0:1, bass.ds(NPG * h + k, 1)], min_val=0, max_val=N_POOL - 1)
                    pool.dma_start(pages[:, p, k, :], t["cache_cmp"][page]).then_inc(page_loaded[p], 16)

            pool.wait_ge(table_loaded, 16)
            load_pages(0, 0)
            load_pages(1, 1)
            pool.wait_ge(a_ready, KT)
            pool.wait_ge(summed, 1)
            for s in range(4):
                pool.dma_start(kv_t[:, s, L_ALL:KVT_W], t["pos"][s // NKV]).then_inc(pos_loaded, 16)
            for n in range(U_KV):
                pool.wait_ge(z_made, n + 1)
                pool.tensor_copy(kv_t[:, n, 0:SEQ], z[:, n % 2, 0:SEQ]).then_inc(z_copied, 1)
            pool.wait_ge(z_copied, 1)
            steps.did(pool.memset(acc_v[:, :], 0.0))

            pool.wait_ge(rel_done, 1)
            pool.dma_start(rel_d, rel_row[:, :]).then_inc(rel_stored, 16)
            pool.wait_ge(rel_stored, 16)
            pool.dma_start(toep_d, bass.AP(tensor=rel_d.tensor, offset=P - 1,
                                           ap=[[NREL, NH], [-1, P], [1, SEQ]])).then_inc(toep_stored, 16)
            load_w_cmp(0)
            load_w_cmp(1)
            with pool.Fori(1, DEC // 2) as i:
                for p in range(2):
                    pool.wait_ge(page_turned, 2 * (2 * i + p - 2) + 2)
                    load_pages(2 * i + p, p)
            pool.wait_ge(page_turned, NPG * DEC)
            pool.dma_start(wg_raw[:, :, :], t["w_gates"]).then_inc(wg_loaded, 16)

            def load_keys(b):
                load_stage(b, 0, keys_loaded)

            def load_values(b):
                load_stage(b, 1, values_loaded)

            def load_stage(b, kv, loaded):
                cut = slice(kv * NKV * HD, (kv + 1) * NKV * HD)
                for k in range(NPG):
                    page = pool.value_load(table[0:1, bass.ds(NPG * b + k, 1)], min_val=0, max_val=N_POOL - 1)
                    pool.dma_start(stage[:, k, cut], t["cache_sel"][page][:, cut]).then_inc(loaded, 16)
                pool.dma_start(stage[:, 2:4, cut], t["state"][b].rearrange("(c p) n -> p c n", c=2)[:, :, cut]
                               ).then_inc(loaded, 16)

            for n in range(2, 2 * CMP_LEN // CJ):
                pool.wait_ge(cmp_used, n - 1)
                load_w_cmp(n)
                if n == 2 * CMP_LEN // CJ - 2:
                    pool.wait_ge(gates_made, 1)
                    pool.dma_start(gate_d, gates[P - DEC:P, NCH, :]).then_inc(gate_stored, 16)
                    pool.wait_ge(gate_stored, 16)
                    pool.dma_start(gs_row, gate_d.rearrange("b (h j) -> h b j", h=NH)).then_inc(gate_loaded, 16)
                    load_keys(0)

            def smp_pair(b, ahead):
                pool.wait_ge(smp_out, b)
                load_values(b)
                pool.wait_ge(smp_base, b + 1)
                pool.tensor_tensor(k_r, k_a, minus_half, ALU.pow).then_inc(smp_guess, 1)
                if ahead:
                    pool.wait_ge(smp_kturned, 2 * b + 2)
                    load_keys(b + 1)
                pool.wait_ge(z_read, 2 * b + 1)
                pool.wait_ge(v_acc, b)
                steps.did(pool.tensor_tensor(sq[:, :], v_t[:, b, :], v_t[:, b, :], ALU.mult))
                pool.tensor_tensor(acc_v[:, :], acc_v[:, :], sq[:, :], ALU.add).then_inc(v_acc, 1)

            with steps.loop(0, DEC - 1, 1) as b:
                smp_pair(b, True)
            smp_pair(DEC - 1, False)

            pool.wait_ge(smp_read, DEC)
            pool.dma_start(wm[:, :, :], t["w_mix"]).then_inc(gm_loaded, 16)
            pool.dma_start(b_bc[:, :, :].rearrange("p g t -> p (g t)"), t["b_mix"].to_broadcast([P, GRP * P])
                           ).then_inc(gm_loaded, 16)
            pool.wait_ge(gm_loaded, 32)
            pool.affine_select(out=wm[:, :, :], in_=wm[:, :, :], compare_op=ALU.is_ge, fill=0.0, base=0,
                               pattern=[[0, GRP], [1, P]], channel_multiplier=-1).then_inc(w_masked, 1)

            pool.wait_ge(v_normed, 1)
            pool.dma_start(t["v_t"], v_t[:, :, SEQ - P:TOK]).then_inc(v_stored, 16)
            pool.dma_start(t["win"], t["state"]).then_inc(win_stored, 16)

            with steps.loop(0, MB, 2) as m:
                for p in range(2):
                    pool.wait_ge(g_tanh, 2 * m + p + 1)
                    carry(nc.gpsimd)
                    steps.did(pool.tensor_scalar(z[:, p, :], z[:, p, :], 0.5, 0.5, ALU.mult, ALU.add))
                    pool.dma_start(merge_d[2 * m + p], z[:, p, :]).then_inc(g_stored[p], 16)

            pool.wait_ge(aux3_read, 6 * NH)
            pool.wait_ge(v_stored, 16)
            pool.wait_ge(win_stored, 16)
            for p in range(2):
                pool.wait_ge(g_stored[p], 16 * MB)
            with pool.Fori(0, MB // 2) as i:
                for p in range(2):
                    pool.wait_ge(mm_read, U_PROJ + 2 * (2 * i + p) - 2)
                    pool.dma_start(g_in[:, p, :, :], merge_d.rearrange("(m t) p n -> m p t n", t=2)[2 * i + p]
                                   ).then_inc(g_loaded[p], 16)
            steps.did(pool.memset(acc_x[:, :], 0.0))
            with steps.loop(0, MB // 2, 2) as i:
                for p in range(2):
                    m = 2 * i + p
                    pool.wait_ge(mm_read, U_OUT + MB - 1 + m)
                    pool.dma_start(z[:, p, :], t["x_t"][m]).then_inc(x_in_loaded[p], 16)
                    pool.wait_ge(act_src, MB + m + 1)
                    pool.wait_ge(x2_squared, m)
                    steps.did(pool.tensor_tensor(nr[:, :], x2[:, m, :], x2[:, m, :], ALU.mult))
                    pool.tensor_tensor(acc_x[:, :], acc_x[:, :], nr[:, :], ALU.add).then_inc(x2_squared, 1)


_INS = ["x_t", "w", "gains", "one_hot", "rel_bias", "w_00", "table", "w_cmp", "pos", "cache_cmp", "cache_sel",
        "state", "w_gates", "w_mix", "b_mix"]
_OUTS = [("y_t", (MB, P, TOK)), ("kv_t", (U_Q, P, TOK)), ("v_t", (P, GRP, P + DEC)), ("win", (DEC, PAST, 512))]


def _layout(a):
    w_in = a["w_in"][0]
    x = np.concatenate([a["x_prompt"][0], a["x_sample"][:, 0]], 0)
    kvw = 2 * NKV * HD

    def blocks(w, rows=KT):
        n = w.shape[1] // P
        return w.reshape(rows, P, n, P).transpose(2, 1, 0, 3).reshape(n, P, rows * P)

    o = 2 * D_GM
    uv, q = blocks(w_in[:, :o]), blocks(w_in[:, o:o + NH * HD])
    o += NH * HD
    kv = [blocks(w_in[:, o + n * kvw:o + (n + 1) * kvw]) for n in range(3)]
    o += 3 * kvw
    w_gates = w_in[:, o:o + N_GATE].reshape(KT, P, N_GATE).transpose(1, 0, 2)
    o += N_GATE
    ga, gb = blocks(w_in[:, o:o + D_MODEL]), blocks(w_in[:, o + D_MODEL:])
    pairs = lambda f, s: np.stack([f, s], 1).reshape(-1, P, KT * P)
    up, down = a["w_up"][0], a["w_down"][0]
    parts = [kv[0], kv[1][[0, 2, 1, 3]], kv[2][[0, 2, 1, 3]], q, pairs(uv[GRP:], uv[:GRP]), pairs(ga, gb),
             np.concatenate([blocks(a["w_proj_gmlp"][0], GRP), blocks(a["w_proj_nsa"][0], NH)], 2),
             blocks(a["w_out"][0])]
    for f in range(FG):
        cut = slice(f * D_MODEL, (f + 1) * D_MODEL)
        parts += [blocks(up[:, cut]), blocks(down[cut])]
    cols = lambda g: g.reshape(-1, P).T
    rel = SEQ - 1 - np.arange(NREL)
    far = np.maximum(rel, 1).astype(np.float32)
    bucket = NB // 2 + (np.log(far / (NB // 2)) / np.log(128 / (NB // 2)) * (NB // 2)).astype(np.int32)
    bucket = np.where(rel < NB // 2, rel, np.minimum(bucket, NB - 1))
    bucket = np.where(rel < 0, NB, bucket)
    one_hot = (np.arange(NB + 1)[:, None] == bucket[None]).astype(np.float32)
    w_sgu = a["w_sgu"][0]
    w_cmp = np.stack([a["w_cmp_k"][0], a["w_cmp_v"][0]]).reshape(2 * CMP_LEN // CJ, CJ, HD, HD)
    return {
        "x_t": x.T.reshape(KT, P, TOK),
        "w": np.concatenate(parts),
        "gains": np.concatenate([cols(a["g_mix_norm"][0]), cols(a["g_mlp_norm"][0]), cols(a["g_sgu"][0]),
                                 cols(a["g_q"][0]), cols(a["g_k"][0])], 1),
        "one_hot": one_hot,
        "rel_bias": a["rel_bias"],
        "w_00": w_sgu[None, :, 0, 0],
        "table": a["page_table"].reshape(1, DEC * NPG),
        "w_cmp": w_cmp.transpose(0, 2, 1, 3),
        "pos": np.stack([a["pos_cmp_k"][0].T, a["pos_cmp_v"][0].T]),
        "cache_cmp": a["cache_cmp_kv"].reshape(N_POOL, PAGE, kvw),
        "cache_sel": a["cache_sel_kv"].reshape(N_POOL, PAGE, kvw),
        "state": a["state_win_kv"].reshape(DEC, PAST, kvw),
        "w_gates": w_gates,
        "w_mix": w_sgu.transpose(2, 0, 1),
        "b_mix": a["b_sgu"].reshape(1, GRP * P),
    }


def kernel(**inputs):
    import concourse.bacc as bacc
    from concourse.bass_utils import run_bass_kernel_spmd

    nc = bacc.Bacc("TRN2", target_bir_lowering=False, num_devices=1, dynamic_dma_scratch_size=8192)
    arrays = {n: np.ascontiguousarray(x) for n, x in _layout({k: np.asarray(v) for k, v in inputs.items()}).items()}
    t = {n: nc.dram_tensor(f"in_{n}", arrays[n].shape, mybir.dt.from_np(arrays[n].dtype), kind="ExternalInput").ap()
         for n in _INS}
    t |= {n: nc.dram_tensor(f"out_{n}", shape, F32, kind="ExternalOutput").ap() for n, shape in _OUTS}
    build(nc, t)
    r = run_bass_kernel_spmd(nc, [{f"in_{n}": arrays[n] for n in _INS}], core_ids=[0]).results[0]
    y = r["out_y_t"].reshape(D_MODEL, TOK).T
    kv = r["out_kv_t"].transpose(2, 0, 1)
    order = {"cmp": [0, 1, 2, 3], "sel": [4, 6, 5, 7], "win": [8, 10, 9, 11]}
    kv = {n: kv[:, o].reshape(TOK, 2, NKV, HD) for n, o in order.items()}
    v = r["out_v_t"].transpose(2, 1, 0).reshape(P + DEC, D_GM)
    prompt = lambda n: np.ascontiguousarray(kv[n][None, None, :SEQ])
    sample = lambda n: np.ascontiguousarray(kv[n][None, SEQ:, None])
    win = np.concatenate([r["out_win"].reshape(1, DEC, PAST, 2, NKV, HD), sample("win")], 2)
    return (np.ascontiguousarray(y[None, :SEQ]), np.ascontiguousarray(y[SEQ:, None]),
            prompt("cmp"), prompt("sel"), prompt("win"), np.ascontiguousarray(v[None, None, :P]),
            sample("cmp"), sample("sel"), win, np.ascontiguousarray(v[None, P:, None]))
```
